# Optimizing a Trainium2 kernel written in Bass

```python
import math
import jax
import jax.numpy as jnp
from jax import lax
import numpy as np

D_MODEL = 1024
BATCH = 1
SEQ = 256
DEPTH = 4

CHUNK = 64
N_MIXERS = 3
N_A = (DEPTH + 2) // 3
N_B = (DEPTH + 1) // 3
N_C = DEPTH // 3
D_FF = 2816
EPS = 1e-6
NEG_INF = -1e30
HEADS_A = 16
HEAD_DIM_A = D_MODEL // HEADS_A
LEFT_CHUNKS = 8
BAND = (LEFT_CHUNKS + 1) * CHUNK
REL_CLIP = 128
GMLP_CHUNK = 128
D_GATE = D_MODEL
GMLP_GROUPS = 8
GMLP_GROUP_DIM = D_GATE // GMLP_GROUPS
HEADS_C = 8
HEAD_DIM_C = D_MODEL // (2 * HEADS_C)
Q_BLOCK = 128


def rms_norm(x, g):
    xf = x.astype(jnp.float32)
    y = xf * lax.rsqrt(jnp.mean(xf * xf, axis=-1, keepdims=True) + EPS)
    return (y * g.astype(jnp.float32)).astype(x.dtype)

def swiglu(h, w_in, w_out):
    gate, up = jnp.split(h @ w_in, 2, axis=-1)
    return (jax.nn.silu(gate) * up) @ w_out

def mixer_a(h, w_qkv, rel_bias, w_o):
    B, S, D = h.shape
    nc = S // CHUNK
    pad = LEFT_CHUNKS * CHUNK
    q, k, v = jnp.split(h @ w_qkv, 3, axis=-1)
    q = q.reshape(B, nc, CHUNK, HEADS_A, HEAD_DIM_A).transpose(1, 0, 2, 3, 4)
    k = jnp.pad(k.reshape(B, S, HEADS_A, HEAD_DIM_A), ((0, 0), (pad, 0), (0, 0), (0, 0)))
    v = jnp.pad(v.reshape(B, S, HEADS_A, HEAD_DIM_A), ((0, 0), (pad, 0), (0, 0), (0, 0)))
    rel = jnp.clip(pad + jnp.arange(CHUNK)[:, None] - jnp.arange(BAND)[None, :], -REL_CLIP, REL_CLIP) + REL_CLIP
    bias = rel_bias.astype(jnp.float32)[:, rel]
    scale = HEAD_DIM_A ** -0.5

    def one_chunk(args):
        c, qc = args
        start = c * CHUNK
        kb = lax.dynamic_slice_in_dim(k, start, BAND, axis=1)
        vb = lax.dynamic_slice_in_dim(v, start, BAND, axis=1)
        s = jnp.einsum('bqhd,bkhd->bhqk', qc, kb).astype(jnp.float32) * scale + bias
        valid = (start - pad + jnp.arange(BAND)) >= 0
        s = jnp.where(valid, s, NEG_INF)
        p = jax.nn.softmax(s, axis=-1).astype(vb.dtype)
        return jnp.einsum('bhqk,bkhd->bqhd', p, vb)

    o = lax.map(one_chunk, (jnp.arange(nc), q))
    o = o.transpose(1, 0, 2, 3, 4).reshape(B, S, D)
    return o @ w_o

def mixer_b(h, w_in, ln_g, ln_b, w_s, b_s, w_o):
    B, S, _ = h.shape
    n = S // GMLP_CHUNK
    u, v = jnp.split(jax.nn.gelu(h @ w_in, approximate=False), 2, axis=-1)
    vf = v.astype(jnp.float32)
    mu = jnp.mean(vf, axis=-1, keepdims=True)
    var = jnp.mean(jnp.square(vf - mu), axis=-1, keepdims=True)
    v = ((vf - mu) * lax.rsqrt(var + EPS) * ln_g.astype(jnp.float32) + ln_b.astype(jnp.float32)).astype(h.dtype)
    v = v.reshape(B, n, GMLP_CHUNK, GMLP_GROUPS, GMLP_GROUP_DIM)
    causal = jnp.tril(jnp.ones((GMLP_CHUNK, GMLP_CHUNK), dtype=bool))
    w = jnp.where(causal[None], w_s, 0.0)
    sv = jnp.einsum('gts,bnsgc->bntgc', w, v) + b_s.T[None, None, :, :, None]
    y = u * sv.reshape(B, S, D_GATE)
    return y @ w_o

def mixer_c(h, w_qkv, lam, subln_g, w_o, lambda_init):
    B, S, D = h.shape
    nb = S // Q_BLOCK
    q, k, v = jnp.split(h @ w_qkv, 3, axis=-1)
    q = q.reshape(B, nb, Q_BLOCK, HEADS_C, 2, HEAD_DIM_C).transpose(1, 0, 2, 3, 4, 5)
    k = k.reshape(B, S, HEADS_C, 2, HEAD_DIM_C)
    v = v.reshape(B, S, HEADS_C, 2 * HEAD_DIM_C)
    lamf = lam.astype(jnp.float32)
    lam_full = jnp.exp(jnp.sum(lamf[0] * lamf[1])) - jnp.exp(jnp.sum(lamf[2] * lamf[3])) + lambda_init
    slopes = 2.0 ** (-8.0 * (jnp.arange(HEADS_C, dtype=jnp.float32) + 1.0) / HEADS_C)
    kpos = jnp.arange(S)
    scale = HEAD_DIM_C ** -0.5

    def one_block(args):
        blk, qblk = args
        qpos = blk * Q_BLOCK + jnp.arange(Q_BLOCK)
        dist = jnp.abs(qpos[:, None] - kpos[None, :]).astype(jnp.float32)
        alibi = -slopes[:, None, None] * dist
        allowed = kpos[None, :] < (qpos[:, None] // CHUNK + 1) * CHUNK
        s = jnp.einsum('bqhmd,bkhmd->bmhqk', qblk, k).astype(jnp.float32) * scale + alibi
        s = jnp.where(allowed, s, NEG_INF)
        p = jax.nn.softmax(s, axis=-1)
        a = p[:, 0] - lam_full * p[:, 1]
        return jnp.einsum('bhqk,bkhe->bqhe', a.astype(v.dtype), v)

    o = lax.map(one_block, (jnp.arange(nb), q))
    o = o.transpose(1, 0, 2, 3, 4).reshape(B, S, HEADS_C, 2 * HEAD_DIM_C)
    o = rms_norm(o, subln_g) * (1.0 - lambda_init)
    return o.reshape(B, S, D) @ w_o

def first_inputs(seed: int = 0) -> dict:
    key = jax.random.key(seed)
    ks = jax.random.split(key, 20)

    def nrm(k, shape, scale):
        return jax.random.normal(k, shape, jnp.float32) * scale

    D = D_MODEL
    return {
        'x': nrm(ks[0], (BATCH, SEQ, D), 1.0),
        'norm_g': 1.0 + nrm(ks[1], (DEPTH, 6, D), 0.05),
        'ff1_w_in': nrm(ks[2], (DEPTH, D, 2 * D_FF), D ** -0.5),
        'ff1_w_out': nrm(ks[3], (DEPTH, D_FF, D), D_FF ** -0.5),
        'ff2_w_in': nrm(ks[4], (DEPTH, D, 2 * D_FF), D ** -0.5),
        'ff2_w_out': nrm(ks[5], (DEPTH, D_FF, D), D_FF ** -0.5),
        'a_w_qkv': nrm(ks[6], (N_A, D, 3 * D), D ** -0.5),
        'a_rel_bias': nrm(ks[7], (N_A, HEADS_A, 2 * REL_CLIP + 1), 0.5),
        'a_w_o': nrm(ks[8], (N_A, D, D), D ** -0.5),
        'b_w_in': nrm(ks[9], (N_B, D, 2 * D_GATE), D ** -0.5),
        'b_ln_g': 1.0 + nrm(ks[10], (N_B, D_GATE), 0.05),
        'b_ln_b': nrm(ks[11], (N_B, D_GATE), 0.05),
        'b_w_s': nrm(ks[12], (N_B, GMLP_GROUPS, GMLP_CHUNK, GMLP_CHUNK), GMLP_CHUNK ** -0.5),
        'b_b_s': 1.0 + nrm(ks[13], (N_B, GMLP_GROUPS, GMLP_CHUNK), 0.1),
        'b_w_o': nrm(ks[14], (N_B, D_GATE, D), D_GATE ** -0.5),
        'c_w_qkv': nrm(ks[15], (N_C, D, 3 * D), D ** -0.5),
        'c_lambda': nrm(ks[16], (N_C, 4, HEAD_DIM_C), 0.1),
        'c_subln_g': 1.0 + nrm(ks[17], (N_C, 2 * HEAD_DIM_C), 0.05),
        'c_w_o': nrm(ks[18], (N_C, D, D), D ** -0.5),
    }

def first_block(x, norm_g, ff1_w_in, ff1_w_out, ff2_w_in, ff2_w_out, a_w_qkv, a_rel_bias, a_w_o, b_w_in, b_ln_g, b_ln_b, b_w_s, b_b_s, b_w_o, c_w_qkv, c_lambda, c_subln_g, c_w_o):
    for i in range(DEPTH):
        g = norm_g[i]
        x = x + 0.5 * rms_norm(swiglu(rms_norm(x, g[0]), ff1_w_in[i], ff1_w_out[i]), g[1])
        h = rms_norm(x, g[2])
        kind, j = i % N_MIXERS, i // N_MIXERS
        if kind == 0:
            m = mixer_a(h, a_w_qkv[j], a_rel_bias[j], a_w_o[j])
        elif kind == 1:
            m = mixer_b(h, b_w_in[j], b_ln_g[j], b_ln_b[j], b_w_s[j], b_b_s[j], b_w_o[j])
        else:
            lambda_init = 0.8 - 0.6 * math.exp(-0.3 * i)
            m = mixer_c(h, c_w_qkv[j], c_lambda[j], c_subln_g[j], c_w_o[j], lambda_init)
        x = x + rms_norm(m, g[3])
        x = x + 0.5 * rms_norm(swiglu(rms_norm(x, g[4]), ff2_w_in[i], ff2_w_out[i]), g[5])
    return x


DEPTH_2 = 2

MEM_LEN = 256
NEG_INF_2 = -1e30
FORCE_SCORE = 1e4

CONV_CH = 512
CONV_WIDTH = 31

NSA_HEADS = 8
NSA_KV_GROUPS = 2
NSA_HEAD_DIM = 64
CMP_BLOCK = 32
CMP_STRIDE = 16
CMP_HIDDEN = 256
SLC_BLOCK = 64
N_SELECT = 16
WINDOW = 512
NSA_QBLOCK = 64

MLA_HEADS = 4
Q_RANK = 384
KV_RANK = 256
QK_NOPE = 128
QK_ROPE = 64
V_DIM = 128
ROPE_THETA = 10000.0
ATTN_QBLOCK = 128

REL_BUCKETS = 32
REL_MAX_DIST = 128

XATTN_HEADS = 4
XATTN_HEAD_DIM = 128

FFN_HIDDEN = -(-8 * D_MODEL // (3 * 256)) * 256

IN_SIZES = (2 * CONV_CH, NSA_HEADS * NSA_HEAD_DIM, 6 * NSA_KV_GROUPS * NSA_HEAD_DIM, 3 * NSA_HEADS, Q_RANK, KV_RANK, QK_ROPE, 3 * D_MODEL)
IN_COLS = 2 * CONV_CH + NSA_HEADS * NSA_HEAD_DIM + 6 * NSA_KV_GROUPS * NSA_HEAD_DIM + 3 * NSA_HEADS + Q_RANK + KV_RANK + QK_ROPE + 3 * D_MODEL


def rmsnorm(x, g):
    xf = x.astype(jnp.float32)
    y = xf * lax.rsqrt(jnp.mean(xf * xf, axis=-1, keepdims=True) + EPS)
    return (y * g.astype(jnp.float32)).astype(x.dtype)

def layernorm(x, g, b):
    xf = x.astype(jnp.float32)
    mu = jnp.mean(xf, axis=-1, keepdims=True)
    var = jnp.mean(jnp.square(xf - mu), axis=-1, keepdims=True)
    y = (xf - mu) * lax.rsqrt(var + EPS) * g.astype(jnp.float32) + b.astype(jnp.float32)
    return y.astype(x.dtype)

def t5_bucket(dist):
    exact = REL_BUCKETS // 2
    d = jnp.maximum(dist, 0)
    log_ratio = jnp.log(jnp.maximum(d, 1).astype(jnp.float32) / exact) / math.log(REL_MAX_DIST / exact)
    large = jnp.minimum(exact + (log_ratio * (REL_BUCKETS - exact)).astype(jnp.int32), REL_BUCKETS - 1)
    return jnp.where(d < exact, d, large)

def apply_rope(x, cos, sin):
    xf = x.astype(jnp.float32)
    x1, x2 = jnp.split(xf, 2, axis=-1)
    return jnp.concatenate([x1 * cos - x2 * sin, x2 * cos + x1 * sin], axis=-1).astype(x.dtype)

def conformer_conv(u_glu, conv_w, conv_b, ln_g, ln_b, w_proj):
    a, b = jnp.split(u_glu, 2, axis=-1)
    u = a * jax.nn.sigmoid(b)
    u = lax.conv_general_dilated(u, conv_w[:, None, :], window_strides=(1,), padding=[(CONV_WIDTH - 1, 0)],
                                 dimension_numbers=('NWC', 'WIO', 'NWC'), feature_group_count=CONV_CH) + conv_b
    u = jax.nn.silu(layernorm(u, ln_g, ln_b))
    return u @ w_proj

def compress_blocks(tok, pos, w1, b1, w2, n_cmp):
    bsz = tok.shape[0]
    idx = CMP_STRIDE * jnp.arange(n_cmp)[:, None] + jnp.arange(CMP_BLOCK)[None, :]
    blk = tok[:, idx] + pos[:, None, :]
    blk = blk.transpose(0, 1, 3, 2, 4).reshape(bsz, n_cmp, NSA_KV_GROUPS, CMP_BLOCK * NSA_HEAD_DIM)
    return jax.nn.gelu(blk @ w1 + b1) @ w2

def nsa_attention(q, kv, gate_logits, rel_bias, cmp_pos_k, cmp_w1_k, cmp_b1_k, cmp_w2_k,
                  cmp_pos_v, cmp_w1_v, cmp_b1_v, cmp_w2_v):
    bsz, seq = q.shape[0], q.shape[1]
    G, HG, dh = NSA_KV_GROUPS, NSA_HEADS // NSA_KV_GROUPS, NSA_HEAD_DIM
    n_cmp = (seq - CMP_BLOCK) // CMP_STRIDE + 1
    n_sb = seq // SLC_BLOCK
    n_sel = min(N_SELECT, n_sb)
    n_keys = n_sel * SLC_BLOCK
    kw_len = NSA_QBLOCK + WINDOW
    scale = dh ** -0.5
    q = q.reshape(bsz, seq, G, HG, dh)
    kv = kv.reshape(bsz, seq, 6, G, dh)
    k_cmp = compress_blocks(kv[:, :, 0], cmp_pos_k, cmp_w1_k, cmp_b1_k, cmp_w2_k, n_cmp)
    v_cmp = compress_blocks(kv[:, :, 1], cmp_pos_v, cmp_w1_v, cmp_b1_v, cmp_w2_v, n_cmp)
    k_slc = kv[:, :, 2].reshape(bsz, n_sb, SLC_BLOCK, G, dh).transpose(0, 3, 1, 2, 4)
    v_slc = kv[:, :, 3].reshape(bsz, n_sb, SLC_BLOCK, G, dh).transpose(0, 3, 1, 2, 4)
    k_win = jnp.pad(kv[:, :, 4], ((0, 0), (WINDOW, 0), (0, 0), (0, 0)))
    v_win = jnp.pad(kv[:, :, 5], ((0, 0), (WINDOW, 0), (0, 0), (0, 0)))
    gates = jax.nn.sigmoid(gate_logits.astype(jnp.float32)).astype(q.dtype).reshape(bsz, seq, G, HG, 3)
    rb_group = rel_bias.reshape(REL_BUCKETS, G, HG).transpose(1, 0, 2)
    c_start = CMP_STRIDE * jnp.arange(n_cmp)
    c_end = c_start + CMP_BLOCK - 1
    s_start = SLC_BLOCK * jnp.arange(n_sb)
    cover = ((c_start[:, None] < s_start[None, :] + SLC_BLOCK) & (c_start[:, None] + CMP_BLOCK > s_start[None, :])).astype(jnp.float32)
    b_idx = jnp.arange(bsz)[:, None, None, None]
    g_idx = jnp.arange(G)[None, :, None, None]
    j_idx = jnp.arange(n_sb)

    def block(i):
        q0 = i * NSA_QBLOCK
        tq = q0 + jnp.arange(NSA_QBLOCK)
        qb = lax.dynamic_slice_in_dim(q, q0, NSA_QBLOCK, axis=1)
        gb = lax.dynamic_slice_in_dim(gates, q0, NSA_QBLOCK, axis=1)
        dist_c = tq[:, None] - c_end[None, :]
        valid_c = dist_c >= 0
        bias_c = rel_bias[t5_bucket(dist_c)].reshape(NSA_QBLOCK, n_cmp, G, HG).transpose(2, 3, 0, 1)
        lc = jnp.einsum('bqghd,bcgd->bghqc', qb, k_cmp, preferred_element_type=jnp.float32) * scale + bias_c
        pc = jax.nn.softmax(jnp.where(valid_c, lc, NEG_INF_2), axis=-1) * jnp.any(valid_c, axis=-1)[:, None]
        o_cmp = jnp.einsum('bghqc,bcgd->bqghd', pc.astype(q.dtype), v_cmp)
        imp = jnp.einsum('bghqc,cn->bgqn', pc, cover)
        cur = tq // SLC_BLOCK
        forced = (j_idx[None] == 0) | (j_idx[None] == cur[:, None]) | (j_idx[None] == cur[:, None] - 1)
        causal_s = s_start[None, :] <= tq[:, None]
        score = jnp.where(forced, FORCE_SCORE, jnp.where(causal_s, imp, -1.0))
        top_val, top_idx = lax.top_k(score, n_sel)
        ks = k_slc[b_idx, g_idx, top_idx]
        vs = v_slc[b_idx, g_idx, top_idx]
        k_pos = top_idx[..., None] * SLC_BLOCK + jnp.arange(SLC_BLOCK)
        dist_s = tq[None, None, :, None, None] - k_pos
        valid_s = ((top_val >= 0)[..., None] & (dist_s >= 0)).reshape(bsz, G, 1, NSA_QBLOCK, n_keys)
        bias_s = rb_group[g_idx[..., None], t5_bucket(dist_s)]
        bias_s = bias_s.transpose(0, 1, 5, 2, 3, 4).reshape(bsz, G, HG, NSA_QBLOCK, n_keys)
        ls = jnp.einsum('bqghd,bgqnkd->bghqnk', qb, ks, preferred_element_type=jnp.float32)
        ls = ls.reshape(bsz, G, HG, NSA_QBLOCK, n_keys) * scale + bias_s
        ps = jax.nn.softmax(jnp.where(valid_s, ls, NEG_INF_2), axis=-1)
        o_slc = jnp.einsum('bghqk,bgqkd->bqghd', ps.astype(q.dtype), vs.reshape(bsz, G, NSA_QBLOCK, n_keys, dh))
        kw = lax.dynamic_slice_in_dim(k_win, q0, kw_len, axis=1)
        vw = lax.dynamic_slice_in_dim(v_win, q0, kw_len, axis=1)
        k_pos_w = q0 - WINDOW + jnp.arange(kw_len)
        dist_w = tq[:, None] - k_pos_w[None, :]
        valid_w = (dist_w >= 0) & (dist_w < WINDOW) & (k_pos_w[None, :] >= 0)
        bias_w = rel_bias[t5_bucket(dist_w)].reshape(NSA_QBLOCK, kw_len, G, HG).transpose(2, 3, 0, 1)
        lw = jnp.einsum('bqghd,bkgd->bghqk', qb, kw, preferred_element_type=jnp.float32) * scale + bias_w
        pw = jax.nn.softmax(jnp.where(valid_w, lw, NEG_INF_2), axis=-1)
        o_win = jnp.einsum('bghqk,bkgd->bqghd', pw.astype(q.dtype), vw)
        out = gb[..., 0:1] * o_cmp + gb[..., 1:2] * o_slc + gb[..., 2:3] * o_win
        return out.reshape(bsz, NSA_QBLOCK, NSA_HEADS * dh)

    out = lax.map(block, jnp.arange(seq // NSA_QBLOCK))
    return out.transpose(1, 0, 2, 3).reshape(bsz, seq, NSA_HEADS * dh)

def mla_attention(c_q, c_kv, k_rope, positions, norm_q, norm_kv, w_uq, w_ukv):
    bsz, seq = c_q.shape[0], c_q.shape[1]
    q = (rmsnorm(c_q, norm_q) @ w_uq).reshape(bsz, seq, MLA_HEADS, QK_NOPE + QK_ROPE)
    kv = (rmsnorm(c_kv, norm_kv) @ w_ukv).reshape(bsz, seq, MLA_HEADS, QK_NOPE + V_DIM)
    q_nope, q_pe = q[..., :QK_NOPE], q[..., QK_NOPE:]
    k_nope, v = kv[..., :QK_NOPE], kv[..., QK_NOPE:]
    half = QK_ROPE // 2
    inv_freq = ROPE_THETA ** (-jnp.arange(half, dtype=jnp.float32) / half)
    ang = positions.astype(jnp.float32)[..., None] * inv_freq
    cos, sin = jnp.cos(ang), jnp.sin(ang)
    q_pe = apply_rope(q_pe, cos[:, :, None, :], sin[:, :, None, :])
    k_pe = apply_rope(k_rope, cos, sin)
    scale = (QK_NOPE + QK_ROPE) ** -0.5
    k_idx = jnp.arange(seq)

    def block(i):
        q0 = i * ATTN_QBLOCK
        qn = lax.dynamic_slice_in_dim(q_nope, q0, ATTN_QBLOCK, axis=1)
        qp = lax.dynamic_slice_in_dim(q_pe, q0, ATTN_QBLOCK, axis=1)
        logits = (jnp.einsum('bqhd,bkhd->bhqk', qn, k_nope, preferred_element_type=jnp.float32)
                  + jnp.einsum('bqhr,bkr->bhqk', qp, k_pe, preferred_element_type=jnp.float32)) * scale
        causal = k_idx[None, :] <= (q0 + jnp.arange(ATTN_QBLOCK))[:, None]
        p = jax.nn.softmax(jnp.where(causal, logits, NEG_INF_2), axis=-1)
        return jnp.einsum('bhqk,bkhd->bqhd', p.astype(v.dtype), v)

    out = lax.map(block, jnp.arange(seq // ATTN_QBLOCK))
    return out.transpose(1, 0, 2, 3, 4).reshape(bsz, seq, MLA_HEADS * V_DIM)

def memory_cross_attention(h, mem_n, w_q, w_kv, w_o):
    bsz, seq = h.shape[0], h.shape[1]
    m_len = mem_n.shape[1]
    q = (h @ w_q).reshape(bsz, seq, XATTN_HEADS, XATTN_HEAD_DIM)
    kv = (mem_n @ w_kv).reshape(bsz, m_len, 2, XATTN_HEADS, XATTN_HEAD_DIM)
    logits = jnp.einsum('bqhd,bmhd->bhqm', q, kv[:, :, 0], preferred_element_type=jnp.float32) * XATTN_HEAD_DIM ** -0.5
    p = jax.nn.softmax(logits, axis=-1)
    o = jnp.einsum('bhqm,bmhd->bqhd', p.astype(h.dtype), kv[:, :, 1]).reshape(bsz, seq, XATTN_HEADS * XATTN_HEAD_DIM)
    return o @ w_o

def second_inputs(seed: int = 0) -> dict:
    key = jax.random.key(seed)
    keys = jax.random.split(key, 48)
    counter = [0]
    L = DEPTH_2

    def nxt():
        k = keys[counter[0]]
        counter[0] += 1
        return k

    def dense(shape, fan_in):
        return jax.random.normal(nxt(), shape, jnp.float32) * fan_in ** -0.5

    def gain(shape):
        return 1.0 + 0.02 * jax.random.normal(nxt(), shape, jnp.float32)

    def small(shape):
        return 0.02 * jax.random.normal(nxt(), shape, jnp.float32)

    dh = NSA_HEAD_DIM
    x = jax.random.normal(nxt(), (BATCH, SEQ, D_MODEL), jnp.float32)
    mem = jax.random.normal(nxt(), (BATCH, MEM_LEN, D_MODEL), jnp.float32)
    offsets = jax.random.randint(nxt(), (BATCH, 1), 0, 2048, dtype=jnp.int32)
    positions = offsets + jnp.arange(SEQ, dtype=jnp.int32)[None, :]
    return {
        'x': x,
        'mem': mem,
        'positions': positions,
        'rel_bias': 0.1 * jax.random.normal(nxt(), (REL_BUCKETS, NSA_HEADS), jnp.float32),
        'norm_mix': gain((L, D_MODEL)),
        'norm_xattn': gain((L, D_MODEL)),
        'norm_mem': gain((L, D_MODEL)),
        'norm_ffn': gain((L, D_MODEL)),
        'norm_final': gain((D_MODEL,)),
        'w_in': dense((L, D_MODEL, IN_COLS), D_MODEL),
        'conv_w': dense((L, CONV_WIDTH, CONV_CH), CONV_WIDTH),
        'conv_b': small((L, CONV_CH)),
        'conv_ln_g': gain((L, CONV_CH)),
        'conv_ln_b': small((L, CONV_CH)),
        'w_branch_conv': dense((L, CONV_CH, D_MODEL), CONV_CH),
        'cmp_pos_k': dense((L, CMP_BLOCK, dh), 4),
        'cmp_w1_k': dense((L, CMP_BLOCK * dh, CMP_HIDDEN), CMP_BLOCK * dh),
        'cmp_b1_k': small((L, CMP_HIDDEN)),
        'cmp_w2_k': dense((L, CMP_HIDDEN, dh), CMP_HIDDEN),
        'cmp_pos_v': dense((L, CMP_BLOCK, dh), 4),
        'cmp_w1_v': dense((L, CMP_BLOCK * dh, CMP_HIDDEN), CMP_BLOCK * dh),
        'cmp_b1_v': small((L, CMP_HIDDEN)),
        'cmp_w2_v': dense((L, CMP_HIDDEN, dh), CMP_HIDDEN),
        'w_branch_nsa': dense((L, NSA_HEADS * dh, D_MODEL), NSA_HEADS * dh),
        'mla_norm_q': gain((L, Q_RANK)),
        'mla_norm_kv': gain((L, KV_RANK)),
        'w_uq': dense((L, Q_RANK, MLA_HEADS * (QK_NOPE + QK_ROPE)), Q_RANK),
        'w_ukv': dense((L, KV_RANK, MLA_HEADS * (QK_NOPE + V_DIM)), KV_RANK),
        'w_branch_mla': dense((L, MLA_HEADS * V_DIM, D_MODEL), MLA_HEADS * V_DIM),
        'w_out': dense((L, D_MODEL, D_MODEL), D_MODEL),
        'w_xq': dense((L, D_MODEL, XATTN_HEADS * XATTN_HEAD_DIM), D_MODEL),
        'w_xkv': dense((L, D_MODEL, 2 * XATTN_HEADS * XATTN_HEAD_DIM), D_MODEL),
        'w_xo': dense((L, XATTN_HEADS * XATTN_HEAD_DIM, D_MODEL), XATTN_HEADS * XATTN_HEAD_DIM),
        'w_gate_up': dense((L, D_MODEL, 2 * FFN_HIDDEN), D_MODEL),
        'w_down': dense((L, FFN_HIDDEN, D_MODEL), FFN_HIDDEN),
    }

def second_block(x, mem, positions, rel_bias, norm_mix, norm_xattn, norm_mem, norm_ffn, norm_final,
              w_in, conv_w, conv_b, conv_ln_g, conv_ln_b, w_branch_conv,
              cmp_pos_k, cmp_w1_k, cmp_b1_k, cmp_w2_k, cmp_pos_v, cmp_w1_v, cmp_b1_v, cmp_w2_v, w_branch_nsa,
              mla_norm_q, mla_norm_kv, w_uq, w_ukv, w_branch_mla, w_out,
              w_xq, w_xkv, w_xo, w_gate_up, w_down):
    split_at = [int(v) for v in np.cumsum(IN_SIZES)[:-1]]
    for layer in range(DEPTH_2):
        h = rmsnorm(x, norm_mix[layer])
        z = h @ w_in[layer]
        u_glu, q_nsa, kv_nsa, g_nsa, c_q, c_kv, k_rope, g_merge = jnp.split(z, split_at, axis=-1)
        y_conv = conformer_conv(u_glu, conv_w[layer], conv_b[layer], conv_ln_g[layer], conv_ln_b[layer], w_branch_conv[layer])
        y_nsa = nsa_attention(q_nsa, kv_nsa, g_nsa, rel_bias,
                              cmp_pos_k[layer], cmp_w1_k[layer], cmp_b1_k[layer], cmp_w2_k[layer],
                              cmp_pos_v[layer], cmp_w1_v[layer], cmp_b1_v[layer], cmp_w2_v[layer]) @ w_branch_nsa[layer]
        y_mla = mla_attention(c_q, c_kv, k_rope, positions, mla_norm_q[layer], mla_norm_kv[layer],
                              w_uq[layer], w_ukv[layer]) @ w_branch_mla[layer]
        g = jax.nn.sigmoid(g_merge.astype(jnp.float32)).astype(x.dtype)
        g_conv, g_attn, g_mla = jnp.split(g, 3, axis=-1)
        x = x + (g_conv * y_conv + g_attn * y_nsa + g_mla * y_mla) @ w_out[layer]
        x = x + memory_cross_attention(rmsnorm(x, norm_xattn[layer]), rmsnorm(mem, norm_mem[layer]),
                                       w_xq[layer], w_xkv[layer], w_xo[layer])
        gate, up = jnp.split(rmsnorm(x, norm_ffn[layer]) @ w_gate_up[layer], 2, axis=-1)
        x = x + (jax.nn.silu(gate) * up) @ w_down[layer]
    return rmsnorm(x, norm_final)


def setup_inputs(seed=0):
    out = dict(first_inputs(seed))
    for name, value in second_inputs(seed + 1).items():
        if name != "x":
            out[name + "_2"] = value
    return out


def reference(
    x, norm_g, ff1_w_in, ff1_w_out, ff2_w_in, ff2_w_out, a_w_qkv, a_rel_bias, a_w_o, b_w_in,
    b_ln_g, b_ln_b, b_w_s, b_b_s, b_w_o, c_w_qkv, c_lambda, c_subln_g, c_w_o, mem_2,
    positions_2, rel_bias_2, norm_mix_2, norm_xattn_2, norm_mem_2, norm_ffn_2, norm_final_2,
    w_in_2, conv_w_2, conv_b_2, conv_ln_g_2, conv_ln_b_2, w_branch_conv_2, cmp_pos_k_2,
    cmp_w1_k_2, cmp_b1_k_2, cmp_w2_k_2, cmp_pos_v_2, cmp_w1_v_2, cmp_b1_v_2, cmp_w2_v_2,
    w_branch_nsa_2, mla_norm_q_2, mla_norm_kv_2, w_uq_2, w_ukv_2, w_branch_mla_2, w_out_2,
    w_xq_2, w_xkv_2, w_xo_2, w_gate_up_2, w_down_2,
):
    x = first_block(
        x, norm_g, ff1_w_in, ff1_w_out, ff2_w_in, ff2_w_out, a_w_qkv, a_rel_bias, a_w_o, b_w_in,
        b_ln_g, b_ln_b, b_w_s, b_b_s, b_w_o, c_w_qkv, c_lambda, c_subln_g, c_w_o,
    )
    return second_block(
        x, mem_2, positions_2, rel_bias_2, norm_mix_2, norm_xattn_2, norm_mem_2, norm_ffn_2,
        norm_final_2, w_in_2, conv_w_2, conv_b_2, conv_ln_g_2, conv_ln_b_2, w_branch_conv_2,
        cmp_pos_k_2, cmp_w1_k_2, cmp_b1_k_2, cmp_w2_k_2, cmp_pos_v_2, cmp_w1_v_2, cmp_b1_v_2,
        cmp_w2_v_2, w_branch_nsa_2, mla_norm_q_2, mla_norm_kv_2, w_uq_2, w_ukv_2,
        w_branch_mla_2, w_out_2, w_xq_2, w_xkv_2, w_xo_2, w_gate_up_2, w_down_2,
    )


_drawn_inputs = setup_inputs


def setup_inputs(seed=0):
    import zlib

    import numpy as np

    out = dict(_drawn_inputs(seed))
    spreads = {}
    factors = {'b_ln_g': 3.661,
     'b_ln_b': 3.528,
     'rel_bias_2': 8.0,
     'norm_mix_2': 8.0,
     'norm_xattn_2': 8.0,
     'norm_mem_2': 8.0,
     'norm_ffn_2': 6.562,
     'norm_final_2': 2.704,
     'conv_b_2': 7.538,
     'conv_ln_g_2': 8.0,
     'conv_ln_b_2': 8.0,
     'cmp_pos_k_2': 8.0,
     'cmp_w1_k_2': 4.474,
     'cmp_b1_k_2': 8.0,
     'cmp_w2_k_2': 4.443,
     'cmp_b1_v_2': 8.0,
     'mla_norm_q_2': 8.0,
     'mla_norm_kv_2': 8.0}
    for name, (base, spread) in spreads.items():
        noise = np.random.default_rng([zlib.crc32(name.encode()), seed]).standard_normal(out[name].shape)
        drawn = base * np.exp(spread * noise) if base else spread * noise
        out[name] = jnp.asarray(drawn.astype(out[name].dtype))
    for name, factor in factors.items():
        out[name] = (out[name] * factor).astype(out[name].dtype)
    return out
```

```python
import math
from contextlib import ExitStack

import concourse.bass as bass
from concourse import mybir

F32 = mybir.dt.float32
I32 = mybir.dt.int32
ALU = mybir.AluOpType
ACT = mybir.ActivationFunctionType
AX = mybir.AxisListType

P = 128
S = 256
NT = S // P
D = 1024
KD = D // P
DEPTH = 4
DEPTH2 = 2
D_FF = 2816
KF = D_FF // P
EPS = 1e-6
NEG = -1e30
CHUNK = 64
HEADS_A = 16
DH = 64
REL_CLIP = 128
HEADS_C = 8
GROUPS_B = 8
CONV_CH = 512
CT = CONV_CH // P
TAPS = 31
NSA_HEADS = 8
CMP_BLOCK = 32
CMP_STRIDE = 16
CMP_HIDDEN = 256
N_CMP = (S - CMP_BLOCK) // CMP_STRIDE + 1
MLA_HEADS = 4
Q_RANK = 384
KV_RANK = 256
NOPE = 128
ROPE = 64
V_DIM = 128
X_HEADS = 4
ROPE_THETA = 10000.0
BUCKETS = 32
COL_GLU, COL_Q, COL_KV, COL_REST = 0, 1024, 1536, 2176
COL_MERGE = 3032
N_REST = COL_MERGE - COL_REST
R_VWIN, R_GATE, R_CQ, R_CKV, R_KPE = 0, 128, 152, 536, 792
TW = 257
SLOTS = 3
SLOT = 4096
MAGIC = 1.5 * 2 ** 23


class Signal:

    def __init__(self, sem, reached, step=1):
        self.sem, self.reached, self.step, self.count = sem, reached, step, 0

    def next(self, key):
        self.count += self.step
        self.reached[key] = self.count
        return self.step

    def at(self, key):
        return self.reached.get(key, 1)

    def has(self, key):
        return key in self.reached


class Banks:

    def __init__(self, tiles, taken, readers):
        self.tiles, self.taken, self.readers, self.n, self.owner = tiles, taken, readers, 0, {}

    def take(self, pe, key):
        i = self.n % len(self.tiles)
        self.n += 1
        if i in self.owner:
            for reader in self.readers:
                if reader.has(self.owner[i]):
                    pe.wait_ge(reader.sem, reader.at(self.owner[i]))
        self.owner[i] = key
        self.taken[key] = i
        return self.tiles[i]

    def of(self, key):
        return self.tiles[self.taken.get(key, 0)]


def t5_bucket(d):
    exact = BUCKETS // 2
    if d < exact:
        return d
    return min(exact + int(math.log(d / exact) / math.log(128 / exact) * (BUCKETS - exact)), BUCKETS - 1)


def weight_chunks(w):
    out = []

    def cols(key, m, c0, n):
        out.append((key, [(lambda s, n=n, k=m.shape[0] // P: s[:, 0:k * n].rearrange("p (k n) -> p k n", k=k),
                           m[:, c0:c0 + n].rearrange("(k p) n -> p k n", p=P))]))

    def rows(key, m, k0, nk):
        n = m.shape[1]
        out.append((key, [(lambda s, n=n, nk=nk: s[:, 0:nk * n].rearrange("p (k n) -> p k n", k=nk),
                           m[k0 * P:(k0 + nk) * P, :].rearrange("(k p) n -> p k n", p=P))]))

    def ffn(key, w_in, w_out):
        for j in range(KF // 2):
            out.append(((key, "in", j), [
                (lambda s, u=u: s[:, :].rearrange("p (k u n) -> p k u n", k=KD, u=2)[:, :, u, :],
                 w_in[:, u * D_FF + j * 256:u * D_FF + (j + 1) * 256].rearrange("(k p) n -> p k n", p=P))
                for u in range(2)]))
        for m in range(0, KF, 4):
            rows((key, "out", m), w_out, m, min(4, KF - m))

    for i in range(DEPTH):
        ffn(("ff1", i), w["ff1_w_in"][i], w["ff1_w_out"][i])
        kind, j = i % 3, i // 3
        win, wo = [("a_w_qkv", "a_w_o"), ("b_w_in", "b_w_o"), ("c_w_qkv", "c_w_o")][kind]
        for c in range(w[win].shape[2] // 512):
            cols((("mix", i), "in", c), w[win][j], c * 512, 512)
        for c in range(2):
            cols((("mix", i), "out", c), w[wo][j], c * 512, 512)
        ffn(("ff2", i), w["ff2_w_in"][i], w["ff2_w_out"][i])
    for l in range(DEPTH2):
        w_in = w["w_in_2"][l]
        for c in range(2):
            cols(("l2", l, "glu", c), w_in, c * 512, 512)
        out.append((("l2", l, "q"), [
            (lambda s, c=c, g=g: s[:, :].rearrange("p (k c g d) -> p k c g d", k=KD, c=4, g=2)[:, :, c, g, :],
             w_in[:, COL_Q + (4 * g + c) * DH:COL_Q + (4 * g + c + 1) * DH].rearrange("(k p) d -> p k d", p=P))
            for c in range(4) for g in range(2)]))
        cols(("l2", l, "kv", 0), w_in, COL_KV, 512)
        cols(("l2", l, "kv", 1), w_in, COL_KV + 512, 512)
        cols(("l2", l, "kv", 2), w_in, COL_KV + 1024, COL_MERGE - COL_KV - 1024)
        for kv in range(2):
            rows(("l2", l, "cmp", kv), w[("cmp_w1_k_2", "cmp_w1_v_2")[kv]][l], 0, 16)
        for c in range(6):
            cols(("l2", l, "merge", c), w_in, COL_MERGE + c * 512, 512)
        rows(("l2", l, "conv"), w["w_branch_conv_2"][l], 0, CT)
        rows(("l2", l, "nsa"), w["w_branch_nsa_2"][l], 0, 4)
        rows(("l2", l, "uq"), w["w_uq_2"][l], 0, Q_RANK // P)
        rows(("l2", l, "ukv"), w["w_ukv_2"][l], 0, KV_RANK // P)
        rows(("l2", l, "mla"), w["w_branch_mla_2"][l], 0, 4)
        for c in range(2):
            cols(("l2", l, "out", c), w["w_out_2"][l], c * 512, 512)
        cols(("l2", l, "xq"), w["w_xq_2"][l], 0, 512)
        cols(("l2", l, "xk"), w["w_xkv_2"][l], 0, 512)
        cols(("l2", l, "xv"), w["w_xkv_2"][l], 512, 512)
        rows(("l2", l, "xo"), w["w_xo_2"][l], 0, 4)
        ffn(("ff3", l), w["w_gate_up_2"][l], w["w_down_2"][l])
    return out


def build(nc, w, out, plan, stop=None):
    chunks = weight_chunks(w)
    chunk_index = {key: n for n, (key, _) in enumerate(chunks)}

    with ExitStack() as ctx:
        def sb(name, shape, dt=F32):
            return ctx.enter_context(nc.sbuf_tensor("sb_" + name, shape, dt))

        def signal(name, step=1):
            return Signal(ctx.enter_context(nc.semaphore(name)), plan.setdefault(name, {}), step)

        slots = [sb(f"slot{i}", [P, SLOT]) for i in range(SLOTS)]
        x = sb("x", [P, NT, D])
        hT = sb("hT", [P, KD, S])
        xn = sb("xn", [P, NT, D])
        gain_row = [sb(f"gain_row{i}", [P, D]) for i in range(2)]
        o_rows = sb("o_rows", [P, NT, D])
        oT = sb("oT", [P, KD, S])
        wide = sb("wide", [P, 6144])
        hidT = wide[:, 0:KF * S].rearrange("p (k s) -> p k s", k=KF)
        merge_gate = wide[:, :].rearrange("p (t n) -> p t n", t=NT)
        xqT = wide[:, 0:1024].rearrange("p (h s) -> p h s", h=X_HEADS)
        xkT = wide[:, 1024:2048].rearrange("p (h s) -> p h s", h=X_HEADS)
        xv = wide[:, 2048:3072].rearrange("p (t n) -> p t n", t=NT)
        memT = wide[:, 3072:5120].rearrange("p (k s) -> p k s", k=KD)

        arena = sb("arena", [P, 15500])
        used = [0]

        def part(n, pattern=None, **dims):
            a = arena[:, used[0]:used[0] + n]
            used[0] += n
            assert used[0] <= 15500
            return a.rearrange(pattern, **dims) if pattern else a

        qkT = part(16 * S, "p (c s) -> p c s", c=16)
        v_rows = part(NT * D, "p (t n) -> p t n", t=NT)
        relA = part(HEADS_A * TW, "p (h w) -> p h w", h=HEADS_A)
        used[0] = 0
        u_rows = part(NT * D, "p (t n) -> p t n", t=NT)
        g_rows = part(NT * D, "p (t n) -> p t n", t=NT)
        ws = part(GROUPS_B * P, "p (g s) -> p g s", g=GROUPS_B)
        wsT = part(GROUPS_B * P, "p (g s) -> p g s", g=GROUPS_B)
        used[0] = 12000
        relC = part(HEADS_C * TW, "p (h w) -> p h w", h=HEADS_C)
        used[0] = 0
        relN = part(NSA_HEADS * TW, "p (h w) -> p h w", h=NSA_HEADS)
        causal = part(TW)
        zeros = part(S)
        rest = part(NT * N_REST, "p (t n) -> p t n", t=NT)
        qsT = part(4 * S, "p (c s) -> p c s", c=4)
        kslcT = part(S)
        kwinT = part(S)
        vslc = part(NT * P, "p (t n) -> p t n", t=NT)
        tokT = part(2 * S, "p (v s) -> p v s", v=2)
        tok2 = part(4 * S, "p (v g s) -> p v g s", v=2, g=2)
        blk = part(2 * 16 * 30, "p (v j g c) -> p v j g c", v=2, j=16, g=2)
        hid_c = part(2 * 2 * 30, "p (v f n) -> p v f n", v=2, f=2)
        kcT = part(32)
        vc = part(2 * DH, "p (g d) -> p g d", g=2)
        merged = part(NT * D, "p (t n) -> p t n", t=NT)
        w2k = part(2 * 2 * DH, "p (f u d) -> p f u d", f=2, u=2)
        w2v = part(2 * DH, "p (f d) -> p f d", f=2)
        here = used[0]
        aT = part(CT * S, "p (c s) -> p c s", c=CT)
        bT = part(CT * S, "p (c s) -> p c s", c=CT)
        glu = part(CT * (S + TAPS - 1), "p (c s) -> p c s", c=CT)
        convT = part(CT * S, "p (c s) -> p c s", c=CT)
        used[0] = here
        qnT = part(MLA_HEADS * S, "p (h s) -> p h s", h=MLA_HEADS)
        knT = part(MLA_HEADS * S, "p (h s) -> p h s", h=MLA_HEADS)
        qpT = part(2 * S, "p (h s) -> p h s", h=2)
        kpT = part(S)
        vm = part(NT * 512, "p (t n) -> p t n", t=NT)

        ident = sb("ident", [P, P])
        minus_half = sb("minus_half", [P, 32])
        gains = sb("gains", [P, 3, P])
        convw = sb("convw", [P, 2, P])
        gT = sb("gT", [P, 3, P])
        convwT = sb("convwT", [P, 2, P])
        lines = oT[0:HEADS_A, 0:5, :].rearrange("p k s -> p (k s)")[:, 0:9 * P].rearrange("p (j w) -> p j w", j=3)
        onehot = sb("onehot", [BUCKETS, 3 * P])
        bias2 = sb("bias2", [BUCKETS, NSA_HEADS])
        lam_in = sb("lam_in", [P, 4, DH])
        lam = sb("lam", [P, 8])
        subln = sb("subln", [P, P])
        pos_i = sb("pos_i", [P, NT], I32)
        pos_f = sb("pos_f", [P, NT])
        freq = sb("freq", [P, 32])
        cosb = sb("cosb", [P, NT, 32])
        sinb = sb("sinb", [P, NT, 32])
        valid = sb("valid", [P, NT])
        square = sb("square", [P, D])
        rtmp = square[:, :].rearrange("p (n m) -> p n m", n=4)
        ssum = sb("ssum", [P, 8])
        mean_sq = sb("mean_sq", [P, 16])
        rstd = sb("rstd", [P, 16])
        stats = sb("stats", [P, 2, 6])
        moments = sb("moments", [P, NT, 2])
        tmp = sb("tmp", [P, 512])
        tmp2 = sb("tmp2", [P, 512])
        sc = sb("sc", [P, 3, S])
        nmax = sb("nmax", [P, 3])
        pr = sb("pr", [P, 3, S])
        prT = sb("prT", [P, 2, S])
        silu = prT
        sums = sb("sums", [P, NT, 32])
        inv = sb("inv", [P, NT, 32])
        line_dram = [nc.dram_tensor(f"line_dram{i}", [HEADS_A, 3 * P], F32).ap() for i in range(3)]

        psum = [ctx.enter_context(nc.psum_tensor(f"bank{i}", [P, 512], F32)) for i in range(8)]

        slot_loaded = [signal(f"slot{i}_loaded", 16) for i in range(SLOTS)]
        consts_loaded = signal("consts_loaded", 16)
        lines_stored = signal("lines_stored", 16)
        table_loaded = signal("table_loaded", 16)
        gain_loaded = [signal(f"gain{i}_loaded", 16) for i in range(2)]
        small_loaded = signal("small_loaded", 16)
        out_stored = signal("out_stored", 16)
        matmul_done = signal("matmul_done")
        transposed = signal("transposed")
        act_read = signal("act_read")
        dve_read = signal("dve_read")
        squared = signal("squared")
        dve_step = signal("dve_step")
        act_step = signal("act_step")
        pool_step = signal("pool_step")
        pe_step = signal("pe_step")
        scored = signal("scored")
        maxed = signal("maxed")
        weighed = signal("weighed")
        mean_ready = signal("mean_ready")
        rstd_ready = signal("rstd_ready")
        x_ready = signal("x_ready")
        rows_ready = signal("rows_ready")
        tok_loaded = signal("tok_loaded", 16)
        mem_loaded = signal("mem_loaded", 16)
        spatial_loaded = signal("spatial_loaded", 16)

        readers = (act_read, dve_read)
        G = Banks(psum[0:4], plan.setdefault("bank_g", {}), readers)
        SB = Banks(psum[4:6], plan.setdefault("bank_s", {}), readers)
        TB = Banks(psum[6:8], plan.setdefault("bank_t", {}), readers)
        chunk_end = plan.setdefault("chunk_end", {})

        col = {}
        loads = []

        tile, row = 0, 0
        gain_tiles = []

        def put(key, ap, n):
            nonlocal tile, row
            if row + n > P:
                gain_tiles.append(row)
                tile, row = tile + 1, 0
            col[key] = (tile, row)
            loads.append((gains[row:row + n, tile, :], ap))
            row += n

        for i in range(DEPTH):
            for n in (0, 2, 4):
                put(("g", i, n), w["norm_g"][i, n].rearrange("(a p) -> a p", p=P), KD)
        for l in range(DEPTH2):
            for name in ("norm_mix_2", "norm_xattn_2", "norm_mem_2", "norm_ffn_2"):
                put((name, l), w[name][l].rearrange("(a p) -> a p", p=P), KD)
        for l in range(DEPTH2):
            for name, n in (("conv_b_2", 4), ("conv_ln_g_2", 4), ("conv_ln_b_2", 4), ("mla_norm_q_2", 3),
                            ("mla_norm_kv_2", 2), ("cmp_b1_k_2", 2), ("cmp_b1_v_2", 2)):
                put((name, l), w[name][l].rearrange("(a p) -> a p", p=P), n)
            for name in ("cmp_pos_k_2", "cmp_pos_v_2"):
                put((name, l), w[name][l].rearrange("(a b) d -> a (b d)", b=2), 16)
        put("b_b_s", w["b_b_s"][0], GROUPS_B)
        assert tile <= 2
        gain_tiles.append(row)

        def gcol(key, k=0):
            t, r = col[key]
            return gT[:, t, r + k:r + k + 1]

        row_gains = []
        for i in range(DEPTH):
            row_gains.append((("g", i, 1), w["norm_g"][i, 1]))
            if i % 3 == 1:
                row_gains += [("ln_g", w["b_ln_g"][0]), ("ln_b", w["b_ln_b"][0])]
            row_gains += [(("g", i, 3), w["norm_g"][i, 3]), (("g", i, 5), w["norm_g"][i, 5])]
        row_gains.append(("final", w["norm_final_2"]))
        gain_n = {key: n for n, (key, _) in enumerate(row_gains)}
        gain_for = {("ff1", i): ("g", i, 1) for i in range(DEPTH)}
        gain_for |= {("mix", i): ("g", i, 3) for i in range(DEPTH)}
        gain_for |= {("ff2", i): ("g", i, 5) for i in range(DEPTH)}

        block = ctx.enter_context(nc.Block())

        def slot_of(key):
            return slots[chunk_index[key] % SLOTS]

        def view(key):
            s = slot_of(key)
            return chunks[chunk_index[key]][1][0][0](s)

        stages = []
        for i in range(DEPTH):
            stages += [("ff1", i), ("mix", i), ("ff2", i)]
        for l in range(DEPTH2):
            stages += [("l2", l), ("xattn", l), ("ff3", l)]
        if stop is not None:
            stages = stages[:stop]
        last = stages[-1]

        def stage_of(key):
            if key[0] == "l2":
                return ("xattn", key[1]) if key[2] in ("xq", "xk", "xv", "xo") else ("l2", key[1])
            return key[0]

        def stage_loads(sp, st, small):
            kind, i = st
            if kind == "mix" and i % 3 == 0:
                sp.wait_ge(lines_stored.sem, lines_stored.at("l"))
                if i:
                    sp.wait_ge(x_ready.sem, x_ready.at((("mix", i - 1), 1)))
                sp.dma_start(relA, bass.AP(tensor=line_dram[i // 3].tensor, offset=0,
                                           ap=[[1, P], [3 * P, HEADS_A], [1, TW]])) \
                    .then_inc(table_loaded.sem, table_loaded.next(st))
            if kind == "l2":
                if i == 0:
                    sp.wait_ge(x_ready.sem, x_ready.at((("mix", DEPTH - 1), 1)))
                    sp.dma_start(relN, bass.AP(tensor=line_dram[2].tensor, offset=0,
                                               ap=[[1, P], [3 * P, NSA_HEADS], [1, TW]])) \
                        .then_inc(table_loaded.sem, table_loaded.next(st))
                else:
                    sp.wait_ge(x_ready.sem, x_ready.at((("l2", i - 1), 1)))
                src = w["cmp_w2_k_2"][i].rearrange("(f p) d -> p f d", p=P)
                small(st, [(w2k[:, :, 0, :], src), (w2k[:, :, 1, :], src),
                           (w2v, w["cmp_w2_v_2"][i].rearrange("(f p) d -> p f d", p=P))])

        @block.sync
        def _(sp):
            def small(key, pairs):
                for dst, src in pairs:
                    sp.dma_start(dst, src, allow_slow_non_contiguous=True).then_inc(small_loaded.sem, small_loaded.next(key))

            sp.dma_start(x[:, :, :], w["x"][0].rearrange("(t p) d -> p t d", p=P)).then_inc(consts_loaded.sem, consts_loaded.next("c"))
            for dst, src in loads:
                sp.dma_start(dst, src).then_inc(consts_loaded.sem, consts_loaded.next("c"))
            for l in range(DEPTH2):
                sp.dma_start(convw[0:TAPS * CT, l, :], w["conv_w_2"][l].rearrange("t (c p) -> (t c) p", p=P)) \
                    .then_inc(consts_loaded.sem, consts_loaded.next("c"))
            sp.dma_start(bias2[:, :], w["rel_bias_2"]).then_inc(consts_loaded.sem, consts_loaded.next("c"))
            sp.dma_start(lam_in[:, :, :].rearrange("p a d -> p (a d)"),
                         w["c_lambda"].rearrange("o a d -> o (a d)").broadcast_to([P, 4 * DH])) \
                .then_inc(consts_loaded.sem, consts_loaded.next("c"))
            sp.dma_start(subln[:, :], w["c_subln_g"].broadcast_to([P, P])).then_inc(consts_loaded.sem, consts_loaded.next("c"))
            sp.dma_start(pos_i[:, :], w["positions_2"][0].rearrange("(t p) -> p t", p=P), allow_slow_non_contiguous=True) \
                .then_inc(consts_loaded.sem, consts_loaded.next("c"))
            for j in range(2):
                sp.dma_start(lines[:, j, 0:2 * REL_CLIP + 1], w["a_rel_bias"][j]).then_inc(consts_loaded.sem, consts_loaded.next("c"))
            sp.wait_ge(dve_step.sem, dve_step.at("lines"))
            for j in range(3):
                n = HEADS_A if j < 2 else NSA_HEADS
                sp.dma_start(line_dram[j][0:n, 0:3 * P], lines[0:n, j, 0:3 * P]).then_inc(lines_stored.sem, lines_stored.next("l"))

            finished = []
            for n, (key, parts) in enumerate(chunks):
                st = stage_of(key)
                if st not in stages:
                    continue
                if st not in finished:
                    finished.append(st)
                    stage_loads(sp, st, small)
                if n >= SLOTS:
                    sp.wait_ge(matmul_done.sem, matmul_done.at(chunk_end.get(chunks[n - SLOTS][0])))
                slot = slots[n % SLOTS]
                for dst, src in parts:
                    sp.dma_start(dst(slot), src).then_inc(slot_loaded[n % SLOTS].sem, slot_loaded[n % SLOTS].next(key))
            if last == ("ff3", DEPTH2 - 1):
                sp.wait_ge(rows_ready.sem, rows_ready.at("final"))
                sp.dma_start(out[0].rearrange("(t p) d -> p t d", p=P), xn[:, :, :]).then_inc(out_stored.sem, out_stored.next("o"))
            else:
                sp.wait_ge(x_ready.sem, x_ready.at((last, 1)))
                sp.dma_start(out[0].rearrange("(t p) d -> p t d", p=P), x[:, :, :]).then_inc(out_stored.sem, out_stored.next("o"))
            if stop is not None:
                sp.wait_ge(lines_stored.sem, lines_stored.at("l"))
                for sig in (*gain_loaded, table_loaded, small_loaded, tok_loaded, mem_loaded, spatial_loaded):
                    if sig.reached:
                        sp.wait_ge(sig.sem, max(sig.reached.values()))
            sp.wait_ge(out_stored.sem, out_stored.at("o"))


        def settle(eng, ins, sig, key=None):
            ins.then_inc(sig.sem, sig.next(key if key is not None else ("n", sig.count)))
            eng.wait_ge(sig.sem, sig.count)

        def rev(table, t, kn):
            top = P * (t + 1)
            return table[:, top:top - kn:-1]

        def units_of(st):
            kind, i = st
            units = []
            if kind == "mix":
                for t in range(NT):
                    for s in range(16):
                        half = slice(DH * (s % 2), DH * (s % 2) + DH)
                        if i % 3 == 0:
                            table, v0, width = relA[:, s, :], s * DH, DH
                        else:
                            table, v0, width = relC[:, s // 2, :], (s // 2) * P, P
                        kn = P * (t + 1)
                        per = 512 // width
                        units.append(dict(
                            qk=[(qkT[half, s // 2, t * P:(t + 1) * P], qkT[half, 8 + s // 2, 0:kn])],
                            t=t, kn=kn, bias=rev(table, t, kn), scale=DH ** -0.5,
                            v=[v_rows[:, b, v0:v0 + width] for b in range(t + 1)],
                            acc=(st, "o", t, s // per), c0=(s % per) * width, width=width, col=s))
            elif kind == "l2":
                for t in range(NT):
                    for br in range(3):
                        for h in range(NSA_HEADS):
                            g = h // 4
                            half = slice(DH * g, DH * g + DH)
                            q = qsT[half, h % 4, t * P:(t + 1) * P]
                            if br == 0:
                                kn = min(N_CMP, (P * (t + 1) - CMP_BLOCK) // CMP_STRIDE + 1)
                                k = kcT[half, g * N_CMP:g * N_CMP + kn]
                                top = P * (t + 1) - (CMP_BLOCK - 1)
                                bias = relN[:, h, top:top - CMP_STRIDE * (kn - 1) - 1:-CMP_STRIDE]
                                v = [vc[0:kn, g, :]]
                            else:
                                kn = P * (t + 1)
                                k = (kslcT if br == 1 else kwinT)[half, 0:kn]
                                bias = rev(relN[:, h, :], t, kn)
                                v = [vslc[:, b, g * DH:g * DH + DH] if br == 1 else
                                     rest[:, b, R_VWIN + g * DH:R_VWIN + g * DH + DH] for b in range(t + 1)]
                            units.append(dict(qk=[(q, k)], t=t, kn=kn, bias=bias, scale=DH ** -0.5, v=v,
                                              acc=(st, "o", t, br), c0=h * DH, width=DH, col=br * 8 + h))
            elif kind == "mla":
                for t in range(NT):
                    for h in range(MLA_HEADS):
                        half = slice(DH * (h % 2), DH * (h % 2) + DH)
                        kn = P * (t + 1)
                        tok = slice(t * P, (t + 1) * P)
                        units.append(dict(
                            qk=[(qnT[:, h, tok], knT[:, h, 0:kn]), (qpT[half, h // 2, tok], kpT[half, 0:kn])],
                            t=t, kn=kn, bias=rev(causal, t, kn), scale=(NOPE + ROPE) ** -0.5,
                            v=[vm[:, b, h * P:(h + 1) * P] for b in range(t + 1)],
                            acc=(st, "o", t, 0), c0=h * P, width=P, col=24 + h))
            elif kind == "xattn":
                for t in range(NT):
                    for h in range(X_HEADS):
                        units.append(dict(
                            qk=[(xqT[:, h, t * P:(t + 1) * P], xkT[:, h, :])], t=t, kn=S, bias=zeros,
                            scale=P ** -0.5, v=[xv[:, b, h * P:(h + 1) * P] for b in range(NT)],
                            acc=(st, "o", t, 0), c0=h * P, width=P, col=24 + h))
            for n, u in enumerate(units):
                u["first"] = n == 0 or not any(m["acc"] == u["acc"] for m in units[:n])
                u["last"] = not any(m["acc"] == u["acc"] for m in units[n + 1:])
                u["blocks"] = [(b * P, min(P, u["kn"] - b * P)) for b in range(len(u["v"]))]
            return units

        @block.tensor
        def _(pe):

            def arrived(key):
                n = chunk_index[key]
                pe.wait_ge(slot_loaded[n % SLOTS].sem, slot_loaded[n % SLOTS].at(key))

            def mm(o, lhsT, rhs, start, stop):
                return nc.tensor.matmul(o, lhsT, rhs, start=start, stop=stop)

            def product(key, pairs, width, rows=P, c0=0, bank=None):
                o = (G.take(pe, key) if bank is None else bank)[0:rows, c0:c0 + width]
                for n, (lhsT, rhs) in enumerate(pairs):
                    ins = mm(o, lhsT, rhs, n == 0, n == len(pairs) - 1)
                ins.then_inc(matmul_done.sem, matmul_done.next(key))

            def to_columns(key, src, nk, nt=NT, waits=()):
                for b in range((nk + 1) // 2):
                    bank = TB.take(pe, (key, b))
                    for kt in range(2 * b, min(2 * b + 2, nk)):
                        for t in range(nt):
                            ins = nc.tensor.transpose(bank[:, (kt % 2) * S + t * P:(kt % 2) * S + (t + 1) * P],
                                                      src(t, kt), ident[:, :])
                    ins.then_inc(transposed.sem, transposed.next((key, b)))

            def norm(n):
                pe.wait_ge(rows_ready.sem, rows_ready.at((n, NT - 1)))
                to_columns(n, lambda t, kt: xn[:, t, kt * P:(kt + 1) * P], KD)
                pe.wait_ge(act_read.sem, act_read.at((n, 2)))
                pe.wait_ge(dve_read.sem, dve_read.at((n, 3)))

            def columns_gemm(ckey, key, n, src, c0=0, k0=0):
                arrived(ckey)
                s = view(ckey)
                for c in range(n):
                    product((key, c), [(s[:, k, c0 + c * P:c0 + (c + 1) * P], src[:, k, :]) for k in range(s.shape[1])], S)
                chunk_end[ckey] = (key, n - 1)

            def rows_gemm(ckey, key, src, c0=0, n=512):
                arrived(ckey)
                s = view(ckey)
                for t in range(NT):
                    product((key, t), [(src[:, k, t * P:(t + 1) * P], s[:, k, c0:c0 + n]) for k in range(s.shape[1])], n)
                chunk_end[ckey] = (key, NT - 1)

            def wide_gemm(st, ckeys, key, src):
                banks = [[G.take(pe, (key, t, h)) for h in range(2)] for t in range(NT)]
                k = 0
                total = sum(view(c).shape[1] for c in ckeys)
                for c in ckeys:
                    arrived(c)
                    s = view(c)
                    for kk in range(s.shape[1]):
                        if kk == 0 and st in ("ff1", "ff2", "ff3"):
                            pe.wait_ge(dve_read.sem, dve_read.at((key[0], "h", k + s.shape[1] - 1)))
                        for t in range(NT):
                            for h in range(2):
                                ins = mm(banks[t][h][:, :], src[:, k, t * P:(t + 1) * P],
                                         s[:, kk, h * 512:(h + 1) * 512], k == 0, k == total - 1)
                        k += 1
                    ins.then_inc(matmul_done.sem, matmul_done.next((key, "chunk", c)))
                    chunk_end[c] = (key, "chunk", c)
                plan.setdefault("wide_end", {})[key] = (key, "chunk", ckeys[-1])

            def ffn(st):
                norm((st, "norm"))
                for j in range(KF // 2):
                    ckey = (st, "in", j)
                    arrived(ckey)
                    s = slot_of(ckey)[:, :].rearrange("p (k u n) -> p k u n", k=KD, u=2)
                    for c in range(2):
                        bank = G.take(pe, (st, "h", 2 * j + c))
                        for u in range(2):
                            for k in range(KD):
                                ins = mm(bank[:, u * S:(u + 1) * S], s[:, k, u, c * P:(c + 1) * P], hT[:, k, :], k == 0, k == KD - 1)
                        ins.then_inc(matmul_done.sem, matmul_done.next((st, "h", 2 * j + c)))
                    chunk_end[ckey] = (st, "h", 2 * j + 1)
                wide_gemm(st[0], [(st, "out", m) for m in range(0, KF, 4)], (st, "y"), hidT)

            def attention(st):
                units = units_of(st)
                banks = {}
                for i in range(len(units) + 2):
                    if i < len(units):
                        u = units[i]
                        bank = SB.take(pe, (st, "s", i))
                        for n, (q, k) in enumerate(u["qk"]):
                            ins = mm(bank[:, 0:u["kn"]], q, k, n == 0, n == len(u["qk"]) - 1)
                        ins.then_inc(scored.sem, scored.next((st, i)))
                    if 1 <= i <= len(units):
                        u = units[i - 1]
                        pe.wait_ge(weighed.sem, weighed.at((st, i - 1)))
                        bank = TB.take(pe, (st, "p", i - 1))
                        for b, (k0, n) in enumerate(u["blocks"]):
                            ins = nc.tensor.transpose(bank[0:n, b * P:(b + 1) * P], pr[:, (i - 1) % 3, k0:k0 + n], ident[:, :])
                        ins.then_inc(transposed.sem, transposed.next((st, "p", i - 1)))
                    if i >= 2:
                        u = units[i - 2]
                        if u["first"]:
                            banks[u["acc"]] = G.take(pe, u["acc"])
                        pe.wait_ge(act_read.sem, act_read.at((st, "p", i - 2)))
                        for b, (k0, n) in enumerate(u["blocks"]):
                            ins = mm(banks[u["acc"]][:, u["c0"]:u["c0"] + u["width"]], prT[0:n, (i - 2) % 2, b * P:(b + 1) * P],
                                     u["v"][b], b == 0, b == len(u["blocks"]) - 1)
                        ins.then_inc(matmul_done.sem, matmul_done.next((st, "pv", i - 2)))

            def output_columns(st, nk):
                pe.wait_ge(rows_ready.sem, rows_ready.at((st, "o", NT - 1)))
                to_columns((st, "oT"), lambda t, kt: o_rows[:, t, kt * P:(kt + 1) * P], nk)
                for b in range((nk + 1) // 2):
                    sig = (act_read, dve_read)[b % 2]
                    pe.wait_ge(sig.sem, sig.at(((st, "oT"), b)))

            def mixer(st):
                i = st[1]
                norm((st, "norm"))
                if i % 3 == 1:
                    for c in range(4):
                        rows_gemm((st, "in", c), (st, "in", c), hT)
                    pe.wait_ge(pool_step.sem, pool_step.at("spatial"))
                    to_columns((st, "ws"), lambda t, kt: ws[:, kt, :], GROUPS_B, nt=1)
                    for b in range(4):
                        sig = (act_read, dve_read)[b % 2]
                        pe.wait_ge(sig.sem, sig.at(((st, "ws"), b)))
                    for t in range(NT):
                        pe.wait_ge(rows_ready.sem, rows_ready.at((st, "v", t)))
                        for h in range(2):
                            bank = G.take(pe, (st, "sv", t, h))
                            for g in range(4):
                                ins = mm(bank[:, g * P:(g + 1) * P], wsT[:, 4 * h + g, :],
                                         g_rows[:, t, (4 * h + g) * P:(4 * h + g + 1) * P], True, True)
                            ins.then_inc(matmul_done.sem, matmul_done.next((st, "sv", t, h)))
                else:
                    for c in range(4):
                        columns_gemm((st, "in", c), (st, "qk", c), 4, hT)
                    for c in range(2):
                        rows_gemm((st, "in", 4 + c), (st, "v", c), hT)
                    pe.wait_ge(act_read.sem, act_read.at(((st, "qk", 3), 2)))
                    pe.wait_ge(dve_read.sem, dve_read.at(((st, "qk", 3), 3)))
                    pe.wait_ge(dve_read.sem, dve_read.at(((st, "v", 1), 1)))
                    pe.wait_ge(act_read.sem, act_read.at(((st, "v", 1), 0)))
                    attention(st)
                output_columns(st, KD)
                for c in range(2):
                    rows_gemm((st, "out", c), (st, "y", c), oT)

            def branches(st):
                l = st[1]
                L = ("l2", l)
                norm((st, "norm"))
                for c in range(2):
                    columns_gemm((*L, "glu", c), (st, "glu", c), 4, hT)
                arrived((*L, "q"))
                s = slot_of((*L, "q"))[:, :].rearrange("p (k n) -> p k n", k=KD)
                for c in range(4):
                    product(((st, "q"), c), [(s[:, k, c * P:(c + 1) * P], hT[:, k, :]) for k in range(KD)], S)
                chunk_end[(*L, "q")] = ((st, "q"), 3)
                columns_gemm((*L, "kv", 0), (st, "kv0"), 3, hT)
                rows_gemm((*L, "kv", 0), (st, "vslc"), hT, 3 * P, P)
                columns_gemm((*L, "kv", 1), (st, "kv1"), 1, hT)
                rows_gemm((*L, "kv", 1), (st, "rest", 0), hT, P, 384)
                rows_gemm((*L, "kv", 2), (st, "rest", 1), hT, 0, N_REST - 384)
                pe.wait_ge(small_loaded.sem, small_loaded.at(st))
                for v in range(2):
                    pe.wait_ge(dve_read.sem, dve_read.at((st, "blk", v)))
                    arrived((*L, "cmp", v))
                    s = view((*L, "cmp", v))
                    for f in range(2):
                        product((st, "hid", v, f), [(s[:, j, f * P:(f + 1) * P], blk[:, v, j, :, :].rearrange("p g c -> p (g c)"))
                                                    for j in range(16)], 30)
                    chunk_end[(*L, "cmp", v)] = (st, "hid", v, 1)
                for c in range(6):
                    rows_gemm((*L, "merge", c), (st, "merge", c), hT)
                    if c == 3:
                        pe.wait_ge(act_read.sem, act_read.at((st, "hid", 1, 1)))
                        product((st, "kc"), [(w2k[:, f, :, :].rearrange("p u d -> p (u d)"), hid_c[:, 0, f, :]) for f in range(2)], 30)
                        for g in range(2):
                            product((st, "vc", g), [(hid_c[:, 1, f, g * N_CMP:(g + 1) * N_CMP], w2v[:, f, :]) for f in range(2)],
                                    DH, rows=N_CMP)
                pe.wait_ge(dve_step.sem, dve_step.at((st, "conv")))
                for t in range(NT):
                    bank = TB.take(pe, (st, "conv_rows", t))
                    for c in range(CT):
                        ins = nc.tensor.transpose(bank[:, c * P:(c + 1) * P], convT[:, c, t * P:(t + 1) * P], ident[:, :])
                    ins.then_inc(transposed.sem, transposed.next((st, "conv_rows", t)))
                pe.wait_ge(rows_ready.sem, rows_ready.at((st, "conv", NT - 1)))
                to_columns((st, "convT"), lambda t, kt: xn[:, t, kt * P:(kt + 1) * P], CT)
                pe.wait_ge(act_read.sem, act_read.at(((st, "convT"), 1)))
                wide_gemm("conv", [(*L, "conv")], (st, "yconv"), oT)
                pe.wait_ge(dve_read.sem, dve_read.at((st, "vc", 1)))
                pe.wait_ge(act_read.sem, act_read.at(((st, "kv1"), 0)))
                attention(st)
                output_columns(st, 4)
                wide_gemm("nsa", [(*L, "nsa")], (st, "ynsa"), oT)
                pe.wait_ge(rows_ready.sem, rows_ready.at((st, "latent")))
                to_columns((st, "latT"), lambda t, kt: xn[:, t, kt * P:(kt + 1) * P], 5)
                for b in range(3):
                    sig = (act_read, dve_read)[b % 2]
                    pe.wait_ge(sig.sem, sig.at(((st, "latT"), b)))
                arrived((*L, "uq"))
                s = view((*L, "uq"))
                for h in range(MLA_HEADS):
                    product((st, "qn", h), [(s[:, k, h * 192:h * 192 + P], hT[:, k, :]) for k in range(3)], S)
                for t in range(NT):
                    product((st, "qp", t), [(hT[:, k, t * P:(t + 1) * P],
                                             s[:, k, :].rearrange("p (h e) -> p h e", h=4)[:, :, P:192]) for k in range(3)], 256)
                chunk_end[(*L, "uq")] = (st, "qp", 1)
                arrived((*L, "ukv"))
                s = view((*L, "ukv"))
                for h in range(MLA_HEADS):
                    product((st, "kn", h), [(s[:, k, h * 256:h * 256 + P], hT[:, 3 + k, :]) for k in range(2)], S)
                for t in range(NT):
                    product((st, "vm", t), [(hT[:, 3 + k, t * P:(t + 1) * P],
                                             s[:, k, :].rearrange("p (h e) -> p h e", h=4)[:, :, P:256]) for k in range(2)], 512)
                chunk_end[(*L, "ukv")] = (st, "vm", 1)
                pe.wait_ge(rows_ready.sem, rows_ready.at((st, "rope")))
                to_columns((st, "peT"), lambda t, kt: xn[:, t, kt * P:(kt + 1) * P], 3)
                for b in range(2):
                    sig = (act_read, dve_read)[b % 2]
                    pe.wait_ge(sig.sem, sig.at(((st, "peT"), b)))
                pe.wait_ge(dve_read.sem, dve_read.at((st, "vm", 1)))
                pe.wait_ge(act_read.sem, act_read.at((st, "kn", 3)))
                attention(("mla", l))
                output_columns(("mla", l), 4)
                wide_gemm("mla", [(*L, "mla")], (st, "ymla"), oT)
                pe.wait_ge(rows_ready.sem, rows_ready.at((st, "merged")))
                to_columns((st, "mT"), lambda t, kt: merged[:, t, kt * P:(kt + 1) * P], KD)
                for b in range(4):
                    sig = (act_read, dve_read)[b % 2]
                    pe.wait_ge(sig.sem, sig.at(((st, "mT"), b)))
                for c in range(2):
                    rows_gemm((*L, "out", c), (st, "y", c), oT)

            def memory(st):
                L = ("l2", st[1])
                norm((st, "norm"))
                columns_gemm((*L, "xq"), (st, "xq"), 4, hT)
                norm((st, "mem"))
                columns_gemm((*L, "xk"), (st, "xk"), 4, memT)
                rows_gemm((*L, "xv"), (st, "xv"), memT)
                pe.wait_ge(act_read.sem, act_read.at(((st, "xk"), 2)))
                pe.wait_ge(dve_read.sem, dve_read.at(((st, "xk"), 3)))
                pe.wait_ge(dve_read.sem, dve_read.at(((st, "xv"), 1)))
                pe.wait_ge(act_read.sem, act_read.at(((st, "xv"), 0)))
                attention(st)
                output_columns(st, 4)
                wide_gemm("xo", [(*L, "xo")], (st, "y"), oT)

            pe.wait_ge(consts_loaded.sem, consts_loaded.at("c"))
            pe.wait_ge(pool_step.sem, pool_step.at("ident"))
            for n, r in enumerate(gain_tiles):
                bank = TB.take(pe, ("gains", n))
                nc.tensor.transpose(bank[:, 0:r], gains[0:r, n, :], ident[0:r, 0:r]) \
                    .then_inc(transposed.sem, transposed.next(("gains", n)))
            bank = TB.take(pe, ("gains", 3))
            for l in range(DEPTH2):
                ins = nc.tensor.transpose(bank[:, l * P:l * P + TAPS * CT], convw[0:TAPS * CT, l, :],
                                          ident[0:TAPS * CT, 0:TAPS * CT])
            ins.then_inc(transposed.sem, transposed.next(("gains", 3)))
            pe.wait_ge(dve_step.sem, dve_step.at("onehot"))
            product("line", [(bias2[:, :], onehot[:, :])], 3 * P, rows=NSA_HEADS)
            for st in stages:
                {"ff1": ffn, "ff2": ffn, "ff3": ffn, "mix": mixer, "l2": branches, "xattn": memory}[st[0]](st)

        @block.scalar
        def _(act):

            def copy(o, i, scale=1.0):
                return nc.scalar.activation(o, i, ACT.Copy, scale=scale)


            def row_gain(n):
                if n >= 2:
                    act.wait_ge(dve_read.sem, dve_read.at(("gain", row_gains[n - 2][0])))
                if n < len(row_gains):
                    key, src = row_gains[n]
                    act.dma_start(gain_row[n % 2][:, :], src.rearrange("(a n) -> a n", a=1).broadcast_to([P, D])) \
                        .then_inc(gain_loaded[n % 2].sem, gain_loaded[n % 2].next(key))

            def squares_free():
                if squared.count:
                    act.wait_ge(squared.sem, squared.count)

            def norm(n, src, ready):
                for t in range(NT):
                    sig, event = ready(t)
                    act.wait_ge(sig.sem, sig.at(event))
                    squares_free()
                    nc.scalar.activation(square[:, :], src[:, t, :], ACT.Square, accum_out=ssum[:, 4 + t:5 + t]) \
                        .then_inc(squared.sem, squared.next((n, t)))

            def columns(n, gain, dst, nk=KD):
                for b in range(0, (nk + 1) // 2, 2):
                    act.wait_ge(transposed.sem, transposed.at((n, b)))
                    bank = TB.of((n, b))
                    for kt in range(2 * b, min(2 * b + 2, nk)):
                        ins = copy(dst(kt), bank[:, (kt % 2) * S:(kt % 2 + 1) * S], gain(kt) if gain else 1.0)
                    ins.then_inc(act_read.sem, act_read.next((n, b)))

            def prev_ready(st, t):
                n = stages.index(st)
                return (x_ready, (stages[n - 1], t)) if n else (consts_loaded, "c")

            def pre(st, key):
                norm((st, "norm"), x, lambda t: prev_ready(st, t))
                n = stages.index(st)
                if n and stages[n - 1] in gain_for:
                    row_gain(gain_n[gain_for[stages[n - 1]]] + 2)
                columns((st, "norm"), lambda k: gcol(key, k), lambda k: hT[:, k, :])

            def post(st, banks):
                for t in range(NT):
                    for h in range(2):
                        bank, done = banks(t, h)
                        act.wait_ge(matmul_done.sem, matmul_done.at(done))
                        squares_free()
                        nc.scalar.activation(square[:, 0:512], bank[:, :], ACT.Square, accum_out=ssum[:, 2 * t + h:2 * t + h + 1]) \
                            .then_inc(squared.sem, squared.next((st, t, h)))

            def ffn(st, key):
                pre(st, key)
                for i in range(KF):
                    act.wait_ge(matmul_done.sem, matmul_done.at((st, "h", i)))
                    if i >= 2:
                        act.wait_ge(dve_read.sem, dve_read.at((st, "h", i - 2)))
                    nc.scalar.activation(silu[:, i % 2, :], G.of((st, "h", i))[:, 0:S], ACT.Silu) \
                        .then_inc(act_step.sem, act_step.next((st, "h", i)))
                if st[0] != "ff3":
                    post(st, lambda t, h: (G.of(((st, "y"), t, h)), ((st, "y"), "chunk", (st, "out", 20))))

            def attention(st):
                units = units_of(st)
                for i in range(len(units) + 1):
                    if i < len(units):
                        u = units[i]
                        act.wait_ge(maxed.sem, maxed.at((st, i)))
                        if i >= 3:
                            act.wait_ge(transposed.sem, transposed.at((st, "p", i - 3)))
                        nc.scalar.activation(pr[:, i % 3, 0:u["kn"]], sc[:, i % 3, 0:u["kn"]], ACT.Exp, bias=nmax[:, i % 3:i % 3 + 1],
                                             accum_out=sums[:, u["t"], u["col"]:u["col"] + 1]) \
                            .then_inc(weighed.sem, weighed.next((st, i)))
                    if i >= 1:
                        u = units[i - 1]
                        act.wait_ge(transposed.sem, transposed.at((st, "p", i - 1)))
                        if i >= 3:
                            act.wait_ge(matmul_done.sem, matmul_done.at((st, "pv", i - 3)))
                        n, width = u["blocks"][0][1], P * len(u["blocks"])
                        copy(prT[0:n, (i - 1) % 2, 0:width], TB.of((st, "p", i - 1))[0:n, 0:width]) \
                            .then_inc(act_read.sem, act_read.next((st, "p", i - 1)))

            def mixer(st):
                i = st[1]
                pre(st, ("g", i, 2))
                if i % 3 == 1:
                    for c in range(4):
                        for t in range(NT):
                            act.wait_ge(matmul_done.sem, matmul_done.at(((st, "in", c), t)))
                            dst = (u_rows if c < 2 else g_rows)[:, t, (c % 2) * 512:(c % 2) * 512 + 512]
                            nc.scalar.activation(dst, G.of(((st, "in", c), t))[:, :], ACT.Gelu) \
                                .then_inc(act_read.sem, act_read.next(((st, "in", c), t)))
                    columns((st, "ws"), None, lambda k: wsT[:, k, :], GROUPS_B) if False else None
                    for b in (0, 2):
                        act.wait_ge(transposed.sem, transposed.at(((st, "ws"), b)))
                        for kt in (2 * b, 2 * b + 1):
                            ins = copy(wsT[:, kt, :], TB.of(((st, "ws"), b))[:, (kt % 2) * S:(kt % 2) * S + P])
                        ins.then_inc(act_read.sem, act_read.next(((st, "ws"), b)))
                    row_gain(gain_n["ln_g"] + 2)
                    row_gain(gain_n["ln_b"] + 2)
                else:
                    for c in range(4):
                        for j in (0, 2):
                            act.wait_ge(matmul_done.sem, matmul_done.at(((st, "qk", c), j)))
                            copy(qkT[:, 4 * c + j, :], G.of(((st, "qk", c), j))[:, 0:S]).then_inc(act_read.sem, act_read.next(((st, "qk", c), j)))
                    for c in range(2):
                        act.wait_ge(matmul_done.sem, matmul_done.at(((st, "v", c), 0)))
                        copy(v_rows[:, 0, c * 512:(c + 1) * 512], G.of(((st, "v", c), 0))[:, :]) \
                            .then_inc(act_read.sem, act_read.next(((st, "v", c), 0)))
                    attention(st)
                columns((st, "oT"), None, lambda k: oT[:, k, :])
                post(st, lambda t, h: (G.of(((st, "y", h), t)), ((st, "y", h), t)))

            def branches(st):
                l = st[1]
                pre(st, ("norm_mix_2", l))
                for j in (0, 2):
                    act.wait_ge(matmul_done.sem, matmul_done.at(((st, "glu", 0), j)))
                    copy(aT[:, j, :], G.of(((st, "glu", 0), j))[:, 0:S]).then_inc(act_read.sem, act_read.next(((st, "glu", 0), j)))
                for j in range(4):
                    act.wait_ge(matmul_done.sem, matmul_done.at(((st, "glu", 1), j)))
                    nc.scalar.activation(bT[:, j, :], G.of(((st, "glu", 1), j))[:, 0:S], ACT.Sigmoid) \
                        .then_inc(act_read.sem, act_read.next(((st, "glu", 1), j)))
                for j in (0, 2):
                    act.wait_ge(matmul_done.sem, matmul_done.at(((st, "q"), j)))
                    copy(qsT[:, j, :], G.of(((st, "q"), j))[:, 0:S]).then_inc(act_read.sem, act_read.next(((st, "q"), j)))
                for j, dst in ((0, tokT[:, 0, :]), (2, kslcT)):
                    act.wait_ge(matmul_done.sem, matmul_done.at(((st, "kv0"), j)))
                    copy(dst, G.of(((st, "kv0"), j))[:, 0:S]).then_inc(act_read.sem, act_read.next(((st, "kv0"), j)))
                act.wait_ge(matmul_done.sem, matmul_done.at(((st, "kv1"), 0)))
                copy(kwinT, G.of(((st, "kv1"), 0))[:, 0:S]).then_inc(act_read.sem, act_read.next(((st, "kv1"), 0)))
                for v in range(2):
                    sig = (act_read, dve_read)[v]
                    act.wait_ge(sig.sem, sig.at(((st, "kv0"), v)))
                    for g in range(2):
                        for nxt in range(2):
                            act.dma_start(tok2[nxt * DH:(nxt + 1) * DH, v, g, 0:S - nxt], tokT[g * DH:(g + 1) * DH, v, nxt:S]) \
                                .then_inc(tok_loaded.sem, tok_loaded.next(st))
                for t in range(NT):
                    act.wait_ge(dve_read.sem, dve_read.at(((st, "rest", 0), t)))
                gates = rest[:, :, R_GATE:R_GATE + 24]
                nc.scalar.activation(gates, gates, ACT.Sigmoid).then_inc(act_step.sem, act_step.next((st, "gates")))
                for v in range(2):
                    for f in range(2):
                        act.wait_ge(matmul_done.sem, matmul_done.at((st, "hid", v, f)))
                        nc.scalar.activation(hid_c[:, v, f, :], G.of((st, "hid", v, f))[:, 0:30], ACT.Gelu_apprx_tanh,
                                                  bias=gcol((("cmp_b1_k_2", "cmp_b1_v_2")[v], l), f)) \
                            .then_inc(act_read.sem, act_read.next((st, "hid", v, f)))
                for c in range(6):
                    for t in range(NT):
                        act.wait_ge(matmul_done.sem, matmul_done.at(((st, "merge", c), t)))
                        nc.scalar.activation(merge_gate[:, t, c * 512:(c + 1) * 512], G.of(((st, "merge", c), t))[:, :],
                                                  ACT.Sigmoid) \
                            .then_inc(act_read.sem, act_read.next(((st, "merge", c), t)))
                for b in range(2):
                    act.wait_ge(transposed.sem, transposed.at(((st, "convT"), b)))
                    bank = TB.of(((st, "convT"), b))
                    for kt in (2 * b, 2 * b + 1):
                        ins = nc.scalar.activation(oT[:, kt, :], bank[:, (kt % 2) * S:(kt % 2 + 1) * S], ACT.Silu,
                                                   scale=gcol(("conv_ln_g_2", l), kt), bias=gcol(("conv_ln_b_2", l), kt))
                    ins.then_inc(act_read.sem, act_read.next(((st, "convT"), b)))
                attention(st)
                columns((st, "oT"), None, lambda k: oT[:, k, :], 4)
                for t in range(NT):
                    act.wait_ge(dve_read.sem, dve_read.at(((st, "rest", 1), t)))
                    for n, (c0, c1) in enumerate(((R_CQ, R_CKV), (R_CKV, R_KPE))):
                        squares_free()
                        nc.scalar.activation(square[:, 0:c1 - c0], rest[:, t, c0:c1], ACT.Square,
                                             accum_out=ssum[:, 2 * n + t:2 * n + t + 1]) \
                            .then_inc(squared.sem, squared.next((st, "latent", n, t)))
                columns((st, "latT"), lambda k: gcol(("mla_norm_q_2", l), k) if k < 3 else gcol(("mla_norm_kv_2", l), k - 3),
                        lambda k: hT[:, k, :], 5)
                for h in range(MLA_HEADS):
                    act.wait_ge(matmul_done.sem, matmul_done.at((st, "qn", h)))
                    copy(qnT[:, h, :], G.of((st, "qn", h))[:, 0:S]).then_inc(act_read.sem, act_read.next((st, "qn", h)))
                for h in range(MLA_HEADS):
                    act.wait_ge(matmul_done.sem, matmul_done.at((st, "kn", h)))
                    copy(knT[:, h, :], G.of((st, "kn", h))[:, 0:S]).then_inc(act_read.sem, act_read.next((st, "kn", h)))
                columns((st, "peT"), None, lambda k: qpT[:, k, :], 2)
                attention(("mla", l))
                columns((("mla", l), "oT"), None, lambda k: oT[:, k, :], 4)
                columns((st, "mT"), None, lambda k: oT[:, k, :])

            def memory(st):
                l = st[1]
                sig, event = prev_ready(st, NT - 1)
                act.wait_ge(sig.sem, sig.at(event))
                act.dma_start(merged[:, :, :], w["mem_2"][0].rearrange("(t p) d -> p t d", p=P)) \
                    .then_inc(mem_loaded.sem, mem_loaded.next(st))
                pre(st, ("norm_xattn_2", l))
                norm((st, "mem"), merged, lambda t: (mem_loaded, st))
                for j in (0, 2):
                    act.wait_ge(matmul_done.sem, matmul_done.at(((st, "xq"), j)))
                    copy(xqT[:, j, :], G.of(((st, "xq"), j))[:, 0:S]).then_inc(act_read.sem, act_read.next(((st, "xq"), j)))
                columns((st, "mem"), lambda k: gcol(("norm_mem_2", l), k), lambda k: memT[:, k, :])
                for j in (0, 2):
                    act.wait_ge(matmul_done.sem, matmul_done.at(((st, "xk"), j)))
                    copy(xkT[:, j, :], G.of(((st, "xk"), j))[:, 0:S]).then_inc(act_read.sem, act_read.next(((st, "xk"), j)))
                act.wait_ge(matmul_done.sem, matmul_done.at(((st, "xv"), 0)))
                copy(xv[:, 0, :], G.of(((st, "xv"), 0))[:, :]).then_inc(act_read.sem, act_read.next(((st, "xv"), 0)))
                attention(st)
                columns((st, "oT"), None, lambda k: oT[:, k, :], 4)

            row_gain(0)
            row_gain(1)
            for n in (0, 2):
                r = gain_tiles[n]
                act.wait_ge(transposed.sem, transposed.at(("gains", n)))
                copy(gT[:, n, 0:r], TB.of(("gains", n))[:, 0:r]).then_inc(act_read.sem, act_read.next(("gains", n)))
            act.wait_ge(dve_step.sem, dve_step.at("lambda"))
            nc.scalar.activation(lam[:, 2:4], lam[:, 0:2], ACT.Exp).then_inc(act_step.sem, act_step.next("lambda"))
            act.wait_ge(dve_step.sem, dve_step.at("angles"))
            nc.scalar.activation(sinb[:, :, :], sinb[:, :, :], ACT.Sin).then_inc(act_step.sem, act_step.next("sin"))
            nc.scalar.activation(cosb[:, :, :], cosb[:, :, :], ACT.Sin).then_inc(act_step.sem, act_step.next("cos"))
            for st in stages:
                i = st[1]
                if st[0] == "ff1":
                    ffn(st, ("g", i, 0))
                elif st[0] == "ff2":
                    ffn(st, ("g", i, 4))
                elif st[0] == "ff3":
                    ffn(st, ("norm_ffn_2", i))
                else:
                    {"mix": mixer, "l2": branches, "xattn": memory}[st[0]](st)
            if last == ("ff3", DEPTH2 - 1):
                norm("final", x, lambda t: (x_ready, (last, t)))

        @block.gpsimd
        def _(pool):

            def step(ins, key=None):
                settle(pool, ins, pool_step, key)

            def power(key, c0, n):
                pool.wait_ge(mean_ready.sem, mean_ready.at(key))
                pool.tensor_tensor(rstd[:, c0:c0 + n], mean_sq[:, c0:c0 + n], minus_half[:, 0:n], ALU.pow) \
                    .then_inc(rstd_ready.sem, rstd_ready.next(key))

            step(pool.memset(ident[:, :], 0.0))
            step(pool.affine_select(out=ident[:, :], in_=ident[:, :], compare_op=ALU.not_equal, fill=1.0, base=0,
                                    pattern=[[-1, P]], channel_multiplier=1), "ident")
            step(pool.memset(minus_half[:, :], -0.5))
            for h in range(HEADS_C):
                ins = pool.iota(relC[:, h, :], pattern=[[1, TW]], base=-P, channel_multiplier=1,
                                allow_small_or_imprecise_dtypes=True)
            step(ins, "distances")
            step(pool.iota(tmp2[0:BUCKETS, 0:16], pattern=[[1, 16]], base=0, channel_multiplier=0,
                           allow_small_or_imprecise_dtypes=True), "exact")
            step(pool.iota(tmp2[0:BUCKETS, 16:17], pattern=[[0, 1]], base=0, channel_multiplier=1,
                           allow_small_or_imprecise_dtypes=True), "bucket")
            for i in range(ROPE // 2):
                ins = pool.memset(freq[:, i:i + 1], ROPE_THETA ** (-i / (ROPE // 2)))
            step(ins, "freq")
            step(pool.memset(valid[:, :], 1.0))
            step(pool.affine_select(out=valid[:, 0:1], in_=valid[:, 0:1], compare_op=ALU.is_ge, fill=0.0,
                                    base=-(CMP_BLOCK - 1), pattern=[[0, 1]], channel_multiplier=1), "valid")
            for st in stages:
                kind, i = st
                power((st, "norm"), 2, 2)
                if kind == "mix" and i % 3 == 1:
                    power((st, "ln"), 4, 2)
                if kind == "mix" and i % 3 == 2:
                    power((st, "subln"), 0, 16)
                if kind == "l2":
                    if i == 0:
                        step(pool.memset(causal, 0.0))
                        step(pool.affine_select(out=causal, in_=causal, compare_op=ALU.is_ge, fill=NEG, base=-P,
                                                pattern=[[1, TW]], channel_multiplier=1))
                        step(pool.memset(zeros, 0.0))
                        pool.wait_ge(table_loaded.sem, table_loaded.at(st))
                        step(pool.affine_select(out=relN, in_=relN, compare_op=ALU.is_ge, fill=NEG, base=-P,
                                                pattern=[[0, NSA_HEADS], [1, TW]], channel_multiplier=1), "relN")
                    power((st, "conv"), 4, 2)
                    power((st, "latent"), 4, 4)
                if kind == "xattn":
                    power((st, "mem"), 2, 2)
                if kind == "mix" and i % 3 == 0:
                    pass
                if st in gain_for:
                    power((st, "post"), 0, 2)
                if st == ("ff1", 1):
                    pool.wait_ge(x_ready.sem, x_ready.at((("ff1", 1), 1)))
                    pool.dma_start(ws, w["b_w_s"][0].rearrange("g t s -> t g s")).then_inc(spatial_loaded.sem, spatial_loaded.next("ws"))
                    pool.wait_ge(spatial_loaded.sem, spatial_loaded.at("ws"))
                    step(pool.affine_select(out=ws, in_=ws, compare_op=ALU.is_ge, fill=0.0, base=0,
                                            pattern=[[0, GROUPS_B], [-1, P]], channel_multiplier=1), "spatial")
            if last == ("ff3", DEPTH2 - 1):
                power("final", 2, 2)

        @block.vector
        def _(dve):
            V = nc.vector


            def step(ins, key=None):
                settle(dve, ins, dve_step, key)


            def tick(sig, key):
                dve.sem_inc(sig.sem, sig.next(key))

            def mean(key, c0, n, src, count):
                V.tensor_scalar(mean_sq[:, c0:c0 + n], src, 1.0 / count, EPS, ALU.mult, ALU.add) \
                    .then_inc(mean_ready.sem, mean_ready.next(key))

            def norm(n, src):
                dve.wait_ge(squared.sem, squared.at((n, 1)))
                mean(n, 2, 2, ssum[:, 4:6], D)
                dve.wait_ge(rstd_ready.sem, rstd_ready.at(n))
                for t in range(NT):
                    V.tensor_scalar(xn[:, t, :], src[:, t, :], rstd[:, 2 + t:3 + t], None, ALU.mult) \
                        .then_inc(rows_ready.sem, rows_ready.next((n, t)))

            def columns(n, gain, dst, nk=KD):
                for b in range(1, (nk + 1) // 2, 2):
                    dve.wait_ge(transposed.sem, transposed.at((n, b)))
                    bank = TB.of((n, b))
                    for kt in range(2 * b, min(2 * b + 2, nk)):
                        src = bank[:, (kt % 2) * S:(kt % 2 + 1) * S]
                        ins = V.tensor_scalar(dst(kt), src, gain(kt), None, ALU.mult) if gain else V.tensor_copy(dst(kt), src)
                    ins.then_inc(dve_read.sem, dve_read.next((n, b)))

            def pre(st, key):
                norm((st, "norm"), x)
                columns((st, "norm"), lambda k: gcol(key, k), lambda k: hT[:, k, :])

            def post(st, banks, factor):
                dve.wait_ge(squared.sem, squared.at((st, 1, 1)))
                step(V.tensor_tensor(mean_sq[:, 0:2], ssum[:, 0:4:2], ssum[:, 1:4:2], ALU.add))
                mean((st, "post"), 0, 2, mean_sq[:, 0:2], D)
                dve.wait_ge(rstd_ready.sem, rstd_ready.at((st, "post")))
                if factor != 1.0:
                    step(V.tensor_scalar(rstd[:, 0:2], rstd[:, 0:2], factor, None, ALU.mult))
                gkey = gain_for[st]
                n = gain_n[gkey]
                dve.wait_ge(gain_loaded[n % 2].sem, gain_loaded[n % 2].at(gkey))
                for t in range(NT):
                    for h in range(2):
                        bank, key = banks(t, h)
                        ins = V.scalar_tensor_tensor(tmp[:, :], bank[:, :], rstd[:, t:t + 1],
                                                     gain_row[n % 2][:, h * 512:(h + 1) * 512], ALU.mult, ALU.mult)
                        ins.then_inc(dve_read.sem, dve_read.next(key))
                        dve.wait_ge(dve_read.sem, dve_read.at(key))
                        xs = x[:, t, h * 512:(h + 1) * 512]
                        ins = V.tensor_tensor(xs, xs, tmp[:, :], ALU.add)
                        if h == 0:
                            step(ins)
                        else:
                            settle(dve, ins, x_ready, (st, t))
                tick(dve_read, ("gain", gkey))

            def add_to_x(st, banks):
                for t in range(NT):
                    for h in range(2):
                        bank, key, done = banks(t, h)
                        dve.wait_ge(matmul_done.sem, matmul_done.at(done))
                        xs = x[:, t, h * 512:(h + 1) * 512]
                        settle(dve, V.tensor_tensor(xs, xs, bank[:, :], ALU.add), dve_read, key)
                    tick(x_ready, (st, t))

            def ffn(st, key):
                pre(st, key)
                for i in range(KF):
                    dve.wait_ge(act_step.sem, act_step.at((st, "h", i)))
                    V.tensor_tensor(hidT[:, i, :], silu[:, i % 2, :], G.of((st, "h", i))[:, S:2 * S], ALU.mult) \
                        .then_inc(dve_read.sem, dve_read.next((st, "h", i)))
                k = (st, "y")
                if st[0] == "ff3":
                    add_to_x(st, lambda t, h: (G.of((k, t, h)), (k, t, h), (k, "chunk", (st, "out", 20))))
                else:
                    post(st, lambda t, h: (G.of((k, t, h)), (k, t, h)), 0.5)

            def attention(st, evacuate):
                units = units_of(st)
                for i in range(len(units) + 3):
                    if i < len(units):
                        u = units[i]
                        kn = u["kn"]
                        dve.wait_ge(scored.sem, scored.at((st, i)))
                        if i >= 3:
                            dve.wait_ge(weighed.sem, weighed.at((st, i - 3)))
                        settle(dve, V.scalar_tensor_tensor(sc[:, i % 3, 0:kn], SB.of((st, "s", i))[:, 0:kn], u["scale"], u["bias"],
                                                           ALU.mult, ALU.add), dve_read, (st, "s", i))
                        V.tensor_reduce(nmax[:, i % 3:i % 3 + 1], sc[:, i % 3, 0:kn], AX.X, ALU.max, negate=True) \
                            .then_inc(maxed.sem, maxed.next((st, i)))
                    if i >= 3 and units[i - 3]["last"]:
                        u = units[i - 3]
                        dve.wait_ge(matmul_done.sem, matmul_done.at((st, "pv", i - 3)))
                        evacuate(u["acc"], G.of(u["acc"]))

            def heads(bank, n):
                return bank[:, :].rearrange("p (h d) -> p h d", h=n)

            def spread(a, width):
                return a.unsqueeze(2).broadcast_to([a.shape[0], a.shape[1], width])

            def even(st, n, c0):
                def f(acc, bank):
                    _, _, t, b = acc
                    cols = slice(c0 + b * n, c0 + (b + 1) * n)
                    step(V.reciprocal(inv[:, t, cols], sums[:, t, cols]))
                    o = o_rows[:, t, b * 512:(b + 1) * 512].rearrange("p (h d) -> p h d", h=n)
                    settle(dve, V.tensor_tensor(o, heads(bank, n), spread(inv[:, t, cols], 512 // n), ALU.mult), dve_read, acc)
                    if b == (1 if st[0] == "mix" else 0):
                        tick(rows_ready, (st, "o", t))
                return f

            def differential(st):
                def f(acc, bank):
                    _, _, t, b = acc
                    cols = inv[:, t, 4 * b:4 * b + 4]
                    step(V.reciprocal(cols, sums[:, t, 4 * b:4 * b + 4]))
                    step(V.tensor_scalar(cols[:, 1:4:2], cols[:, 1:4:2], lam[:, 6:7], None, ALU.mult))
                    both = bank[:, :].rearrange("p (h m d) -> p h m d", h=2, m=2)
                    o = o_rows[:, t, b * 256:(b + 1) * 256].rearrange("p (h d) -> p h d", h=2)
                    t0 = tmp[:, 0:256].rearrange("p (h d) -> p h d", h=2)
                    t1 = tmp2[:, 0:256].rearrange("p (h d) -> p h d", h=2)
                    step(V.tensor_tensor(t0, both[:, :, 0, :], spread(cols[:, 0:4:2], P), ALU.mult))
                    settle(dve, V.tensor_tensor(t1, both[:, :, 1, :], spread(cols[:, 1:4:2], P), ALU.mult), dve_read, acc)
                    step(V.tensor_tensor(o, t0, t1, ALU.add))
                return f

            def sparse(st):
                def f(acc, bank):
                    _, _, t, br = acc
                    cols = inv[:, t, 8 * br:8 * br + 8]
                    step(V.reciprocal(cols, sums[:, t, 8 * br:8 * br + 8]))
                    if t == 0 and br == 0:
                        step(V.tensor_scalar(cols, cols, valid[:, 0:1], None, ALU.mult))
                    if br == 0:
                        dve.wait_ge(act_step.sem, act_step.at((st, "gates")))
                    step(V.tensor_tensor(cols, cols, rest[:, t, R_GATE + br:R_GATE + 24:3], ALU.mult))
                    o = o_rows[:, t, 0:512]
                    oh = o.rearrange("p (h d) -> p h d", h=8)
                    th = tmp[:, :].rearrange("p (h d) -> p h d", h=8)
                    settle(dve, V.tensor_tensor(oh if br == 0 else th, heads(bank, 8), spread(cols, DH), ALU.mult), dve_read, acc)
                    if br:
                        ins = V.tensor_tensor(o, o, tmp[:, :], ALU.add)
                        if br == 2:
                            settle(dve, ins, rows_ready, (st, "o", t))
                        else:
                            step(ins)
                return f

            def mixer(st):
                i = st[1]
                pre(st, ("g", i, 2))
                if i % 3 == 1:
                    for b in (1, 3):
                        dve.wait_ge(transposed.sem, transposed.at(((st, "ws"), b)))
                        for kt in (2 * b, 2 * b + 1):
                            ins = V.tensor_copy(wsT[:, kt, :], TB.of(((st, "ws"), b))[:, (kt % 2) * S:(kt % 2) * S + P])
                        ins.then_inc(dve_read.sem, dve_read.next(((st, "ws"), b)))
                    for t in range(NT):
                        dve.wait_ge(act_read.sem, act_read.at(((st, "in", 3), 1)))
                        for h in range(2):
                            step(V.bn_stats(stats[:, h, :], g_rows[:, t, h * 512:(h + 1) * 512]))
                        step(V.bn_aggr(moments[:, t, :], stats[:, :, :]))
                    mean((st, "ln"), 4, 2, moments[:, :, 1], 1.0)
                    dve.wait_ge(rstd_ready.sem, rstd_ready.at((st, "ln")))
                    for key in ("ln_g", "ln_b"):
                        dve.wait_ge(gain_loaded[gain_n[key] % 2].sem, gain_loaded[gain_n[key] % 2].at(key))
                    for t in range(NT):
                        g = g_rows[:, t, :]
                        step(V.tensor_scalar(g, g, moments[:, t, 0:1], rstd[:, 4 + t:5 + t], ALU.subtract, ALU.mult))
                        ins = V.tensor_tensor(g, g, gain_row[gain_n["ln_g"] % 2][:, :], ALU.mult)
                        settle(dve, ins, dve_read, ("gain", "ln_g") if t == 1 else ("ln", t))
                        ins = V.tensor_tensor(g, g, gain_row[gain_n["ln_b"] % 2][:, :], ALU.add)
                        settle(dve, ins, rows_ready, (st, "v", t))
                    tick(dve_read, ("gain", "ln_b"))
                    for t in range(NT):
                        for h in range(2):
                            dve.wait_ge(matmul_done.sem, matmul_done.at((st, "sv", t, h)))
                            bank = G.of((st, "sv", t, h))
                            for g in range(4):
                                c = slice((4 * h + g) * P, (4 * h + g + 1) * P)
                                ins = V.scalar_tensor_tensor(o_rows[:, t, c], bank[:, g * P:(g + 1) * P], gcol("b_b_s", 4 * h + g),
                                                             u_rows[:, t, c], ALU.add, ALU.mult)
                            settle(dve, ins, dve_read, (st, "sv", t, h))
                        tick(rows_ready, (st, "o", t))
                else:
                    for c in range(4):
                        for j in (1, 3):
                            dve.wait_ge(matmul_done.sem, matmul_done.at(((st, "qk", c), j)))
                            V.tensor_copy(qkT[:, 4 * c + j, :], G.of(((st, "qk", c), j))[:, 0:S]) \
                                .then_inc(dve_read.sem, dve_read.next(((st, "qk", c), j)))
                    for c in range(2):
                        dve.wait_ge(matmul_done.sem, matmul_done.at(((st, "v", c), 1)))
                        V.tensor_copy(v_rows[:, 1, c * 512:(c + 1) * 512], G.of(((st, "v", c), 1))[:, :]) \
                            .then_inc(dve_read.sem, dve_read.next(((st, "v", c), 1)))
                    if i % 3 == 0:
                        dve.wait_ge(table_loaded.sem, table_loaded.at(st))
                        step(V.memset(relA[0:CHUNK, :, 1:CHUNK + 1], NEG))
                    attention(st, even(st, 8, 0) if i % 3 == 0 else differential(st))
                    if i % 3 == 2:
                        o4 = o_rows[:, :, :].rearrange("p t (h d) -> p t h d", h=HEADS_C)
                        x4 = xn[:, :, :].rearrange("p t (h d) -> p t h d", h=HEADS_C)
                        for t in range(NT):
                            step(V.tensor_tensor(xn[:, t, :], o_rows[:, t, :], o_rows[:, t, :], ALU.mult))
                            step(V.tensor_reduce(mean_sq[:, 8 * t:8 * t + 8], x4[:, t, :, :], AX.X, ALU.add))
                        mean((st, "subln"), 0, 16, mean_sq[:, 0:16], P)
                        dve.wait_ge(rstd_ready.sem, rstd_ready.at((st, "subln")))
                        lambda_init = 0.8 - 0.6 * math.exp(-0.3 * i)
                        step(V.tensor_scalar(rstd[:, 0:16], rstd[:, 0:16], 1.0 - lambda_init, None, ALU.mult))
                        for t in range(NT):
                            step(V.tensor_tensor(o4[:, t, :, :], o4[:, t, :, :], spread(rstd[:, 8 * t:8 * t + 8], P), ALU.mult))
                            ins = V.tensor_tensor(o4[:, t, :, :], o4[:, t, :, :],
                                                  subln[:, :].unsqueeze(1).broadcast_to([P, HEADS_C, P]), ALU.mult)
                            ins.then_inc(rows_ready.sem, rows_ready.next((st, "o", t)))
                columns((st, "oT"), None, lambda k: oT[:, k, :])
                post(st, lambda t, h: (G.of(((st, "y", h), t)), ((st, "y", h), t)), 1.0)

            def merge(st, name, n):
                k = (st, name)
                for t in range(NT):
                    for h in range(2):
                        dve.wait_ge(matmul_done.sem, matmul_done.at((k, "chunk", ("l2", st[1], name[1:]))))
                        bank = G.of((k, t, h))
                        gate = merge_gate[:, t, n * D + h * 512:n * D + (h + 1) * 512]
                        m = merged[:, t, h * 512:(h + 1) * 512]
                        ins = V.tensor_tensor(m if n == 0 else tmp[:, :], bank[:, :], gate, ALU.mult)
                        settle(dve, ins, dve_read, (k, t, h))
                        if n:
                            ins = V.tensor_tensor(m, m, tmp[:, :], ALU.add)
                            if n == 2 and t == 1 and h == 1:
                                settle(dve, ins, rows_ready, (st, "merged"))
                            else:
                                step(ins)

            def branches(st):
                l = st[1]
                pre(st, ("norm_mix_2", l))
                for j in (1, 3):
                    dve.wait_ge(matmul_done.sem, matmul_done.at(((st, "glu", 0), j)))
                    V.tensor_copy(aT[:, j, :], G.of(((st, "glu", 0), j))[:, 0:S]) \
                        .then_inc(dve_read.sem, dve_read.next(((st, "glu", 0), j)))
                for j in (1, 3):
                    dve.wait_ge(matmul_done.sem, matmul_done.at(((st, "q"), j)))
                    V.tensor_copy(qsT[:, j, :], G.of(((st, "q"), j))[:, 0:S]).then_inc(dve_read.sem, dve_read.next(((st, "q"), j)))
                dve.wait_ge(matmul_done.sem, matmul_done.at(((st, "kv0"), 1)))
                V.tensor_copy(tokT[:, 1, :], G.of(((st, "kv0"), 1))[:, 0:S]).then_inc(dve_read.sem, dve_read.next(((st, "kv0"), 1)))
                for t in range(NT):
                    dve.wait_ge(matmul_done.sem, matmul_done.at(((st, "vslc"), t)))
                    V.tensor_copy(vslc[:, t, :], G.of(((st, "vslc"), t))[:, 0:P]) \
                        .then_inc(dve_read.sem, dve_read.next(((st, "vslc"), t)))
                for n, (c0, c1) in enumerate(((0, 384), (384, N_REST))):
                    for t in range(NT):
                        dve.wait_ge(matmul_done.sem, matmul_done.at(((st, "rest", n), t)))
                        V.tensor_copy(rest[:, t, c0:c1], G.of(((st, "rest", n), t))[:, 0:c1 - c0]) \
                            .then_inc(dve_read.sem, dve_read.next(((st, "rest", n), t)))
                dve.wait_ge(tok_loaded.sem, tok_loaded.at(st))
                for v in range(2):
                    for g in range(2):
                        for half in range(2):
                            src = tok2[:, v, g, half * CMP_STRIDE:half * CMP_STRIDE + N_CMP * CMP_STRIDE] \
                                .rearrange("p (c r) -> p r c", r=CMP_STRIDE)[:, 0:CMP_STRIDE:2, :]
                            t_, r = col[(("cmp_pos_k_2", "cmp_pos_v_2")[v], l)]
                            pos = gT[:, t_, r + 8 * half:r + 8 * half + 8].unsqueeze(2).broadcast_to([P, 8, N_CMP])
                            ins = V.tensor_tensor(blk[:, v, 8 * half:8 * half + 8, g, :], src, pos, ALU.add)
                    ins.then_inc(dve_read.sem, dve_read.next((st, "blk", v)))
                step(V.memset(glu[:, :, 0:TAPS - 1], 0.0))
                dve.wait_ge(act_read.sem, act_read.at(((st, "glu", 1), 3)))
                dve.wait_ge(dve_read.sem, dve_read.at(((st, "glu", 0), 3)))
                step(V.tensor_tensor(glu[:, :, TAPS - 1:TAPS - 1 + S], aT, bT, ALU.mult))
                for tap in range(TAPS):
                    for c in range(CT):
                        if tap:
                            dve.wait_ge(dve_step.sem, dve_step.count - CT + 1)
                        wt = convwT[:, l, tap * CT + c:tap * CT + c + 1]
                        src = glu[:, c, tap:tap + S]
                        if tap == 0:
                            ins = V.tensor_scalar(convT[:, c, :], src, wt, gcol(("conv_b_2", l), c), ALU.mult, ALU.add)
                        else:
                            ins = V.scalar_tensor_tensor(convT[:, c, :], src, wt, convT[:, c, :], ALU.mult, ALU.add)
                        ins.then_inc(dve_step.sem, dve_step.next((st, "conv")))
                dve.wait_ge(matmul_done.sem, matmul_done.at((st, "kc")))
                V.tensor_copy(kcT[:, 0:30], G.of((st, "kc"))[:, 0:30]).then_inc(dve_read.sem, dve_read.next((st, "kc")))
                for g in range(2):
                    dve.wait_ge(matmul_done.sem, matmul_done.at((st, "vc", g)))
                    V.tensor_copy(vc[0:N_CMP, g, :], G.of((st, "vc", g))[0:N_CMP, 0:DH]) \
                        .then_inc(dve_read.sem, dve_read.next((st, "vc", g)))
                for t in range(NT):
                    dve.wait_ge(transposed.sem, transposed.at((st, "conv_rows", t)))
                    step(V.bn_stats(stats[:, 0, :], TB.of((st, "conv_rows", t))[:, :]))
                    step(V.bn_aggr(moments[:, t, :], stats[:, 0, :]))
                mean((st, "conv"), 4, 2, moments[:, :, 1], 1.0)
                dve.wait_ge(rstd_ready.sem, rstd_ready.at((st, "conv")))
                for t in range(NT):
                    ins = V.tensor_scalar(xn[:, t, 0:CONV_CH], TB.of((st, "conv_rows", t))[:, :], moments[:, t, 0:1],
                                          rstd[:, 4 + t:5 + t], ALU.subtract, ALU.mult)
                    settle(dve, ins, dve_read, (st, "conv_rows", t))
                    tick(rows_ready, (st, "conv", t))
                merge(st, "yconv", 0)
                dve.wait_ge(pool_step.sem, pool_step.at("relN"))
                attention(st, sparse(st))
                columns((st, "oT"), None, lambda k: oT[:, k, :], 4)
                merge(st, "ynsa", 1)
                for n, (c0, c1) in enumerate(((R_CQ, R_CKV), (R_CKV, R_KPE))):
                    dve.wait_ge(squared.sem, squared.at((st, "latent", 1, 1)))
                    ins = V.tensor_scalar(mean_sq[:, 4 + 2 * n:6 + 2 * n], ssum[:, 2 * n:2 * n + 2], 1.0 / (c1 - c0), EPS,
                                          ALU.mult, ALU.add)
                    if n:
                        ins.then_inc(mean_ready.sem, mean_ready.next((st, "latent")))
                    else:
                        step(ins)
                dve.wait_ge(rstd_ready.sem, rstd_ready.at((st, "latent")))
                for n, (c0, c1) in enumerate(((R_CQ, R_CKV), (R_CKV, R_KPE))):
                    for t in range(NT):
                        step(V.tensor_scalar(xn[:, t, c0 - R_CQ:c1 - R_CQ], rest[:, t, c0:c1],
                                             rstd[:, 4 + 2 * n + t:5 + 2 * n + t], None, ALU.mult))
                tick(rows_ready, (st, "latent"))
                columns((st, "latT"), lambda k: gcol(("mla_norm_q_2", l), k) if k < 3 else gcol(("mla_norm_kv_2", l), k - 3),
                        lambda k: hT[:, k, :], 5)
                def rotate(x1, x2, cos, sin, shape, outs, key):
                    r = [rtmp[:, n, 0:shape[0] * shape[1]].rearrange("p (h d) -> p h d", h=shape[0]) for n in range(4)]
                    step(V.tensor_tensor(r[0], x1, cos, ALU.mult))
                    step(V.tensor_tensor(r[1], x2, sin, ALU.mult))
                    step(V.tensor_tensor(r[2], x2, cos, ALU.mult))
                    ins = V.tensor_tensor(r[3], x1, sin, ALU.mult)
                    settle(dve, ins, dve_read, key)
                    for o1, o2 in outs:
                        step(V.tensor_tensor(o1, r[0], r[1], ALU.subtract))
                        step(V.tensor_tensor(o2, r[2], r[3], ALU.add))

                dve.wait_ge(act_step.sem, act_step.at("cos"))
                for t in range(NT):
                    dve.wait_ge(matmul_done.sem, matmul_done.at((st, "qp", t)))
                    q = G.of((st, "qp", t))[:, 0:256].rearrange("p (h e) -> p h e", h=4)
                    o = xn[:, t, 0:256].rearrange("p (h e) -> p h e", h=4)
                    cos, sin = (a[:, t, :].unsqueeze(1).broadcast_to([P, 4, 32]) for a in (cosb, sinb))
                    rotate(q[:, :, 0:32], q[:, :, 32:64], cos, sin, (4, 32), [(o[:, :, 0:32], o[:, :, 32:64])], (st, "qp", t))
                rotate(rest[:, :, R_KPE:R_KPE + 32], rest[:, :, R_KPE + 32:R_KPE + 64], cosb[:, :, :], sinb[:, :, :], (2, 32),
                       [(xn[:, :, 256 + 64 * u:288 + 64 * u], xn[:, :, 288 + 64 * u:320 + 64 * u]) for u in range(2)], (st, "kpe"))
                tick(rows_ready, (st, "rope"))
                for t in range(NT):
                    dve.wait_ge(matmul_done.sem, matmul_done.at((st, "vm", t)))
                    V.tensor_copy(vm[:, t, :], G.of((st, "vm", t))[:, :]).then_inc(dve_read.sem, dve_read.next((st, "vm", t)))
                columns((st, "peT"), None, lambda k: kpT, 3)
                attention(("mla", l), even(("mla", l), 4, 24))
                columns((("mla", l), "oT"), None, lambda k: oT[:, k, :], 4)
                merge(st, "ymla", 2)
                columns((st, "mT"), None, lambda k: oT[:, k, :])
                add_to_x(st, lambda t, h: (G.of(((st, "y", h), t)), ((st, "y", h), t), ((st, "y", h), t)))

            def memory(st):
                l = st[1]
                pre(st, ("norm_xattn_2", l))
                for j in (1, 3):
                    dve.wait_ge(matmul_done.sem, matmul_done.at(((st, "xq"), j)))
                    V.tensor_copy(xqT[:, j, :], G.of(((st, "xq"), j))[:, 0:S]).then_inc(dve_read.sem, dve_read.next(((st, "xq"), j)))
                norm((st, "mem"), merged)
                columns((st, "mem"), lambda k: gcol(("norm_mem_2", l), k), lambda k: memT[:, k, :])
                for j in (1, 3):
                    dve.wait_ge(matmul_done.sem, matmul_done.at(((st, "xk"), j)))
                    V.tensor_copy(xkT[:, j, :], G.of(((st, "xk"), j))[:, 0:S]).then_inc(dve_read.sem, dve_read.next(((st, "xk"), j)))
                dve.wait_ge(matmul_done.sem, matmul_done.at(((st, "xv"), 1)))
                V.tensor_copy(xv[:, 1, :], G.of(((st, "xv"), 1))[:, :]).then_inc(dve_read.sem, dve_read.next(((st, "xv"), 1)))
                attention(st, even(st, 4, 24))
                columns((st, "oT"), None, lambda k: oT[:, k, :], 4)
                k = (st, "y")
                add_to_x(st, lambda t, h: (G.of((k, t, h)), (k, t, h), (k, "chunk", ("l2", l, "xo"))))

            dve.wait_ge(consts_loaded.sem, consts_loaded.at("c"))
            for j in range(2):
                ins = V.tensor_copy(lines[:, j, 2 * REL_CLIP + 1:3 * P],
                                    lines[:, j, 2 * REL_CLIP:2 * REL_CLIP + 1].broadcast_to([HEADS_A, P - 1]))
            step(ins)
            for n in (1, 3):
                dve.wait_ge(transposed.sem, transposed.at(("gains", n)))
                if n == 1:
                    ins = V.tensor_copy(gT[:, 1, 0:gain_tiles[1]], TB.of(("gains", 1))[:, 0:gain_tiles[1]])
                else:
                    ins = V.tensor_copy(convwT[:, :, 0:TAPS * CT],
                                        TB.of(("gains", 3))[:, 0:2 * P].rearrange("p (l n) -> p l n", l=2)[:, :, 0:TAPS * CT])
                settle(dve, ins, dve_read, ("gains", n))
            dve.wait_ge(pool_step.sem, pool_step.at("bucket"))
            buckets = rtmp[0:BUCKETS, 0:2, :].rearrange("p a b -> p (a b)")[:, 0:3 * P]
            step(V.memset(buckets, -1.0))
            step(V.tensor_copy(buckets[:, P:P + 16], tmp2[0:BUCKETS, 0:16]))
            for b in range(16, BUCKETS):
                ds = [d for d in range(S) if t5_bucket(d) == b]
                step(V.memset(buckets[:, P + ds[0]:P + ds[-1] + 1], float(b)))
            step(V.tensor_scalar(onehot[:, :], buckets, tmp2[0:BUCKETS, 16:17], None, ALU.is_equal), "onehot")
            dve.wait_ge(matmul_done.sem, matmul_done.at("line"))
            settle(dve, V.tensor_copy(lines[0:NSA_HEADS, 2, :], G.of("line")[0:NSA_HEADS, 0:3 * P]), dve_read, "line")
            tick(dve_step, "lines")
            dve.wait_ge(act_read.sem, act_read.at(("gains", 2)))
            dve.wait_ge(pool_step.sem, pool_step.at("distances"))
            step(V.scalar_tensor_tensor(relC, relC, -1.0, relC, ALU.mult, ALU.max))
            for h in range(HEADS_C):
                step(V.tensor_scalar(relC[:, h, :], relC[:, h, :], -(2.0 ** (-8.0 * (h + 1) / HEADS_C)), None, ALU.mult))
            step(V.memset(relC[0:CHUNK, :, 1:CHUNK + 1], NEG))
            for n in range(2):
                step(V.tensor_tensor(tmp[:, 0:DH], lam_in[:, 2 * n, :], lam_in[:, 2 * n + 1, :], ALU.mult))
                step(V.tensor_reduce(lam[:, n:n + 1], tmp[:, 0:DH], AX.X, ALU.add), "lambda")
            lambda_init = 0.8 - 0.6 * math.exp(-0.3 * 2)
            dve.wait_ge(act_step.sem, act_step.at("lambda"))
            step(V.tensor_tensor(lam[:, 5:6], lam[:, 3:4], lam[:, 2:3], ALU.subtract))
            step(V.tensor_scalar(lam[:, 6:7], lam[:, 5:6], lambda_init, None, ALU.subtract))
            dve.wait_ge(pool_step.sem, pool_step.at("valid"))
            step(V.tensor_copy(pos_f[:, :], pos_i[:, :]))
            for t in range(NT):
                step(V.tensor_scalar(sinb[:, t, :], freq[:, :], pos_f[:, t:t + 1], None, ALU.mult))
            turns = tmp[:, 0:64].rearrange("p (t f) -> p t f", t=NT)
            step(V.tensor_scalar(turns, sinb[:, :, :], 1.0 / (2 * math.pi), None, ALU.mult))
            step(V.tensor_scalar(turns, turns, MAGIC, None, ALU.add))
            step(V.tensor_scalar(turns, turns, MAGIC, None, ALU.subtract))
            for part_of_turn in (6.28125, 0.0019340515136718750, 2 * math.pi - 6.28125 - 0.0019340515136718750):
                step(V.scalar_tensor_tensor(sinb[:, :, :], turns, -part_of_turn, sinb[:, :, :], ALU.mult, ALU.add))
            step(V.tensor_scalar(sinb[:, :, :], sinb[:, :, :], 3.1415925, -3.1415925, ALU.min, ALU.max))
            step(V.scalar_tensor_tensor(cosb[:, :, :], sinb[:, :, :], -1.0, sinb[:, :, :], ALU.mult, ALU.max))
            step(V.tensor_scalar(cosb[:, :, :], cosb[:, :, :], -1.0, math.pi / 2, ALU.mult, ALU.add), "angles")
            for st in stages:
                i = st[1]
                if st[0] == "ff1":
                    ffn(st, ("g", i, 0))
                elif st[0] == "ff2":
                    ffn(st, ("g", i, 4))
                elif st[0] == "ff3":
                    ffn(st, ("norm_ffn_2", i))
                else:
                    {"mix": mixer, "l2": branches, "xattn": memory}[st[0]](st)
            if last == ("ff3", DEPTH2 - 1):
                dve.wait_ge(squared.sem, squared.at(("final", 1)))
                mean("final", 2, 2, ssum[:, 4:6], D)
                dve.wait_ge(rstd_ready.sem, rstd_ready.at("final"))
                n = gain_n["final"]
                dve.wait_ge(gain_loaded[n % 2].sem, gain_loaded[n % 2].at("final"))
                for t in range(NT):
                    ins = V.scalar_tensor_tensor(xn[:, t, :], x[:, t, :], rstd[:, 2 + t:3 + t], gain_row[n % 2][:, :], ALU.mult, ALU.mult)
                    ins.then_inc(rows_ready.sem, rows_ready.next("final"))


_INS = """x norm_g ff1_w_in ff1_w_out ff2_w_in ff2_w_out a_w_qkv a_rel_bias a_w_o b_w_in b_ln_g b_ln_b b_w_s b_b_s b_w_o
c_w_qkv c_lambda c_subln_g c_w_o mem_2 positions_2 rel_bias_2 norm_mix_2 norm_xattn_2 norm_mem_2 norm_ffn_2 norm_final_2
w_in_2 conv_w_2 conv_b_2 conv_ln_g_2 conv_ln_b_2 w_branch_conv_2 cmp_pos_k_2 cmp_w1_k_2 cmp_b1_k_2 cmp_w2_k_2 cmp_pos_v_2
cmp_w1_v_2 cmp_b1_v_2 cmp_w2_v_2 w_branch_nsa_2 mla_norm_q_2 mla_norm_kv_2 w_uq_2 w_ukv_2 w_branch_mla_2 w_out_2 w_xq_2
w_xkv_2 w_xo_2 w_gate_up_2 w_down_2""".split()
STOP = None


def kernel(**inputs):
    import numpy as np
    import concourse.bacc as bacc
    from concourse.bass_utils import run_bass_kernel_spmd

    plan = {}
    for _ in range(2):
        nc = bacc.Bacc("TRN2", target_bir_lowering=False, num_devices=1)
        arrays, args = {}, {}
        for name in _INS:
            a = np.ascontiguousarray(inputs[name])
            arrays[f"in_{name}_dram"] = a
            args[name] = nc.dram_tensor(f"in_{name}_dram", a.shape, mybir.dt.from_np(a.dtype), kind="ExternalInput").ap()
        out = nc.dram_tensor("out_0_dram", (1, S, D), F32, kind="ExternalOutput").ap()
        build(nc, args, out, plan, STOP)
    return run_bass_kernel_spmd(nc, [arrays], core_ids=[0]).results[0]["out_0_dram"]
```

```python
import math
from contextlib import ExitStack

import concourse.bass as bass
from concourse import mybir

F32 = mybir.dt.float32
F32R = mybir.dt.float32r
I32 = mybir.dt.int32
ALU = mybir.AluOpType
ACT = mybir.ActivationFunctionType
AX = mybir.AxisListType

P = 128
S = 256
NT = S // P
D = 1024
KD = D // P
DEPTH = 4
DEPTH2 = 2
D_FF = 2816
KF = D_FF // P
EPS = 1e-6
NEG = -1e30
CHUNK = 64
HEADS_A = 16
DH = 64
REL_CLIP = 128
HEADS_C = 8
GROUPS_B = 8
CONV_CH = 512
CT = CONV_CH // P
TAPS = 31
NSA_HEADS = 8
CMP_BLOCK = 32
CMP_STRIDE = 16
CMP_HIDDEN = 256
N_CMP = (S - CMP_BLOCK) // CMP_STRIDE + 1
MLA_HEADS = 4
Q_RANK = 384
KV_RANK = 256
NOPE = 128
ROPE = 64
V_DIM = 128
X_HEADS = 4
ROPE_THETA = 10000.0
BUCKETS = 32
COL_GLU, COL_Q, COL_KV, COL_REST = 0, 1024, 1536, 2304
COL_MERGE = 3032
N_REST = COL_MERGE - COL_REST
R_GATE, R_CQ, R_CKV, R_KPE = 0, 24, 408, 664
TW = 257
SLOTS = 3
SLOT = 2048
AHEAD = 2
MAGIC = 1.5 * 2 ** 23


class Signal:

    def __init__(self, sem, reached, step=1):
        self.sem, self.reached, self.step, self.count = sem, reached, step, 0

    def next(self, key):
        self.count += self.step
        self.reached[key] = self.count
        return self.step

    def at(self, key):
        return self.reached.get(key, 1)

    def has(self, key):
        return key in self.reached


class Banks:

    def __init__(self, tiles, taken, readers):
        self.tiles, self.taken, self.readers, self.n, self.owner = tiles, taken, readers, 0, {}

    def take(self, pe, key):
        i = self.n % len(self.tiles)
        self.n += 1
        if i in self.owner:
            for reader in self.readers:
                if reader.has(self.owner[i]):
                    pe.wait_ge(reader.sem, reader.at(self.owner[i]))
        self.owner[i] = key
        self.taken[key] = i
        return self.tiles[i]

    def of(self, key):
        return self.tiles[self.taken.get(key, 0)]


class Split:

    def __init__(self, high, low):
        self.high, self.low = high, low

    def __getitem__(self, i):
        return Split(self.high[i], self.low[i])


def three(a, b):
    return [(a.high, b.high), (a.high, b.low), (a.low, b.high)]


def t5_bucket(d):
    exact = BUCKETS // 2
    if d < exact:
        return d
    return min(exact + int(math.log(d / exact) / math.log(128 / exact) * (BUCKETS - exact)), BUCKETS - 1)


def weight_chunks(w):
    out = []

    def cols(key, m, c0, n, each=256):
        for h, c in enumerate(range(c0, c0 + n, each)):
            nn = min(each, c0 + n - c)
            out.append(((*key, h), [(lambda s, n=nn, k=m.shape[0] // P: s[:, 0:k * n].rearrange("p (k n) -> p k n", k=k),
                                     m[:, c:c + nn].rearrange("(k p) n -> p k n", p=P))]))

    def rows(key, m, nk):
        n, total = m.shape[1], m.shape[0] // P
        for h, k0 in enumerate(range(0, total, nk)):
            out.append(((*key, h), [(lambda s, n=n, nk=min(nk, total - k0): s[:, 0:nk * n].rearrange("p (k n) -> p k n", k=nk),
                                     m[k0 * P:min(k0 + nk, total) * P, :].rearrange("(k p) n -> p k n", p=P))]))

    def ffn(key, w_in, w_out):
        for j in range(KF // 2):
            cols((key, "gate", j), w_in, j * 256, 256)
            cols((key, "up", j), w_in, D_FF + j * 256, 256)
        rows((key, "out"), w_out, 2)

    for i in range(DEPTH):
        ffn(("ff1", i), w["ff1_w_in"][i], w["ff1_w_out"][i])
        kind, j = i % 3, i // 3
        win, wo = [("a_w_qkv", "a_w_o"), ("b_w_in", "b_w_o"), ("c_w_qkv", "c_w_o")][kind]
        for c in range(w[win].shape[2] // 512):
            cols((("mix", i), "in", c), w[win][j], c * 512, 512)
        for c in range(2):
            cols((("mix", i), "out", c), w[wo][j], c * 512, 512)
        ffn(("ff2", i), w["ff2_w_in"][i], w["ff2_w_out"][i])
    for l in range(DEPTH2):
        w_in = w["w_in_2"][l]
        L = ("l2", l)
        for c in range(2):
            cols((*L, "glu", c), w_in, c * 512, 512)
        for h in range(2):
            out.append(((*L, "q", h), [
                (lambda s, c=c, g=g: s[:, :].rearrange("p (k c g d) -> p k c g d", k=KD, c=2, g=2)[:, :, c, g, :],
                 w_in[:, COL_Q + (4 * g + 2 * h + c) * DH:COL_Q + (4 * g + 2 * h + c + 1) * DH].rearrange("(k p) d -> p k d", p=P))
                for c in range(2) for g in range(2)]))
        cols((*L, "kv"), w_in, COL_KV, 768)
        cols((*L, "rest"), w_in, COL_REST, N_REST)
        for v in range(2):
            rows((*L, "cmp", v), w[("cmp_w1_k_2", "cmp_w1_v_2")[v]][l], 8)
        for c in range(4):
            cols((*L, "merge", c), w_in, COL_MERGE + c * 512, 512)
        rows((*L, "conv"), w["w_branch_conv_2"][l], 2)
        rows((*L, "nsa"), w["w_branch_nsa_2"][l], 2)
        for c in range(4, 6):
            cols((*L, "merge", c), w_in, COL_MERGE + c * 512, 512)
        cols((*L, "uq"), w["w_uq_2"][l], 0, 768, 384)
        rows((*L, "ukv"), w["w_ukv_2"][l], 2)
        rows((*L, "mla"), w["w_branch_mla_2"][l], 2)
        for c in range(2):
            cols((*L, "out", c), w["w_out_2"][l], c * 512, 512)
        cols((*L, "xq"), w["w_xq_2"][l], 0, 512)
        cols((*L, "xk"), w["w_xkv_2"][l], 0, 512)
        cols((*L, "xv"), w["w_xkv_2"][l], 512, 512)
        rows((*L, "xo"), w["w_xo_2"][l], 2)
        ffn(("ff3", l), w["w_gate_up_2"][l], w["w_down_2"][l])
    return out


def build(nc, w, out, plan, stop=None):
    chunks = weight_chunks(w)
    chunk_index = {key: n for n, (key, _) in enumerate(chunks)}
    whole = [len(key) > 2 and key[2] == "cmp" for key, _ in chunks]
    split_no = [n - sum(whole[:n]) for n in range(len(chunks))]

    with ExitStack() as ctx:
        def sb(name, shape, dt=F32):
            return ctx.enter_context(nc.sbuf_tensor("sb_" + name, shape, dt))

        def signal(name, step=1):
            return Signal(ctx.enter_context(nc.semaphore(name)), plan.setdefault(name, {}), step)

        slots = [sb(f"slot{i}", [P, SLOT]) for i in range(SLOTS)]
        high = [sb(f"high{i}", [P, SLOT], F32R) for i in range(SLOTS)]
        low = [sb(f"low{i}", [P, SLOT], F32R) for i in range(SLOTS)]
        x = sb("x", [P, NT, D])
        hT = Split(sb("hT_high", [P, KD, S], F32R), sb("hT_low", [P, KD, S], F32R))
        oT = Split(sb("oT_high", [P, KD, S], F32R), sb("oT_low", [P, KD, S], F32R))
        xn = sb("xn", [P, NT, D])
        gain_row = [sb(f"gain_row{i}", [P, D]) for i in range(2)]
        o_rows = sb("o_rows", [P, NT, D])
        ident = sb("ident", [P, P])
        minus_half = sb("minus_half", [P, 16])
        gT = sb("gT", [P, 3, P])
        convwT = sb("convwT", [P, 2, P])
        lam = sb("lam", [P, 8])
        subln = sb("subln", [P, P])
        cosb = sb("cosb", [P, NT, 32])
        sinb = sb("sinb", [P, NT, 32])
        valid = sb("valid", [P, NT])
        ssum = sb("ssum", [P, 8])
        mean_sq = sb("mean_sq", [P, 16])
        rstd = sb("rstd", [P, 16])
        stats = sb("stats", [P, 2, 6])
        moments = sb("moments", [P, NT, 2])
        tmp = sb("tmp", [P, 512])
        sc = sb("sc", [P, 3, S])
        nmax = sb("nmax", [P, 3])
        pr = sb("pr", [P, 3, S])
        prT = sb("prT", [P, 2, S])
        sums = sb("sums", [P, NT, 32])
        inv = sb("inv", [P, NT, 32])
        silu = prT
        hid_f = sc
        tmp2 = xn[:, 1, 512:1024]
        rtmp = o_rows[:, 0, :].rearrange("p (n m) -> p n m", n=4)
        line_dram = [nc.dram_tensor(f"line_dram{i}", [HEADS_A, 3 * P], F32).ap() for i in range(3)]

        with nc.sbuf_tensor("sb_hidden_high", [P, KF, S], F32R) as hid_high, \
                nc.sbuf_tensor("sb_hidden_low", [P, KF, S], F32R) as hid_low:
            hidT = Split(hid_high, hid_low)
        AR = 14500
        arena = sb("arena", [P, AR])
        used = [0]

        def part(values, pattern=None, **dims):
            a = arena[:, used[0]:used[0] + values]
            used[0] += values
            assert used[0] <= AR, used[0]
            return a.rearrange(pattern, **dims) if pattern else a

        gains = part(3 * P, "p (n m) -> p n m", n=3)
        convw = part(2 * P, "p (n m) -> p n m", n=2)
        lines = part(9 * P, "p (j w) -> p j w", j=3)[0:HEADS_A]
        onehot = part(3 * P)[0:BUCKETS]
        bias2 = part(NSA_HEADS)[0:BUCKETS]
        lam_in = part(4 * DH, "p (a d) -> p a d", a=4)
        pos_i = part(NT).bitcast(I32)
        pos_f = part(NT)
        freq = part(32)
        used[0] = 0
        qkT = part(16 * S, "p (c s) -> p c s", c=16)
        v_rows = part(NT * D, "p (t n) -> p t n", t=NT)
        relA = part(HEADS_A * TW, "p (h w) -> p h w", h=HEADS_A)
        relC = relA[:, 0:HEADS_C, :]
        used[0] = 0
        u_rows = part(NT * D, "p (t n) -> p t n", t=NT)
        g_rows = part(NT * D, "p (t n) -> p t n", t=NT)
        ws = part(GROUPS_B * P, "p (g s) -> p g s", g=GROUPS_B)
        wsT = part(GROUPS_B * P, "p (g s) -> p g s", g=GROUPS_B)
        used[0] = 0
        merge_gate = part(NT * 2 * D, "p (t n) -> p t n", t=NT)
        merged = merge_gate[:, :, 0:D]
        relN = part(NSA_HEADS * TW, "p (h w) -> p h w", h=NSA_HEADS)
        causal = part(TW)
        rest = part(NT * N_REST, "p (t n) -> p t n", t=NT)
        vwin = part(NT * P, "p (t n) -> p t n", t=NT)
        qsT = part(4 * S, "p (c s) -> p c s", c=4)
        kslcT = part(S)
        kwinT = part(S)
        vslc = part(NT * P, "p (t n) -> p t n", t=NT)
        hid_c = part(2 * 2 * 30, "p (v f n) -> p v f n", v=2, f=2)
        kcT = part(32)
        vc = part(2 * DH, "p (g d) -> p g d", g=2)
        w2k = part(2 * 2 * DH, "p (f u d) -> p f u d", f=2, u=2)
        w2v = part(2 * DH, "p (f d) -> p f d", f=2)
        here = used[0]
        bT = part(CT * S, "p (c s) -> p c s", c=CT)
        glu = part(CT * (S + TAPS - 1), "p (c s) -> p c s", c=CT)
        convT = part(CT * S, "p (c s) -> p c s", c=CT)
        aT = glu[:, :, TAPS - 1:TAPS - 1 + S]
        used[0] = here
        qnT = part(MLA_HEADS * S, "p (h s) -> p h s", h=MLA_HEADS)
        knT = part(MLA_HEADS * S, "p (h s) -> p h s", h=MLA_HEADS)
        qpT = part(2 * S, "p (h s) -> p h s", h=2)
        kpT = part(S)
        vm = part(NT * 512, "p (t n) -> p t n", t=NT)
        used[0] = 0
        xqT = part(X_HEADS * S, "p (h s) -> p h s", h=X_HEADS)
        xkT = part(X_HEADS * S, "p (h s) -> p h s", h=X_HEADS)
        xv = part(NT * 512, "p (t n) -> p t n", t=NT)
        zeros = part(S)
        mem = o_rows
        tokT = xn[:, 0, 0:2 * S].rearrange("p (v s) -> p v s", v=2)
        flat = o_rows[:, :, :].rearrange("p t n -> p (t n)")
        tok2 = flat[:, 0:4 * S].rearrange("p (v g s) -> p v g s", v=2, g=2)
        blk = flat[:, 4 * S:4 * S + 960].rearrange("p (v j g c) -> p v j g c", v=2, j=16, g=2)

        psum = [ctx.enter_context(nc.psum_tensor(f"bank{i}", [P, 512], F32)) for i in range(8)]

        slot_loaded = [signal(f"slot{i}_loaded", 16) for i in range(SLOTS)]
        consts_loaded = signal("consts_loaded", 16)
        lines_stored = signal("lines_stored", 16)
        table_loaded = signal("table_loaded", 16)
        gain_loaded = [signal(f"gain{i}_loaded", 16) for i in range(2)]
        small_loaded = signal("small_loaded", 16)
        out_stored = signal("out_stored", 16)
        matmul_done = signal("matmul_done")
        transposed = signal("transposed")
        act_read = signal("act_read")
        dve_read = signal("dve_read")
        squared = signal("squared")
        high_ready = signal("high_ready")
        low_ready = signal("low_ready")
        dve_step = signal("dve_step")
        act_step = signal("act_step")
        pool_step = signal("pool_step")
        pe_step = signal("pe_step")
        scored = signal("scored")
        maxed = signal("maxed")
        weighed = signal("weighed")
        mean_ready = signal("mean_ready")
        rstd_ready = signal("rstd_ready")
        x_ready = signal("x_ready")
        rows_ready = signal("rows_ready")
        tok_loaded = signal("tok_loaded", 16)
        mem_loaded = signal("mem_loaded", 16)
        spatial_loaded = signal("spatial_loaded", 16)

        readers = (act_read, dve_read)
        G = Banks(psum[0:4], plan.setdefault("bank_g", {}), readers)
        SB = Banks(psum[4:6], plan.setdefault("bank_s", {}), readers)
        TB = Banks(psum[6:8], plan.setdefault("bank_t", {}), readers)
        chunk_end = plan.setdefault("chunk_end", {})
        chunk_of = plan.setdefault("chunk_of", {})

        col = {}
        loads = []

        tile, row = 0, 0
        gain_tiles = []

        def put(key, ap, n):
            nonlocal tile, row
            if row + n > P:
                gain_tiles.append(row)
                tile, row = tile + 1, 0
            col[key] = (tile, row)
            loads.append((gains[row:row + n, tile, :], ap))
            row += n

        for i in range(DEPTH):
            for n in (0, 2, 4):
                put(("g", i, n), w["norm_g"][i, n].rearrange("(a p) -> a p", p=P), KD)
        for l in range(DEPTH2):
            for name in ("norm_mix_2", "norm_xattn_2", "norm_mem_2", "norm_ffn_2"):
                put((name, l), w[name][l].rearrange("(a p) -> a p", p=P), KD)
        for l in range(DEPTH2):
            for name, n in (("conv_b_2", 4), ("conv_ln_g_2", 4), ("conv_ln_b_2", 4), ("mla_norm_q_2", 3),
                            ("mla_norm_kv_2", 2), ("cmp_b1_k_2", 2), ("cmp_b1_v_2", 2)):
                put((name, l), w[name][l].rearrange("(a p) -> a p", p=P), n)
            for name in ("cmp_pos_k_2", "cmp_pos_v_2"):
                put((name, l), w[name][l].rearrange("(a b) d -> a (b d)", b=2), 16)
        put("b_b_s", w["b_b_s"][0], GROUPS_B)
        assert tile <= 2
        gain_tiles.append(row)

        def gcol(key, k=0):
            t, r = col[key]
            return gT[:, t, r + k:r + k + 1]

        row_gains = []
        for i in range(DEPTH):
            row_gains.append((("g", i, 1), w["norm_g"][i, 1]))
            if i % 3 == 1:
                row_gains += [("ln_g", w["b_ln_g"][0]), ("ln_b", w["b_ln_b"][0])]
            row_gains += [(("g", i, 3), w["norm_g"][i, 3]), (("g", i, 5), w["norm_g"][i, 5])]
        row_gains.append(("final", w["norm_final_2"]))
        gain_n = {key: n for n, (key, _) in enumerate(row_gains)}
        gain_for = {("ff1", i): ("g", i, 1) for i in range(DEPTH)}
        gain_for |= {("mix", i): ("g", i, 3) for i in range(DEPTH)}
        gain_for |= {("ff2", i): ("g", i, 5) for i in range(DEPTH)}

        block = ctx.enter_context(nc.Block())

        stages = []
        for i in range(DEPTH):
            stages += [("ff1", i), ("mix", i), ("ff2", i)]
        for l in range(DEPTH2):
            stages += [("l2", l), ("xattn", l), ("ff3", l)]
        if stop is not None:
            stages = stages[:stop]
        last = stages[-1]

        def stage_of(key):
            if key[0] == "l2":
                return ("xattn", key[1]) if key[2] in ("xq", "xk", "xv", "xo") else ("l2", key[1])
            return key[0]

        def raw_view(key):
            n = chunk_index[key]
            return chunks[n][1][0][0](slots[n % SLOTS])

        def view(key):
            n = chunk_index[key]
            i = split_no[n] % SLOTS
            if key[0] == "l2" and key[2] == "q":
                return Split(*(a[i][:, :].rearrange("p (k n) -> p k n", k=KD) for a in (high, low)))
            return Split(*(chunks[n][1][0][0](a[i]) for a in (high, low)))

        last_chunk = max(n for n, (key, _) in enumerate(chunks) if stage_of(key) in stages)

        def users(n):
            before = [m for m in range(n) if not whole[m] and split_no[m] == split_no[n] - SLOTS]
            return before[0] if before else None

        def filled(n):
            return sum(src.shape[1] * src.shape[2] for _, src in chunks[n][1])



        @block.sync
        def _(sp):
            sp.dma_start(x[:, :, :], w["x"][0].rearrange("(t p) d -> p t d", p=P)).then_inc(consts_loaded.sem, consts_loaded.next("c"))
            for dst, src in loads:
                sp.dma_start(dst, src).then_inc(consts_loaded.sem, consts_loaded.next("c"))
            for l in range(DEPTH2):
                sp.dma_start(convw[0:TAPS * CT, l, :], w["conv_w_2"][l].rearrange("t (c p) -> (t c) p", p=P)) \
                    .then_inc(consts_loaded.sem, consts_loaded.next("c"))
            sp.dma_start(bias2[:, :], w["rel_bias_2"]).then_inc(consts_loaded.sem, consts_loaded.next("c"))
            sp.dma_start(lam_in[:, :, :].rearrange("p a d -> p (a d)"),
                         w["c_lambda"].rearrange("o a d -> o (a d)").broadcast_to([P, 4 * DH])) \
                .then_inc(consts_loaded.sem, consts_loaded.next("c"))
            sp.dma_start(subln[:, :], w["c_subln_g"].broadcast_to([P, P])).then_inc(consts_loaded.sem, consts_loaded.next("c"))
            sp.dma_start(pos_i[:, :], w["positions_2"][0].rearrange("(t p) -> p t", p=P), allow_slow_non_contiguous=True) \
                .then_inc(consts_loaded.sem, consts_loaded.next("c"))
            for j in range(2):
                sp.dma_start(lines[:, j, 0:2 * REL_CLIP + 1], w["a_rel_bias"][j]).then_inc(consts_loaded.sem, consts_loaded.next("c"))
            sp.wait_ge(dve_step.sem, dve_step.at("lines"))
            for j in range(3):
                n = HEADS_A if j < 2 else NSA_HEADS
                sp.dma_start(line_dram[j][0:n, 0:3 * P], lines[0:n, j, 0:3 * P]).then_inc(lines_stored.sem, lines_stored.next("l"))

            for n, (key, parts) in enumerate(chunks):
                st = stage_of(key)
                if st not in stages:
                    continue
                before = n - SLOTS
                if before >= 0 and whole[before]:
                    sp.wait_ge(matmul_done.sem, matmul_done.at(chunk_end.get(chunks[before][0])))
                elif before >= 0:
                    sp.wait_ge(low_ready.sem, low_ready.at(before))
                slot = slots[n % SLOTS]
                for dst, src in parts:
                    sp.dma_start(dst(slot), src).then_inc(slot_loaded[n % SLOTS].sem, slot_loaded[n % SLOTS].next(key))
            if last == ("ff3", DEPTH2 - 1):
                sp.wait_ge(rows_ready.sem, rows_ready.at("final"))
                sp.dma_start(out[0].rearrange("(t p) d -> p t d", p=P), xn[:, :, :]).then_inc(out_stored.sem, out_stored.next("o"))
            else:
                sp.wait_ge(x_ready.sem, x_ready.at((last, 1)))
                sp.dma_start(out[0].rearrange("(t p) d -> p t d", p=P), x[:, :, :]).then_inc(out_stored.sem, out_stored.next("o"))
            if stop is not None:
                sp.wait_ge(lines_stored.sem, lines_stored.at("l"))
                for sig in (*gain_loaded, table_loaded, small_loaded, tok_loaded, mem_loaded, spatial_loaded):
                    if sig.reached:
                        sp.wait_ge(sig.sem, max(sig.reached.values()))
            sp.wait_ge(out_stored.sem, out_stored.at("o"))


        def settle(eng, ins, sig, key=None):
            ins.then_inc(sig.sem, sig.next(key if key is not None else ("n", sig.count)))
            eng.wait_ge(sig.sem, sig.count)

        def rev(table, t, kn):
            top = P * (t + 1)
            return table[:, top:top - kn:-1]

        def units_of(st):
            kind, i = st
            units = []
            if kind == "mix":
                for t in range(NT):
                    for s in range(16):
                        half = slice(DH * (s % 2), DH * (s % 2) + DH)
                        if i % 3 == 0:
                            table, v0, width = relA[:, s, :], s * DH, DH
                        else:
                            table, v0, width = relC[:, s // 2, :], (s // 2) * P, P
                        kn = P * (t + 1)
                        per = 512 // width
                        units.append(dict(
                            qk=[(qkT[half, s // 2, t * P:(t + 1) * P], qkT[half, 8 + s // 2, 0:kn])],
                            t=t, kn=kn, bias=rev(table, t, kn), scale=DH ** -0.5,
                            v=[v_rows[:, b, v0:v0 + width] for b in range(t + 1)],
                            acc=(st, "o", t, s // per), c0=(s % per) * width, width=width, col=s))
            elif kind == "l2":
                for t in range(NT):
                    for br in range(3):
                        for h in range(NSA_HEADS):
                            g = h // 4
                            half = slice(DH * g, DH * g + DH)
                            q = qsT[half, h % 4, t * P:(t + 1) * P]
                            if br == 0:
                                kn = min(N_CMP, (P * (t + 1) - CMP_BLOCK) // CMP_STRIDE + 1)
                                k = kcT[half, g * N_CMP:g * N_CMP + kn]
                                top = P * (t + 1) - (CMP_BLOCK - 1)
                                bias = relN[:, h, top:top - CMP_STRIDE * (kn - 1) - 1:-CMP_STRIDE]
                                v = [vc[0:kn, g, :]]
                            else:
                                kn = P * (t + 1)
                                k = (kslcT if br == 1 else kwinT)[half, 0:kn]
                                bias = rev(relN[:, h, :], t, kn)
                                v = [vslc[:, b, g * DH:g * DH + DH] if br == 1 else
                                     vwin[:, b, g * DH:g * DH + DH] for b in range(t + 1)]
                            units.append(dict(qk=[(q, k)], t=t, kn=kn, bias=bias, scale=DH ** -0.5, v=v,
                                              acc=(st, "o", t, br), c0=h * DH, width=DH, col=br * 8 + h))
            elif kind == "mla":
                for t in range(NT):
                    for h in range(MLA_HEADS):
                        half = slice(DH * (h % 2), DH * (h % 2) + DH)
                        kn = P * (t + 1)
                        tok = slice(t * P, (t + 1) * P)
                        units.append(dict(
                            qk=[(qnT[:, h, tok], knT[:, h, 0:kn]), (qpT[half, h // 2, tok], kpT[half, 0:kn])],
                            t=t, kn=kn, bias=rev(causal, t, kn), scale=(NOPE + ROPE) ** -0.5,
                            v=[vm[:, b, h * P:(h + 1) * P] for b in range(t + 1)],
                            acc=(st, "o", t, 0), c0=h * P, width=P, col=24 + h))
            elif kind == "xattn":
                for t in range(NT):
                    for h in range(X_HEADS):
                        units.append(dict(
                            qk=[(xqT[:, h, t * P:(t + 1) * P], xkT[:, h, :])], t=t, kn=S, bias=zeros,
                            scale=P ** -0.5, v=[xv[:, b, h * P:(h + 1) * P] for b in range(NT)],
                            acc=(st, "o", t, 0), c0=h * P, width=P, col=24 + h))
            for n, u in enumerate(units):
                u["first"] = n == 0 or not any(m["acc"] == u["acc"] for m in units[:n])
                u["last"] = not any(m["acc"] == u["acc"] for m in units[n + 1:])
                u["blocks"] = [(b * P, min(P, u["kn"] - b * P)) for b in range(len(u["v"]))]
            return units

        @block.tensor
        def _(pe):

            def arrived(key):
                n = chunk_index[key]
                if whole[n]:
                    pe.wait_ge(slot_loaded[n % SLOTS].sem, slot_loaded[n % SLOTS].at(key))
                else:
                    pe.wait_ge(low_ready.sem, low_ready.at(n))

            def mm(o, lhsT, rhs, start, stop):
                return nc.tensor.matmul(o, lhsT, rhs, start=start, stop=stop)

            def split_mm(o, lhsT, rhs, start, stop):
                for n, (a, b) in enumerate(three(lhsT, rhs)):
                    ins = mm(o, a, b, start and n == 0, stop and n == 2)
                return ins

            def product(key, pairs, width, rows=P, c0=0, bank=None, done=True):
                o = (G.take(pe, key) if bank is None else bank)[0:rows, c0:c0 + width]
                for n, (lhsT, rhs) in enumerate(pairs):
                    one = split_mm if type(lhsT) is Split else mm
                    ins = one(o, lhsT, rhs, n == 0, n == len(pairs) - 1)
                if done:
                    ins.then_inc(matmul_done.sem, matmul_done.next(key))

            def to_columns(key, src, nk, nt=NT, waits=()):
                for b in range((nk + 1) // 2):
                    bank = TB.take(pe, (key, b))
                    for kt in range(2 * b, min(2 * b + 2, nk)):
                        for t in range(nt):
                            ins = nc.tensor.transpose(bank[:, (kt % 2) * S + t * P:(kt % 2) * S + (t + 1) * P],
                                                      src(t, kt), ident[:, :])
                    ins.then_inc(transposed.sem, transposed.next((key, b)))

            def norm(n):
                pe.wait_ge(rows_ready.sem, rows_ready.at((n, NT - 1)))
                to_columns(n, lambda t, kt: xn[:, t, kt * P:(kt + 1) * P], KD)
                pe.wait_ge(dve_read.sem, dve_read.at((n, 3)))

            def columns_gemm(ckeys, key, src):
                c = 0
                for ckey in ckeys:
                    arrived(ckey)
                    s = view(ckey)
                    for h in range(s.high.shape[2] // P):
                        chunk_of[(key, c)] = ckey
                        product((key, c), [(s[:, k, h * P:(h + 1) * P], src[:, k, :]) for k in range(KD)], S)
                        chunk_end[ckey] = (key, c)
                        c += 1

            def rows_gemm(ckeys, key, src):
                banks = [G.take(pe, (key, t)) for t in range(NT)]
                c0 = 0
                for ckey in ckeys:
                    arrived(ckey)
                    s = view(ckey)
                    n = s.high.shape[2]
                    for t in range(NT):
                        last_one = ckey == ckeys[-1]
                        ekey = (key, t) if last_one else (key, "part", t)
                        chunk_of[ekey] = ckey
                        product(ekey, [(src[:, k, t * P:(t + 1) * P], s[:, k, :]) for k in range(KD)], n, c0=c0, bank=banks[t],
                                done=last_one or t == NT - 1)
                        chunk_end[ckey] = ekey
                    c0 += n

            def wide_gemm(st, ckeys, key, src):
                banks = [[G.take(pe, (key, t, h)) for h in range(2)] for t in range(NT)]
                k = 0
                total = 2 * len(ckeys)
                for c in ckeys:
                    if st in ("ff1", "ff2", "ff3"):
                        pe.wait_ge(dve_step.sem, dve_step.at((key[0], "h", k + 1)))
                    arrived(c)
                    s = view(c)
                    for kk in range(2):
                        for t in range(NT):
                            for h in range(2):
                                ins = split_mm(banks[t][h][:, :], src[:, k, t * P:(t + 1) * P],
                                               s[:, kk, h * 512:(h + 1) * 512], k == 0, k == total - 1)
                        k += 1
                    ins.then_inc(matmul_done.sem, matmul_done.next((key, "chunk", c)))
                    chunk_end[c] = (key, "chunk", c)

            def ffn(st):
                norm((st, "norm"))
                for j in range(KF // 2):
                    banks = [G.take(pe, (st, "h", 2 * j + c)) for c in range(2)]
                    for u, kind in enumerate(("gate", "up")):
                        ckey = (st, kind, j, 0)
                        arrived(ckey)
                        s = view(ckey)
                        for c in range(2):
                            key = (st, "h", 2 * j + c) if u else (st, "gate", j)
                            product(key, [(s[:, k, c * P:(c + 1) * P], hT[:, k, :]) for k in range(KD)], S,
                                    c0=u * S, bank=banks[c], done=bool(u or c))
                            chunk_end[ckey] = key
                wide_gemm(st[0], [(st, "out", m) for m in range(KF // 2)], (st, "y"), hidT)

            def attention(st):
                units = units_of(st)
                banks = {}
                for i in range(len(units) + 2):
                    if i < len(units):
                        u = units[i]
                        bank = SB.take(pe, (st, "s", i))
                        for n, (q, k) in enumerate(u["qk"]):
                            ins = mm(bank[:, 0:u["kn"]], q, k, n == 0, n == len(u["qk"]) - 1)
                        ins.then_inc(scored.sem, scored.next((st, i)))
                    if 1 <= i <= len(units):
                        u = units[i - 1]
                        pe.wait_ge(weighed.sem, weighed.at((st, i - 1)))
                        bank = TB.take(pe, (st, "p", i - 1))
                        for b, (k0, n) in enumerate(u["blocks"]):
                            ins = nc.tensor.transpose(bank[0:n, b * P:(b + 1) * P], pr[:, (i - 1) % 3, k0:k0 + n], ident[:, :])
                        ins.then_inc(transposed.sem, transposed.next((st, "p", i - 1)))
                    if i >= 2:
                        u = units[i - 2]
                        if u["first"]:
                            banks[u["acc"]] = G.take(pe, u["acc"])
                        pe.wait_ge(act_read.sem, act_read.at((st, "p", i - 2)))
                        for b, (k0, n) in enumerate(u["blocks"]):
                            ins = mm(banks[u["acc"]][:, u["c0"]:u["c0"] + u["width"]], prT[0:n, (i - 2) % 2, b * P:(b + 1) * P],
                                     u["v"][b], b == 0, b == len(u["blocks"]) - 1)
                        ins.then_inc(matmul_done.sem, matmul_done.next((st, "pv", i - 2)))

            def output_columns(st, nk):
                pe.wait_ge(rows_ready.sem, rows_ready.at((st, "o", NT - 1)))
                to_columns((st, "oT"), lambda t, kt: o_rows[:, t, kt * P:(kt + 1) * P], nk)
                pe.wait_ge(dve_read.sem, dve_read.at(((st, "oT"), (nk + 1) // 2 - 1)))

            def mixer(st):
                i = st[1]
                norm((st, "norm"))
                if i % 3 == 1:
                    for c in range(4):
                        rows_gemm([(st, "in", c, h) for h in range(2)], (st, "in", c), hT)
                    pe.wait_ge(pool_step.sem, pool_step.at("spatial"))
                    to_columns((st, "ws"), lambda t, kt: ws[:, kt, :], GROUPS_B, nt=1)
                    for b in range(4):
                        sig = (act_read, dve_read)[b % 2]
                        pe.wait_ge(sig.sem, sig.at(((st, "ws"), b)))
                    for t in range(NT):
                        pe.wait_ge(rows_ready.sem, rows_ready.at((st, "v", t)))
                        for h in range(2):
                            bank = G.take(pe, (st, "sv", t, h))
                            for g in range(4):
                                ins = mm(bank[:, g * P:(g + 1) * P], wsT[:, 4 * h + g, :],
                                         g_rows[:, t, (4 * h + g) * P:(4 * h + g + 1) * P], True, True)
                            ins.then_inc(matmul_done.sem, matmul_done.next((st, "sv", t, h)))
                else:
                    for c in range(4):
                        columns_gemm([(st, "in", c, h) for h in range(2)], (st, "qk", c), hT)
                    for c in range(2):
                        rows_gemm([(st, "in", 4 + c, h) for h in range(2)], (st, "v", c), hT)
                    pe.wait_ge(act_read.sem, act_read.at(((st, "qk", 3), 2)))
                    pe.wait_ge(dve_read.sem, dve_read.at(((st, "qk", 3), 3)))
                    pe.wait_ge(dve_read.sem, dve_read.at(((st, "v", 1), 1)))
                    pe.wait_ge(act_read.sem, act_read.at(((st, "v", 1), 0)))
                    attention(st)
                output_columns(st, KD)
                for c in range(2):
                    rows_gemm([(st, "out", c, h) for h in range(2)], (st, "y", c), oT)

            def branches(st):
                l = st[1]
                L = ("l2", l)
                norm((st, "norm"))
                for c in range(2):
                    columns_gemm([(*L, "glu", c, h) for h in range(2)], (st, "glu", c), hT)
                columns_gemm([(*L, "q", h) for h in range(2)], (st, "q"), hT)
                for h, names in enumerate((("tok", 0), ("tok", 1), "kslc", "vslc", "kwin", "vwin")):
                    ckey = (*L, "kv", h // 2)
                    arrived(ckey)
                    s = view(ckey)[:, :, (h % 2) * P:(h % 2 + 1) * P]
                    if names in ("vslc", "vwin"):
                        for t in range(NT):
                            chunk_of[((st, names), t)] = ckey
                            product(((st, names), t), [(hT[:, k, t * P:(t + 1) * P], s[:, k, :]) for k in range(KD)], P)
                        chunk_end[ckey] = ((st, names), 1)
                    else:
                        chunk_of[(st, names)] = ckey
                        product((st, names), [(s[:, k, :], hT[:, k, :]) for k in range(KD)], S)
                        chunk_end[ckey] = (st, names)
                rows_gemm([(*L, "rest", h) for h in range(2)], (st, "rest", 0), hT)
                rows_gemm([(*L, "rest", 2)], (st, "rest", 1), hT)
                pe.wait_ge(small_loaded.sem, small_loaded.at(st))
                for v in range(2):
                    pe.wait_ge(dve_read.sem, dve_read.at((st, "blk", v)))
                    for f in range(2):
                        for h in range(2):
                            arrived((*L, "cmp", v, h))
                        product((st, "hid", v, f), [(raw_view((*L, "cmp", v, j // 8))[:, j % 8, f * P:(f + 1) * P],
                                                     blk[:, v, j, :, :].rearrange("p g c -> p (g c)")) for j in range(16)], 30)
                    for h in range(2):
                        chunk_end[(*L, "cmp", v, h)] = (st, "hid", v, 1)
                for c in range(4):
                    rows_gemm([(*L, "merge", c, h) for h in range(2)], (st, "merge", c), hT)
                    if c == 2:
                        pe.wait_ge(act_read.sem, act_read.at((st, "hid", 1, 1)))
                        product((st, "kc"), [(w2k[:, f, :, :].rearrange("p u d -> p (u d)"), hid_c[:, 0, f, :]) for f in range(2)], 30)
                        for g in range(2):
                            product((st, "vc", g), [(hid_c[:, 1, f, g * N_CMP:(g + 1) * N_CMP], w2v[:, f, :]) for f in range(2)],
                                    DH, rows=N_CMP)
                pe.wait_ge(dve_step.sem, dve_step.at((st, "conv")))
                for t in range(NT):
                    bank = TB.take(pe, (st, "conv_rows", t))
                    for c in range(CT):
                        ins = nc.tensor.transpose(bank[:, c * P:(c + 1) * P], convT[:, c, t * P:(t + 1) * P], ident[:, :])
                    ins.then_inc(transposed.sem, transposed.next((st, "conv_rows", t)))
                pe.wait_ge(rows_ready.sem, rows_ready.at((st, "conv", NT - 1)))
                to_columns((st, "convT"), lambda t, kt: xn[:, t, kt * P:(kt + 1) * P], CT)
                pe.wait_ge(dve_read.sem, dve_read.at(((st, "convT"), 1)))
                wide_gemm("conv", [(*L, "conv", h) for h in range(2)], (st, "yconv"), oT)
                pe.wait_ge(dve_read.sem, dve_read.at((st, "vc", 1)))
                pe.wait_ge(act_read.sem, act_read.at((st, "kwin")))
                attention(st)
                output_columns(st, 4)
                wide_gemm("nsa", [(*L, "nsa", h) for h in range(2)], (st, "ynsa"), oT)
                for c in range(4, 6):
                    rows_gemm([(*L, "merge", c, h) for h in range(2)], (st, "merge", c), hT)
                pe.wait_ge(rows_ready.sem, rows_ready.at((st, "latent")))
                to_columns((st, "latT"), lambda t, kt: xn[:, t, kt * P:(kt + 1) * P], 5)
                pe.wait_ge(dve_read.sem, dve_read.at(((st, "latT"), 2)))
                for h in range(2):
                    arrived((*L, "uq", h))
                    s = view((*L, "uq", h))
                    for g in range(2):
                        product((st, "qn", 2 * h + g), [(s[:, k, g * 192:g * 192 + P], hT[:, k, :]) for k in range(3)], S)
                    for t in range(NT):
                        product((st, "qp", h, t), [(hT[:, k, t * P:(t + 1) * P],
                                                    Split(*(a[:, k, :].rearrange("p (h e) -> p h e", h=2)[:, :, P:192]
                                                            for a in (s.high, s.low)))) for k in range(3)], 128)
                    chunk_end[(*L, "uq", h)] = (st, "qp", h, 1)
                arrived((*L, "ukv", 0))
                s = view((*L, "ukv", 0))
                for h in range(MLA_HEADS):
                    product((st, "kn", h), [(s[:, k, h * 256:h * 256 + P], hT[:, 3 + k, :]) for k in range(2)], S)
                for t in range(NT):
                    product((st, "vm", t), [(hT[:, 3 + k, t * P:(t + 1) * P],
                                             Split(*(a[:, k, :].rearrange("p (h e) -> p h e", h=4)[:, :, P:256]
                                                     for a in (s.high, s.low)))) for k in range(2)], 512)
                chunk_end[(*L, "ukv", 0)] = (st, "vm", 1)
                pe.wait_ge(rows_ready.sem, rows_ready.at((st, "rope")))
                to_columns((st, "peT"), lambda t, kt: xn[:, t, kt * P:(kt + 1) * P], 3)
                for b in range(2):
                    sig = (act_read, dve_read)[b % 2]
                    pe.wait_ge(sig.sem, sig.at(((st, "peT"), b)))
                pe.wait_ge(dve_read.sem, dve_read.at((st, "vm", 1)))
                pe.wait_ge(act_read.sem, act_read.at((st, "kn", 3)))
                attention(("mla", l))
                output_columns(("mla", l), 4)
                wide_gemm("mla", [(*L, "mla", h) for h in range(2)], (st, "ymla"), oT)
                pe.wait_ge(rows_ready.sem, rows_ready.at((st, "merged")))
                to_columns((st, "mT"), lambda t, kt: merged[:, t, kt * P:(kt + 1) * P], KD)
                pe.wait_ge(dve_read.sem, dve_read.at(((st, "mT"), 3)))
                for c in range(2):
                    rows_gemm([(*L, "out", c, h) for h in range(2)], (st, "y", c), oT)

            def memory(st):
                L = ("l2", st[1])
                norm((st, "norm"))
                columns_gemm([(*L, "xq", h) for h in range(2)], (st, "xq"), hT)
                norm((st, "mem"))
                columns_gemm([(*L, "xk", h) for h in range(2)], (st, "xk"), oT)
                rows_gemm([(*L, "xv", h) for h in range(2)], (st, "xv"), oT)
                pe.wait_ge(act_read.sem, act_read.at(((st, "xk"), 2)))
                pe.wait_ge(dve_read.sem, dve_read.at(((st, "xk"), 3)))
                pe.wait_ge(dve_read.sem, dve_read.at(((st, "xv"), 1)))
                pe.wait_ge(act_read.sem, act_read.at(((st, "xv"), 0)))
                attention(st)
                output_columns(st, 4)
                wide_gemm("xo", [(*L, "xo", h) for h in range(2)], (st, "y"), oT)

            pe.wait_ge(consts_loaded.sem, consts_loaded.at("c"))
            pe.wait_ge(pool_step.sem, pool_step.at("ident"))
            for n, r in enumerate(gain_tiles):
                bank = TB.take(pe, ("gains", n))
                nc.tensor.transpose(bank[:, 0:r], gains[0:r, n, :], ident[0:r, 0:r]) \
                    .then_inc(transposed.sem, transposed.next(("gains", n)))
            bank = TB.take(pe, ("gains", 3))
            for l in range(DEPTH2):
                ins = nc.tensor.transpose(bank[:, l * P:l * P + TAPS * CT], convw[0:TAPS * CT, l, :],
                                          ident[0:TAPS * CT, 0:TAPS * CT])
            ins.then_inc(transposed.sem, transposed.next(("gains", 3)))
            pe.wait_ge(dve_step.sem, dve_step.at("onehot"))
            product("line", [(bias2[:, :], onehot[:, :])], 3 * P, rows=NSA_HEADS)
            for st in stages:
                {"ff1": ffn, "ff2": ffn, "ff3": ffn, "mix": mixer, "l2": branches, "xattn": memory}[st[0]](st)

        @block.scalar
        def _(act):

            def copy(o, i, scale=1.0):
                return nc.scalar.activation(o, i, ACT.Copy, scale=scale)


            def row_gain(n):
                if n >= 2:
                    act.wait_ge(dve_read.sem, dve_read.at(("gain", row_gains[n - 2][0])))
                if n < len(row_gains):
                    key, src = row_gains[n]
                    act.dma_start(gain_row[n % 2][:, :], src.rearrange("(a n) -> a n", a=1).broadcast_to([P, D])) \
                        .then_inc(gain_loaded[n % 2].sem, gain_loaded[n % 2].next(key))

            split_to = [0]

            def ahead(key):
                while split_to[0] <= min(chunk_index[key] + AHEAD, last_chunk):
                    n = split_to[0]
                    split_to[0] += 1
                    if whole[n]:
                        continue
                    act.wait_ge(slot_loaded[n % SLOTS].sem, slot_loaded[n % SLOTS].at(chunks[n][0]))
                    m = users(n)
                    if m is not None:
                        act.wait_ge(matmul_done.sem, matmul_done.at(chunk_end.get(chunks[m][0])))
                    i = split_no[n] % SLOTS
                    nc.scalar.activation(high[i][:, 0:filled(n)], slots[n % SLOTS][:, 0:filled(n)], ACT.Copy) \
                        .then_inc(high_ready.sem, high_ready.next(n))

            def squares_free():
                if squared.count:
                    act.wait_ge(squared.sem, squared.count)

            def norm(n, src, ready):
                for t in range(NT):
                    sig, event = ready(t)
                    act.wait_ge(sig.sem, sig.at(event))
                    squares_free()
                    nc.scalar.activation(xn[:, t, :], src[:, t, :], ACT.Square, accum_out=ssum[:, 4 + t:5 + t]) \
                        .then_inc(squared.sem, squared.next((n, t)))

            def columns(n, gain, dst, nk=KD):
                for b in range((nk + 1) // 2):
                    act.wait_ge(transposed.sem, transposed.at((n, b)))
                    bank = TB.of((n, b))
                    for kt in range(2 * b, min(2 * b + 2, nk)):
                        ins = copy(dst(kt).high, bank[:, (kt % 2) * S:(kt % 2 + 1) * S], gain(kt) if gain else 1.0)
                    ins.then_inc(act_step.sem, act_step.next((n, b)))

            def prev_ready(st, t):
                n = stages.index(st)
                return (x_ready, (stages[n - 1], t)) if n else (consts_loaded, "c")

            def pre(st, key):
                norm((st, "norm"), x, lambda t: prev_ready(st, t))
                n = stages.index(st)
                if n and stages[n - 1] in gain_for:
                    row_gain(gain_n[gain_for[stages[n - 1]]] + 2)
                columns((st, "norm"), lambda k: gcol(key, k), lambda k: hT[:, k, :])

            def post(st, banks):
                for t in range(NT):
                    for h in range(2):
                        bank, done = banks(t, h)
                        act.wait_ge(matmul_done.sem, matmul_done.at(done))
                        squares_free()
                        nc.scalar.activation(xn[:, 0, 0:512], bank[:, :], ACT.Square, accum_out=ssum[:, 2 * t + h:2 * t + h + 1]) \
                            .then_inc(squared.sem, squared.next((st, t, h)))

            def ffn(st, key):
                pre(st, key)
                for i in range(KF):
                    ahead((st, "gate" if i % 2 == 0 else "up", i // 2, 0))
                    act.wait_ge(matmul_done.sem, matmul_done.at((st, "h", i)))
                    if i >= 2:
                        act.wait_ge(dve_read.sem, dve_read.at((st, "h", i - 2)))
                    nc.scalar.activation(silu[:, i % 2, :], G.of((st, "h", i))[:, 0:S], ACT.Silu) \
                        .then_inc(act_step.sem, act_step.next((st, "h", i)))
                    if i:
                        hidden_high(st, i - 1)
                hidden_high(st, KF - 1)
                for m in range(KF // 2):
                    ahead((st, "out", m))
                if st[0] != "ff3":
                    post(st, lambda t, h: (G.of(((st, "y"), t, h)), ((st, "y"), "chunk", (st, "out", KF // 2 - 1))))

            def hidden_high(st, i):
                act.wait_ge(dve_read.sem, dve_read.at((st, "h", i)))
                copy(hidT.high[:, i, :], hid_f[:, i % 3, :]).then_inc(act_step.sem, act_step.next((st, "hh", i)))

            def attention(st):
                units = units_of(st)
                for i in range(len(units) + 1):
                    if i < len(units):
                        u = units[i]
                        act.wait_ge(maxed.sem, maxed.at((st, i)))
                        if i >= 3:
                            act.wait_ge(transposed.sem, transposed.at((st, "p", i - 3)))
                        nc.scalar.activation(pr[:, i % 3, 0:u["kn"]], sc[:, i % 3, 0:u["kn"]], ACT.Exp, bias=nmax[:, i % 3:i % 3 + 1],
                                             accum_out=sums[:, u["t"], u["col"]:u["col"] + 1]) \
                            .then_inc(weighed.sem, weighed.next((st, i)))
                    if i >= 1:
                        u = units[i - 1]
                        act.wait_ge(transposed.sem, transposed.at((st, "p", i - 1)))
                        if i >= 3:
                            act.wait_ge(matmul_done.sem, matmul_done.at((st, "pv", i - 3)))
                        n, width = u["blocks"][0][1], P * len(u["blocks"])
                        copy(prT[0:n, (i - 1) % 2, 0:width], TB.of((st, "p", i - 1))[0:n, 0:width]) \
                            .then_inc(act_read.sem, act_read.next((st, "p", i - 1)))

            def mixer(st):
                i = st[1]
                if i % 3 == 0:
                    sig, event = prev_ready(st, NT - 1)
                    act.wait_ge(sig.sem, sig.at(event))
                    act.wait_ge(lines_stored.sem, lines_stored.at("l"))
                    act.dma_start(relA, bass.AP(tensor=line_dram[i // 3].tensor, offset=0,
                                                ap=[[1, P], [3 * P, HEADS_A], [1, TW]])) \
                        .then_inc(table_loaded.sem, table_loaded.next(st))
                if i % 3 == 1:
                    sig, event = prev_ready(st, NT - 1)
                    act.wait_ge(sig.sem, sig.at(event))
                    act.dma_start(ws, w["b_w_s"][0].rearrange("g t s -> t g s")) \
                        .then_inc(spatial_loaded.sem, spatial_loaded.next("ws"))
                pre(st, ("g", i, 2))
                if i % 3 == 1:
                    for c in range(4):
                        for t in range(NT):
                            ahead((st, "in", c, t))
                            act.wait_ge(matmul_done.sem, matmul_done.at(((st, "in", c), t)))
                            dst = (u_rows if c < 2 else g_rows)[:, t, (c % 2) * 512:(c % 2) * 512 + 512]
                            nc.scalar.activation(dst, G.of(((st, "in", c), t))[:, :], ACT.Gelu) \
                                .then_inc(act_read.sem, act_read.next(((st, "in", c), t)))
                    for b in (0, 2):
                        act.wait_ge(transposed.sem, transposed.at(((st, "ws"), b)))
                        for kt in (2 * b, 2 * b + 1):
                            ins = copy(wsT[:, kt, :], TB.of(((st, "ws"), b))[:, (kt % 2) * S:(kt % 2) * S + P])
                        ins.then_inc(act_read.sem, act_read.next(((st, "ws"), b)))
                    row_gain(gain_n["ln_g"] + 2)
                    row_gain(gain_n["ln_b"] + 2)
                else:
                    for c in range(4):
                        for j in (0, 2):
                            ahead((st, "in", c, j // 2))
                            act.wait_ge(matmul_done.sem, matmul_done.at(((st, "qk", c), j)))
                            copy(qkT[:, 4 * c + j, :], G.of(((st, "qk", c), j))[:, 0:S]).then_inc(act_read.sem, act_read.next(((st, "qk", c), j)))
                    for c in range(2):
                        for h in range(2):
                            ahead((st, "in", 4 + c, h))
                        act.wait_ge(matmul_done.sem, matmul_done.at(((st, "v", c), 0)))
                        copy(v_rows[:, 0, c * 512:(c + 1) * 512], G.of(((st, "v", c), 0))[:, :]) \
                            .then_inc(act_read.sem, act_read.next(((st, "v", c), 0)))
                    attention(st)
                columns((st, "oT"), None, lambda k: oT[:, k, :])
                for c in range(2):
                    for h in range(2):
                        ahead((st, "out", c, h))
                post(st, lambda t, h: (G.of(((st, "y", h), t)), ((st, "y", h), t)))

            def branches(st):
                l = st[1]
                L = ("l2", l)
                sig, event = prev_ready(st, NT - 1)
                act.wait_ge(sig.sem, sig.at(event))
                act.dma_start(relN, bass.AP(tensor=line_dram[2].tensor, offset=0, ap=[[1, P], [3 * P, NSA_HEADS], [1, TW]])) \
                    .then_inc(table_loaded.sem, table_loaded.next(st))
                src = w["cmp_w2_k_2"][l].rearrange("(f p) d -> p f d", p=P)
                for dst, src in ((w2k[:, :, 0, :], src), (w2k[:, :, 1, :], src),
                                 (w2v, w["cmp_w2_v_2"][l].rearrange("(f p) d -> p f d", p=P))):
                    act.dma_start(dst, src).then_inc(small_loaded.sem, small_loaded.next(st))
                pre(st, ("norm_mix_2", l))
                for j in (0, 2):
                    ahead((*L, "glu", 0, j // 2))
                    act.wait_ge(matmul_done.sem, matmul_done.at(((st, "glu", 0), j)))
                    copy(aT[:, j, :], G.of(((st, "glu", 0), j))[:, 0:S]).then_inc(act_read.sem, act_read.next(((st, "glu", 0), j)))
                for j in range(4):
                    ahead((*L, "glu", 1, j // 2))
                    act.wait_ge(matmul_done.sem, matmul_done.at(((st, "glu", 1), j)))
                    nc.scalar.activation(bT[:, j, :], G.of(((st, "glu", 1), j))[:, 0:S], ACT.Sigmoid) \
                        .then_inc(act_read.sem, act_read.next(((st, "glu", 1), j)))
                for j in (0, 2):
                    ahead((*L, "q", j // 2))
                    act.wait_ge(matmul_done.sem, matmul_done.at(((st, "q"), j)))
                    copy(qsT[:, j, :], G.of(((st, "q"), j))[:, 0:S]).then_inc(act_read.sem, act_read.next(((st, "q"), j)))
                for h, name, dst in ((0, ("tok", 0), tokT[:, 0, :]), (1, "kslc", kslcT), (2, "kwin", kwinT)):
                    ahead((*L, "kv", h))
                    act.wait_ge(matmul_done.sem, matmul_done.at((st, name)))
                    copy(dst, G.of((st, name))[:, 0:S]).then_inc(act_read.sem, act_read.next((st, name)))
                for v in range(2):
                    sig = (act_read, dve_read)[v]
                    act.wait_ge(sig.sem, sig.at((st, ("tok", v))))
                    for g in range(2):
                        for nxt in range(2):
                            act.dma_start(tok2[nxt * DH:(nxt + 1) * DH, v, g, 0:S - nxt], tokT[g * DH:(g + 1) * DH, v, nxt:S]) \
                                .then_inc(tok_loaded.sem, tok_loaded.next(st))
                for h in range(3):
                    ahead((*L, "rest", h))
                for t in range(NT):
                    act.wait_ge(dve_read.sem, dve_read.at(((st, "rest", 0), t)))
                gates = rest[:, :, R_GATE:R_GATE + 24]
                nc.scalar.activation(gates, gates, ACT.Sigmoid).then_inc(act_step.sem, act_step.next((st, "gates")))
                for v in range(2):
                    for f in range(2):
                        act.wait_ge(matmul_done.sem, matmul_done.at((st, "hid", v, f)))
                        nc.scalar.activation(hid_c[:, v, f, :], G.of((st, "hid", v, f))[:, 0:30], ACT.Gelu_apprx_tanh,
                                                  bias=gcol((("cmp_b1_k_2", "cmp_b1_v_2")[v], l), f)) \
                            .then_inc(act_read.sem, act_read.next((st, "hid", v, f)))
                for v in range(2):
                    for h in range(2):
                        ahead((*L, "cmp", v, h))
                for c in range(4):
                    for t in range(NT):
                        ahead((*L, "merge", c, t))
                        act.wait_ge(matmul_done.sem, matmul_done.at(((st, "merge", c), t)))
                        nc.scalar.activation(merge_gate[:, t, c * 512:(c + 1) * 512], G.of(((st, "merge", c), t))[:, :], ACT.Sigmoid) \
                            .then_inc(act_read.sem, act_read.next(((st, "merge", c), t)))
                for b in range(2):
                    act.wait_ge(transposed.sem, transposed.at(((st, "convT"), b)))
                    bank = TB.of(((st, "convT"), b))
                    for kt in (2 * b, 2 * b + 1):
                        ins = nc.scalar.activation(convT[:, kt, :], bank[:, (kt % 2) * S:(kt % 2 + 1) * S], ACT.Silu,
                                                   scale=gcol(("conv_ln_g_2", l), kt), bias=gcol(("conv_ln_b_2", l), kt))
                    ins.then_inc(act_read.sem, act_read.next(((st, "convT"), b)))
                    act.wait_ge(act_read.sem, act_read.at(((st, "convT"), b)))
                    copy(oT.high[:, 2 * b:2 * b + 2, :], convT[:, 2 * b:2 * b + 2, :]) \
                        .then_inc(act_step.sem, act_step.next(((st, "convT"), b)))
                for h in range(2):
                    ahead((*L, "conv", h))
                attention(st)
                columns((st, "oT"), None, lambda k: oT[:, k, :], 4)
                for h in range(2):
                    ahead((*L, "nsa", h))
                for c in range(4, 6):
                    for t in range(NT):
                        ahead((*L, "merge", c, t))
                        act.wait_ge(matmul_done.sem, matmul_done.at(((st, "merge", c), t)))
                        act.wait_ge(dve_read.sem, dve_read.at(((st, "ynsa"), 1, 1)))
                        nc.scalar.activation(merge_gate[:, t, (c - 2) * 512:(c - 1) * 512], G.of(((st, "merge", c), t))[:, :],
                                             ACT.Sigmoid).then_inc(act_read.sem, act_read.next(((st, "merge", c), t)))
                for t in range(NT):
                    act.wait_ge(dve_read.sem, dve_read.at(((st, "rest", 1), t)))
                    for n, (c0, c1) in enumerate(((R_CQ, R_CKV), (R_CKV, R_KPE))):
                        squares_free()
                        nc.scalar.activation(xn[:, 1, 512:512 + c1 - c0], rest[:, t, c0:c1], ACT.Square,
                                             accum_out=ssum[:, 2 * n + t:2 * n + t + 1]) \
                            .then_inc(squared.sem, squared.next((st, "latent", n, t)))
                columns((st, "latT"), lambda k: gcol(("mla_norm_q_2", l), k) if k < 3 else gcol(("mla_norm_kv_2", l), k - 3),
                        lambda k: hT[:, k, :], 5)
                for h in range(MLA_HEADS):
                    ahead((*L, "uq", h // 2))
                    act.wait_ge(matmul_done.sem, matmul_done.at((st, "qn", h)))
                    copy(qnT[:, h, :], G.of((st, "qn", h))[:, 0:S]).then_inc(act_read.sem, act_read.next((st, "qn", h)))
                ahead((*L, "ukv", 0))
                for h in range(MLA_HEADS):
                    act.wait_ge(matmul_done.sem, matmul_done.at((st, "kn", h)))
                    copy(knT[:, h, :], G.of((st, "kn", h))[:, 0:S]).then_inc(act_read.sem, act_read.next((st, "kn", h)))
                act.wait_ge(transposed.sem, transposed.at(((st, "peT"), 0)))
                copy(qpT[:, :, :].rearrange("p h s -> p (h s)"), TB.of(((st, "peT"), 0))[:, :]) \
                    .then_inc(act_read.sem, act_read.next(((st, "peT"), 0)))
                attention(("mla", l))
                columns((("mla", l), "oT"), None, lambda k: oT[:, k, :], 4)
                for h in range(2):
                    ahead((*L, "mla", h))
                columns((st, "mT"), None, lambda k: oT[:, k, :])
                for c in range(2):
                    for h in range(2):
                        ahead((*L, "out", c, h))

            def memory(st):
                l = st[1]
                L = ("l2", l)
                sig, event = prev_ready(st, NT - 1)
                act.wait_ge(sig.sem, sig.at(event))
                act.dma_start(mem[:, :, :], w["mem_2"][0].rearrange("(t p) d -> p t d", p=P)) \
                    .then_inc(mem_loaded.sem, mem_loaded.next(st))
                pre(st, ("norm_xattn_2", l))
                act.wait_ge(transposed.sem, transposed.at(((st, "norm"), 3)))
                norm((st, "mem"), mem, lambda t: (mem_loaded, st))
                for j in (0, 2):
                    ahead((*L, "xq", j // 2))
                    act.wait_ge(matmul_done.sem, matmul_done.at(((st, "xq"), j)))
                    copy(xqT[:, j, :], G.of(((st, "xq"), j))[:, 0:S]).then_inc(act_read.sem, act_read.next(((st, "xq"), j)))
                columns((st, "mem"), lambda k: gcol(("norm_mem_2", l), k), lambda k: oT[:, k, :])
                for j in (0, 2):
                    ahead((*L, "xk", j // 2))
                    act.wait_ge(matmul_done.sem, matmul_done.at(((st, "xk"), j)))
                    copy(xkT[:, j, :], G.of(((st, "xk"), j))[:, 0:S]).then_inc(act_read.sem, act_read.next(((st, "xk"), j)))
                for h in range(2):
                    ahead((*L, "xv", h))
                act.wait_ge(matmul_done.sem, matmul_done.at(((st, "xv"), 0)))
                copy(xv[:, 0, :], G.of(((st, "xv"), 0))[:, :]).then_inc(act_read.sem, act_read.next(((st, "xv"), 0)))
                attention(st)
                columns((st, "oT"), None, lambda k: oT[:, k, :], 4)
                for h in range(2):
                    ahead((*L, "xo", h))

            row_gain(0)
            row_gain(1)
            for n in (0, 2):
                r = gain_tiles[n]
                act.wait_ge(transposed.sem, transposed.at(("gains", n)))
                copy(gT[:, n, 0:r], TB.of(("gains", n))[:, 0:r]).then_inc(act_read.sem, act_read.next(("gains", n)))
            act.wait_ge(dve_step.sem, dve_step.at("lambda"))
            nc.scalar.activation(lam[:, 2:4], lam[:, 0:2], ACT.Exp).then_inc(act_step.sem, act_step.next("lambda"))
            act.wait_ge(dve_step.sem, dve_step.at("angles"))
            nc.scalar.activation(sinb[:, :, :], sinb[:, :, :], ACT.Sin).then_inc(act_step.sem, act_step.next("sin"))
            nc.scalar.activation(cosb[:, :, :], cosb[:, :, :], ACT.Sin).then_inc(act_step.sem, act_step.next("cos"))
            ahead(chunks[0][0])
            for st in stages:
                i = st[1]
                if st[0] == "ff1":
                    ffn(st, ("g", i, 0))
                elif st[0] == "ff2":
                    ffn(st, ("g", i, 4))
                elif st[0] == "ff3":
                    ffn(st, ("norm_ffn_2", i))
                else:
                    {"mix": mixer, "l2": branches, "xattn": memory}[st[0]](st)
            if last == ("ff3", DEPTH2 - 1):
                norm("final", x, lambda t: (x_ready, (last, t)))

        @block.gpsimd
        def _(pool):

            def step(ins, key=None):
                settle(pool, ins, pool_step, key)

            def power(key, c0, n):
                pool.wait_ge(mean_ready.sem, mean_ready.at(key))
                pool.tensor_tensor(rstd[:, c0:c0 + n], mean_sq[:, c0:c0 + n], minus_half[:, 0:n], ALU.pow) \
                    .then_inc(rstd_ready.sem, rstd_ready.next(key))

            step(pool.memset(ident[:, :], 0.0))
            step(pool.affine_select(out=ident[:, :], in_=ident[:, :], compare_op=ALU.not_equal, fill=1.0, base=0,
                                    pattern=[[-1, P]], channel_multiplier=1), "ident")
            step(pool.memset(minus_half[:, :], -0.5))
            step(pool.iota(tmp2[0:BUCKETS, 0:16], pattern=[[1, 16]], base=0, channel_multiplier=0,
                           allow_small_or_imprecise_dtypes=True), "exact")
            step(pool.iota(tmp2[0:BUCKETS, 16:17], pattern=[[0, 1]], base=0, channel_multiplier=1,
                           allow_small_or_imprecise_dtypes=True), "bucket")
            for i in range(ROPE // 2):
                ins = pool.memset(freq[:, i:i + 1], ROPE_THETA ** (-i / (ROPE // 2)))
            step(ins, "freq")
            step(pool.memset(valid[:, :], 1.0))
            step(pool.affine_select(out=valid[:, 0:1], in_=valid[:, 0:1], compare_op=ALU.is_ge, fill=0.0,
                                    base=-(CMP_BLOCK - 1), pattern=[[0, 1]], channel_multiplier=1), "valid")
            for st in stages:
                kind, i = st
                power((st, "norm"), 2, 2)
                if kind == "mix" and i % 3 == 1:
                    pool.wait_ge(spatial_loaded.sem, spatial_loaded.at("ws"))
                    step(pool.affine_select(out=ws, in_=ws, compare_op=ALU.is_ge, fill=0.0, base=0,
                                            pattern=[[0, GROUPS_B], [-1, P]], channel_multiplier=1), "spatial")
                    power((st, "ln"), 4, 2)
                if kind == "mix" and i % 3 == 2:
                    for h in range(HEADS_C):
                        ins = pool.iota(relC[:, h, :], pattern=[[1, TW]], base=-P, channel_multiplier=1,
                                        allow_small_or_imprecise_dtypes=True)
                    step(ins, "distances")
                    power((st, "subln"), 0, 16)
                if kind == "l2":
                    step(pool.memset(causal, 0.0))
                    step(pool.affine_select(out=causal, in_=causal, compare_op=ALU.is_ge, fill=NEG, base=-P,
                                            pattern=[[1, TW]], channel_multiplier=1))
                    pool.wait_ge(table_loaded.sem, table_loaded.at(st))
                    step(pool.affine_select(out=relN, in_=relN, compare_op=ALU.is_ge, fill=NEG, base=-P,
                                            pattern=[[0, NSA_HEADS], [1, TW]], channel_multiplier=1), ("relN", i))
                    power((st, "conv"), 4, 2)
                    power((st, "latent"), 4, 4)
                if kind == "xattn":
                    step(pool.memset(zeros, 0.0), ("zeros", i))
                    power((st, "mem"), 2, 2)
                if st in gain_for:
                    power((st, "post"), 0, 2)
            if last == ("ff3", DEPTH2 - 1):
                power("final", 2, 2)

        @block.vector
        def _(dve):
            V = nc.vector


            def step(ins, key=None):
                settle(dve, ins, dve_step, key)


            split_to = [0]

            def ahead(key):
                while split_to[0] <= min(chunk_index[key] + AHEAD, last_chunk):
                    n = split_to[0]
                    split_to[0] += 1
                    if whole[n]:
                        continue
                    dve.wait_ge(high_ready.sem, high_ready.at(n))
                    i, size = split_no[n] % SLOTS, filled(n)
                    V.tensor_tensor(low[i][:, 0:size], slots[n % SLOTS][:, 0:size], high[i][:, 0:size].bitcast(F32), ALU.subtract) \
                        .then_inc(low_ready.sem, low_ready.next(n))

            def tick(sig, key):
                dve.sem_inc(sig.sem, sig.next(key))

            def mean(key, c0, n, src, count):
                V.tensor_scalar(mean_sq[:, c0:c0 + n], src, 1.0 / count, EPS, ALU.mult, ALU.add) \
                    .then_inc(mean_ready.sem, mean_ready.next(key))

            def norm(n, src):
                dve.wait_ge(squared.sem, squared.at((n, 1)))
                mean(n, 2, 2, ssum[:, 4:6], D)
                dve.wait_ge(rstd_ready.sem, rstd_ready.at(n))
                for t in range(NT):
                    V.tensor_scalar(xn[:, t, :], src[:, t, :], rstd[:, 2 + t:3 + t], None, ALU.mult) \
                        .then_inc(rows_ready.sem, rows_ready.next((n, t)))

            def columns(n, gain, dst, nk=KD):
                for b in range((nk + 1) // 2):
                    dve.wait_ge(act_step.sem, act_step.at((n, b)))
                    bank = TB.of((n, b))
                    for kt in range(2 * b, min(2 * b + 2, nk)):
                        src = bank[:, (kt % 2) * S:(kt % 2 + 1) * S]
                        d = dst(kt)
                        if gain:
                            ins = V.scalar_tensor_tensor(d.low, src, gain(kt), d.high.bitcast(F32), ALU.mult, ALU.subtract)
                        else:
                            ins = V.tensor_tensor(d.low, src, d.high.bitcast(F32), ALU.subtract)
                    ins.then_inc(dve_read.sem, dve_read.next((n, b)))

            def pre(st, key):
                norm((st, "norm"), x)
                columns((st, "norm"), lambda k: gcol(key, k), lambda k: hT[:, k, :])

            def post(st, banks, factor):
                dve.wait_ge(squared.sem, squared.at((st, 1, 1)))
                step(V.tensor_tensor(mean_sq[:, 0:2], ssum[:, 0:4:2], ssum[:, 1:4:2], ALU.add))
                mean((st, "post"), 0, 2, mean_sq[:, 0:2], D)
                dve.wait_ge(rstd_ready.sem, rstd_ready.at((st, "post")))
                if factor != 1.0:
                    step(V.tensor_scalar(rstd[:, 0:2], rstd[:, 0:2], factor, None, ALU.mult))
                gkey = gain_for[st]
                n = gain_n[gkey]
                dve.wait_ge(gain_loaded[n % 2].sem, gain_loaded[n % 2].at(gkey))
                for t in range(NT):
                    for h in range(2):
                        bank, key = banks(t, h)
                        ins = V.scalar_tensor_tensor(tmp[:, :], bank[:, :], rstd[:, t:t + 1],
                                                     gain_row[n % 2][:, h * 512:(h + 1) * 512], ALU.mult, ALU.mult)
                        ins.then_inc(dve_read.sem, dve_read.next(key))
                        dve.wait_ge(dve_read.sem, dve_read.at(key))
                        xs = x[:, t, h * 512:(h + 1) * 512]
                        ins = V.tensor_tensor(xs, xs, tmp[:, :], ALU.add)
                        if h == 0:
                            step(ins)
                        else:
                            settle(dve, ins, x_ready, (st, t))
                tick(dve_read, ("gain", gkey))

            def add_to_x(st, banks):
                for t in range(NT):
                    for h in range(2):
                        bank, key, done = banks(t, h)
                        dve.wait_ge(matmul_done.sem, matmul_done.at(done))
                        xs = x[:, t, h * 512:(h + 1) * 512]
                        settle(dve, V.tensor_tensor(xs, xs, bank[:, :], ALU.add), dve_read, key)
                    tick(x_ready, (st, t))

            def ffn(st, key):
                pre(st, key)
                for i in range(KF):
                    ahead((st, "gate" if i % 2 == 0 else "up", i // 2, 0))
                    if i >= 3:
                        dve.wait_ge(act_step.sem, act_step.at((st, "hh", i - 3)))
                        dve.wait_ge(dve_step.sem, dve_step.at((st, "h", i - 3)))
                    dve.wait_ge(act_step.sem, act_step.at((st, "h", i)))
                    V.tensor_tensor(hid_f[:, i % 3, :], silu[:, i % 2, :], G.of((st, "h", i))[:, S:2 * S], ALU.mult) \
                        .then_inc(dve_read.sem, dve_read.next((st, "h", i)))
                    if i:
                        hidden_low(st, i - 1)
                hidden_low(st, KF - 1)
                for m in range(KF // 2):
                    ahead((st, "out", m))
                k = (st, "y")
                if st[0] == "ff3":
                    add_to_x(st, lambda t, h: (G.of((k, t, h)), (k, t, h), (k, "chunk", (st, "out", KF // 2 - 1))))
                else:
                    post(st, lambda t, h: (G.of((k, t, h)), (k, t, h)), 0.5)

            def hidden_low(st, i):
                dve.wait_ge(act_step.sem, act_step.at((st, "hh", i)))
                V.tensor_tensor(hidT.low[:, i, :], hid_f[:, i % 3, :], hidT.high[:, i, :].bitcast(F32), ALU.subtract) \
                    .then_inc(dve_step.sem, dve_step.next((st, "h", i)))

            def attention(st, evacuate):
                units = units_of(st)
                for i in range(len(units) + 3):
                    if i < len(units):
                        u = units[i]
                        kn = u["kn"]
                        dve.wait_ge(scored.sem, scored.at((st, i)))
                        if i >= 3:
                            dve.wait_ge(weighed.sem, weighed.at((st, i - 3)))
                        settle(dve, V.scalar_tensor_tensor(sc[:, i % 3, 0:kn], SB.of((st, "s", i))[:, 0:kn], u["scale"], u["bias"],
                                                           ALU.mult, ALU.add), dve_read, (st, "s", i))
                        V.tensor_reduce(nmax[:, i % 3:i % 3 + 1], sc[:, i % 3, 0:kn], AX.X, ALU.max, negate=True) \
                            .then_inc(maxed.sem, maxed.next((st, i)))
                    if i >= 3 and units[i - 3]["last"]:
                        u = units[i - 3]
                        dve.wait_ge(matmul_done.sem, matmul_done.at((st, "pv", i - 3)))
                        evacuate(u["acc"], G.of(u["acc"]))

            def heads(bank, n):
                return bank[:, :].rearrange("p (h d) -> p h d", h=n)

            def spread(a, width):
                return a.unsqueeze(2).broadcast_to([a.shape[0], a.shape[1], width])

            def even(st, n, c0):
                def f(acc, bank):
                    _, _, t, b = acc
                    cols = slice(c0 + b * n, c0 + (b + 1) * n)
                    step(V.reciprocal(inv[:, t, cols], sums[:, t, cols]))
                    o = o_rows[:, t, b * 512:(b + 1) * 512].rearrange("p (h d) -> p h d", h=n)
                    settle(dve, V.tensor_tensor(o, heads(bank, n), spread(inv[:, t, cols], 512 // n), ALU.mult), dve_read, acc)
                    if b == (1 if st[0] == "mix" else 0):
                        tick(rows_ready, (st, "o", t))
                return f

            def differential(st):
                def f(acc, bank):
                    _, _, t, b = acc
                    cols = inv[:, t, 4 * b:4 * b + 4]
                    step(V.reciprocal(cols, sums[:, t, 4 * b:4 * b + 4]))
                    step(V.tensor_scalar(cols[:, 1:4:2], cols[:, 1:4:2], lam[:, 6:7], None, ALU.mult))
                    both = bank[:, :].rearrange("p (h m d) -> p h m d", h=2, m=2)
                    o = o_rows[:, t, b * 256:(b + 1) * 256].rearrange("p (h d) -> p h d", h=2)
                    t0 = tmp[:, 0:256].rearrange("p (h d) -> p h d", h=2)
                    t1 = tmp2[:, 0:256].rearrange("p (h d) -> p h d", h=2)
                    step(V.tensor_tensor(t0, both[:, :, 0, :], spread(cols[:, 0:4:2], P), ALU.mult))
                    settle(dve, V.tensor_tensor(t1, both[:, :, 1, :], spread(cols[:, 1:4:2], P), ALU.mult), dve_read, acc)
                    step(V.tensor_tensor(o, t0, t1, ALU.add))
                return f

            def sparse(st):
                def f(acc, bank):
                    _, _, t, br = acc
                    cols = inv[:, t, 8 * br:8 * br + 8]
                    step(V.reciprocal(cols, sums[:, t, 8 * br:8 * br + 8]))
                    if t == 0 and br == 0:
                        step(V.tensor_scalar(cols, cols, valid[:, 0:1], None, ALU.mult))
                    if br == 0:
                        dve.wait_ge(act_step.sem, act_step.at((st, "gates")))
                    step(V.tensor_tensor(cols, cols, rest[:, t, R_GATE + br:R_GATE + 24:3], ALU.mult))
                    o = o_rows[:, t, 0:512]
                    oh = o.rearrange("p (h d) -> p h d", h=8)
                    th = tmp[:, :].rearrange("p (h d) -> p h d", h=8)
                    settle(dve, V.tensor_tensor(oh if br == 0 else th, heads(bank, 8), spread(cols, DH), ALU.mult), dve_read, acc)
                    if br:
                        ins = V.tensor_tensor(o, o, tmp[:, :], ALU.add)
                        if br == 2:
                            settle(dve, ins, rows_ready, (st, "o", t))
                        else:
                            step(ins)
                return f

            def mixer(st):
                i = st[1]
                pre(st, ("g", i, 2))
                if i % 3 == 1:
                    for c in range(4):
                        for h in range(2):
                            ahead((st, "in", c, h))
                    for b in (1, 3):
                        dve.wait_ge(transposed.sem, transposed.at(((st, "ws"), b)))
                        for kt in (2 * b, 2 * b + 1):
                            ins = V.tensor_copy(wsT[:, kt, :], TB.of(((st, "ws"), b))[:, (kt % 2) * S:(kt % 2) * S + P])
                        ins.then_inc(dve_read.sem, dve_read.next(((st, "ws"), b)))
                    for t in range(NT):
                        dve.wait_ge(act_read.sem, act_read.at(((st, "in", 3), 1)))
                        for h in range(2):
                            step(V.bn_stats(stats[:, h, :], g_rows[:, t, h * 512:(h + 1) * 512]))
                        step(V.bn_aggr(moments[:, t, :], stats[:, :, :]))
                    mean((st, "ln"), 4, 2, moments[:, :, 1], 1.0)
                    dve.wait_ge(rstd_ready.sem, rstd_ready.at((st, "ln")))
                    for key in ("ln_g", "ln_b"):
                        dve.wait_ge(gain_loaded[gain_n[key] % 2].sem, gain_loaded[gain_n[key] % 2].at(key))
                    for t in range(NT):
                        g = g_rows[:, t, :]
                        step(V.tensor_scalar(g, g, moments[:, t, 0:1], rstd[:, 4 + t:5 + t], ALU.subtract, ALU.mult))
                        ins = V.tensor_tensor(g, g, gain_row[gain_n["ln_g"] % 2][:, :], ALU.mult)
                        settle(dve, ins, dve_read, ("gain", "ln_g") if t == 1 else ("ln", t))
                        ins = V.tensor_tensor(g, g, gain_row[gain_n["ln_b"] % 2][:, :], ALU.add)
                        settle(dve, ins, rows_ready, (st, "v", t))
                    tick(dve_read, ("gain", "ln_b"))
                    for t in range(NT):
                        for h in range(2):
                            dve.wait_ge(matmul_done.sem, matmul_done.at((st, "sv", t, h)))
                            bank = G.of((st, "sv", t, h))
                            for g in range(4):
                                c = slice((4 * h + g) * P, (4 * h + g + 1) * P)
                                ins = V.scalar_tensor_tensor(o_rows[:, t, c], bank[:, g * P:(g + 1) * P], gcol("b_b_s", 4 * h + g),
                                                             u_rows[:, t, c], ALU.add, ALU.mult)
                            settle(dve, ins, dve_read, (st, "sv", t, h))
                        tick(rows_ready, (st, "o", t))
                else:
                    for c in range(4):
                        for j in (1, 3):
                            ahead((st, "in", c, j // 2))
                            dve.wait_ge(matmul_done.sem, matmul_done.at(((st, "qk", c), j)))
                            V.tensor_copy(qkT[:, 4 * c + j, :], G.of(((st, "qk", c), j))[:, 0:S]) \
                                .then_inc(dve_read.sem, dve_read.next(((st, "qk", c), j)))
                    for c in range(2):
                        for h in range(2):
                            ahead((st, "in", 4 + c, h))
                        dve.wait_ge(matmul_done.sem, matmul_done.at(((st, "v", c), 1)))
                        V.tensor_copy(v_rows[:, 1, c * 512:(c + 1) * 512], G.of(((st, "v", c), 1))[:, :]) \
                            .then_inc(dve_read.sem, dve_read.next(((st, "v", c), 1)))
                    if i % 3 == 0:
                        dve.wait_ge(table_loaded.sem, table_loaded.at(st))
                        step(V.memset(relA[0:CHUNK, :, 1:CHUNK + 1], NEG))
                    else:
                        dve.wait_ge(pool_step.sem, pool_step.at("distances"))
                        step(V.scalar_tensor_tensor(relC, relC, -1.0, relC, ALU.mult, ALU.max))
                        for h in range(HEADS_C):
                            step(V.tensor_scalar(relC[:, h, :], relC[:, h, :], -(2.0 ** (-8.0 * (h + 1) / HEADS_C)), None, ALU.mult))
                        step(V.memset(relC[0:CHUNK, :, 1:CHUNK + 1], NEG))
                    attention(st, even(st, 8, 0) if i % 3 == 0 else differential(st))
                    if i % 3 == 2:
                        o4 = o_rows[:, :, :].rearrange("p t (h d) -> p t h d", h=HEADS_C)
                        x4 = xn[:, :, :].rearrange("p t (h d) -> p t h d", h=HEADS_C)
                        for t in range(NT):
                            step(V.tensor_tensor(xn[:, t, :], o_rows[:, t, :], o_rows[:, t, :], ALU.mult))
                            step(V.tensor_reduce(mean_sq[:, 8 * t:8 * t + 8], x4[:, t, :, :], AX.X, ALU.add))
                        mean((st, "subln"), 0, 16, mean_sq[:, 0:16], P)
                        dve.wait_ge(rstd_ready.sem, rstd_ready.at((st, "subln")))
                        lambda_init = 0.8 - 0.6 * math.exp(-0.3 * i)
                        step(V.tensor_scalar(rstd[:, 0:16], rstd[:, 0:16], 1.0 - lambda_init, None, ALU.mult))
                        for t in range(NT):
                            step(V.tensor_tensor(o4[:, t, :, :], o4[:, t, :, :], spread(rstd[:, 8 * t:8 * t + 8], P), ALU.mult))
                            ins = V.tensor_tensor(o4[:, t, :, :], o4[:, t, :, :],
                                                  subln[:, :].unsqueeze(1).broadcast_to([P, HEADS_C, P]), ALU.mult)
                            ins.then_inc(rows_ready.sem, rows_ready.next((st, "o", t)))
                columns((st, "oT"), None, lambda k: oT[:, k, :])
                for c in range(2):
                    for h in range(2):
                        ahead((st, "out", c, h))
                post(st, lambda t, h: (G.of(((st, "y", h), t)), ((st, "y", h), t)), 1.0)

            def merge(st, name, n):
                k = (st, name)
                if n == 2:
                    dve.wait_ge(act_read.sem, act_read.at(((st, "merge", 5), 1)))
                for t in range(NT):
                    for h in range(2):
                        dve.wait_ge(matmul_done.sem, matmul_done.at((k, "chunk", ("l2", st[1], name[1:], 1))))
                        bank = G.of((k, t, h))
                        gate = merge_gate[:, t, min(n, 1) * D + h * 512:min(n, 1) * D + (h + 1) * 512]
                        m = merged[:, t, h * 512:(h + 1) * 512]
                        ins = V.tensor_tensor(m if n == 0 else tmp[:, :], bank[:, :], gate, ALU.mult)
                        settle(dve, ins, dve_read, (k, t, h))
                        if n:
                            ins = V.tensor_tensor(m, m, tmp[:, :], ALU.add)
                            if n == 2 and t == 1 and h == 1:
                                settle(dve, ins, rows_ready, (st, "merged"))
                            else:
                                step(ins)

            def branches(st):
                l = st[1]
                pre(st, ("norm_mix_2", l))
                L = ("l2", l)
                for j in (1, 3):
                    ahead((*L, "glu", 0, j // 2))
                    dve.wait_ge(matmul_done.sem, matmul_done.at(((st, "glu", 0), j)))
                    V.tensor_copy(aT[:, j, :], G.of(((st, "glu", 0), j))[:, 0:S]) \
                        .then_inc(dve_read.sem, dve_read.next(((st, "glu", 0), j)))
                for h in range(2):
                    ahead((*L, "glu", 1, h))
                for j in (1, 3):
                    ahead((*L, "q", j // 2))
                    dve.wait_ge(matmul_done.sem, matmul_done.at(((st, "q"), j)))
                    V.tensor_copy(qsT[:, j, :], G.of(((st, "q"), j))[:, 0:S]) \
                        .then_inc(dve_read.sem, dve_read.next(((st, "q"), j)))
                ahead((*L, "kv", 0))
                dve.wait_ge(matmul_done.sem, matmul_done.at((st, ("tok", 1))))
                V.tensor_copy(tokT[:, 1, :], G.of((st, ("tok", 1)))[:, 0:S]).then_inc(dve_read.sem, dve_read.next((st, ("tok", 1))))
                for h, name, dst in ((1, "vslc", vslc), (2, "vwin", vwin)):
                    ahead((*L, "kv", h))
                    for t in range(NT):
                        dve.wait_ge(matmul_done.sem, matmul_done.at(((st, name), t)))
                        V.tensor_copy(dst[:, t, :], G.of(((st, name), t))[:, 0:P]) \
                            .then_inc(dve_read.sem, dve_read.next(((st, name), t)))
                for n, (c0, c1) in enumerate(((0, 512), (512, N_REST))):
                    for h in ((0, 1), (2,))[n]:
                        ahead((*L, "rest", h))
                    for t in range(NT):
                        dve.wait_ge(matmul_done.sem, matmul_done.at(((st, "rest", n), t)))
                        V.tensor_copy(rest[:, t, c0:c1], G.of(((st, "rest", n), t))[:, 0:c1 - c0]) \
                            .then_inc(dve_read.sem, dve_read.next(((st, "rest", n), t)))
                dve.wait_ge(tok_loaded.sem, tok_loaded.at(st))
                for v in range(2):
                    for g in range(2):
                        for half in range(2):
                            src = tok2[:, v, g, half * CMP_STRIDE:half * CMP_STRIDE + N_CMP * CMP_STRIDE] \
                                .rearrange("p (c r) -> p r c", r=CMP_STRIDE)[:, 0:CMP_STRIDE:2, :]
                            t_, r = col[(("cmp_pos_k_2", "cmp_pos_v_2")[v], l)]
                            pos = gT[:, t_, r + 8 * half:r + 8 * half + 8].unsqueeze(2).broadcast_to([P, 8, N_CMP])
                            ins = V.tensor_tensor(blk[:, v, 8 * half:8 * half + 8, g, :], src, pos, ALU.add)
                    ins.then_inc(dve_read.sem, dve_read.next((st, "blk", v)))
                step(V.memset(glu[:, :, 0:TAPS - 1], 0.0))
                dve.wait_ge(act_read.sem, act_read.at(((st, "glu", 1), 3)))
                dve.wait_ge(dve_read.sem, dve_read.at(((st, "glu", 0), 3)))
                step(V.tensor_tensor(glu[:, :, TAPS - 1:TAPS - 1 + S], aT, bT, ALU.mult))
                for v in range(2):
                    for h in range(2):
                        ahead((*L, "cmp", v, h))
                for tap in range(TAPS):
                    if tap % 4 == 3:
                        ahead((*L, "merge", tap // 8, tap // 4 % 2))
                    for c in range(CT):
                        if tap:
                            dve.wait_ge(dve_step.sem, dve_step.count - CT + 1)
                        wt = convwT[:, l, tap * CT + c:tap * CT + c + 1]
                        src = glu[:, c, tap:tap + S]
                        if tap == 0:
                            ins = V.tensor_scalar(convT[:, c, :], src, wt, gcol(("conv_b_2", l), c), ALU.mult, ALU.add)
                        else:
                            ins = V.scalar_tensor_tensor(convT[:, c, :], src, wt, convT[:, c, :], ALU.mult, ALU.add)
                        ins.then_inc(dve_step.sem, dve_step.next((st, "conv")))
                dve.wait_ge(matmul_done.sem, matmul_done.at((st, "kc")))
                V.tensor_copy(kcT[:, 0:30], G.of((st, "kc"))[:, 0:30]).then_inc(dve_read.sem, dve_read.next((st, "kc")))
                for g in range(2):
                    dve.wait_ge(matmul_done.sem, matmul_done.at((st, "vc", g)))
                    V.tensor_copy(vc[0:N_CMP, g, :], G.of((st, "vc", g))[0:N_CMP, 0:DH]) \
                        .then_inc(dve_read.sem, dve_read.next((st, "vc", g)))
                for h in range(2):
                    ahead((*L, "merge", 3, h))
                for t in range(NT):
                    dve.wait_ge(transposed.sem, transposed.at((st, "conv_rows", t)))
                    step(V.bn_stats(stats[:, 0, :], TB.of((st, "conv_rows", t))[:, :]))
                    step(V.bn_aggr(moments[:, t, :], stats[:, 0, :]))
                mean((st, "conv"), 4, 2, moments[:, :, 1], 1.0)
                dve.wait_ge(rstd_ready.sem, rstd_ready.at((st, "conv")))
                for t in range(NT):
                    ins = V.tensor_scalar(xn[:, t, 0:CONV_CH], TB.of((st, "conv_rows", t))[:, :], moments[:, t, 0:1],
                                          rstd[:, 4 + t:5 + t], ALU.subtract, ALU.mult)
                    settle(dve, ins, dve_read, (st, "conv_rows", t))
                    tick(rows_ready, (st, "conv", t))
                for b in range(2):
                    dve.wait_ge(act_step.sem, act_step.at(((st, "convT"), b)))
                    d = oT[:, 2 * b:2 * b + 2, :]
                    V.tensor_tensor(d.low, convT[:, 2 * b:2 * b + 2, :], d.high.bitcast(F32), ALU.subtract) \
                        .then_inc(dve_read.sem, dve_read.next(((st, "convT"), b)))
                for h in range(2):
                    ahead((*L, "conv", h))
                dve.wait_ge(act_read.sem, act_read.at(((st, "merge", 3), 1)))
                merge(st, "yconv", 0)
                dve.wait_ge(pool_step.sem, pool_step.at(("relN", l)))
                attention(st, sparse(st))
                columns((st, "oT"), None, lambda k: oT[:, k, :], 4)
                for h in range(2):
                    ahead((*L, "nsa", h))
                merge(st, "ynsa", 1)
                for c in range(4, 6):
                    for h in range(2):
                        ahead((*L, "merge", c, h))
                for n, (c0, c1) in enumerate(((R_CQ, R_CKV), (R_CKV, R_KPE))):
                    dve.wait_ge(squared.sem, squared.at((st, "latent", 1, 1)))
                    ins = V.tensor_scalar(mean_sq[:, 4 + 2 * n:6 + 2 * n], ssum[:, 2 * n:2 * n + 2], 1.0 / (c1 - c0), EPS,
                                          ALU.mult, ALU.add)
                    if n:
                        ins.then_inc(mean_ready.sem, mean_ready.next((st, "latent")))
                    else:
                        step(ins)
                dve.wait_ge(rstd_ready.sem, rstd_ready.at((st, "latent")))
                for n, (c0, c1) in enumerate(((R_CQ, R_CKV), (R_CKV, R_KPE))):
                    for t in range(NT):
                        step(V.tensor_scalar(xn[:, t, c0 - R_CQ:c1 - R_CQ], rest[:, t, c0:c1],
                                             rstd[:, 4 + 2 * n + t:5 + 2 * n + t], None, ALU.mult))
                tick(rows_ready, (st, "latent"))
                columns((st, "latT"), lambda k: gcol(("mla_norm_q_2", l), k) if k < 3 else gcol(("mla_norm_kv_2", l), k - 3),
                        lambda k: hT[:, k, :], 5)
                def rotate(x1, x2, cos, sin, shape, outs, key):
                    r = [rtmp[:, n, 0:shape[0] * shape[1]].rearrange("p (h d) -> p h d", h=shape[0]) for n in range(4)]
                    step(V.tensor_tensor(r[0], x1, cos, ALU.mult))
                    step(V.tensor_tensor(r[1], x2, sin, ALU.mult))
                    step(V.tensor_tensor(r[2], x2, cos, ALU.mult))
                    ins = V.tensor_tensor(r[3], x1, sin, ALU.mult)
                    settle(dve, ins, dve_read, key)
                    for o1, o2 in outs:
                        step(V.tensor_tensor(o1, r[0], r[1], ALU.subtract))
                        step(V.tensor_tensor(o2, r[2], r[3], ALU.add))

                dve.wait_ge(act_step.sem, act_step.at("cos"))
                for h in range(2):
                    ahead((*L, "uq", h))
                    for t in range(NT):
                        dve.wait_ge(matmul_done.sem, matmul_done.at((st, "qp", h, t)))
                        q = G.of((st, "qp", h, t))[:, 0:128].rearrange("p (h e) -> p h e", h=2)
                        o = xn[:, t, h * P:(h + 1) * P].rearrange("p (h e) -> p h e", h=2)
                        cos, sin = (a[:, t, :].unsqueeze(1).broadcast_to([P, 2, 32]) for a in (cosb, sinb))
                        rotate(q[:, :, 0:32], q[:, :, 32:64], cos, sin, (2, 32), [(o[:, :, 0:32], o[:, :, 32:64])],
                               (st, "qp", h, t))
                ahead((*L, "ukv", 0))
                rotate(rest[:, :, R_KPE:R_KPE + 32], rest[:, :, R_KPE + 32:R_KPE + 64], cosb[:, :, :], sinb[:, :, :], (2, 32),
                       [(xn[:, :, 256 + 64 * u:288 + 64 * u], xn[:, :, 288 + 64 * u:320 + 64 * u]) for u in range(2)], (st, "kpe"))
                tick(rows_ready, (st, "rope"))
                for t in range(NT):
                    dve.wait_ge(matmul_done.sem, matmul_done.at((st, "vm", t)))
                    V.tensor_copy(vm[:, t, :], G.of((st, "vm", t))[:, :]).then_inc(dve_read.sem, dve_read.next((st, "vm", t)))
                dve.wait_ge(transposed.sem, transposed.at(((st, "peT"), 1)))
                V.tensor_copy(kpT, TB.of(((st, "peT"), 1))[:, 0:S]).then_inc(dve_read.sem, dve_read.next(((st, "peT"), 1)))
                attention(("mla", l), even(("mla", l), 4, 24))
                columns((("mla", l), "oT"), None, lambda k: oT[:, k, :], 4)
                for h in range(2):
                    ahead((*L, "mla", h))
                merge(st, "ymla", 2)
                columns((st, "mT"), None, lambda k: oT[:, k, :])
                for c in range(2):
                    for h in range(2):
                        ahead((*L, "out", c, h))
                add_to_x(st, lambda t, h: (G.of(((st, "y", h), t)), ((st, "y", h), t), ((st, "y", h), t)))

            def memory(st):
                l = st[1]
                L = ("l2", l)
                pre(st, ("norm_xattn_2", l))
                for j in (1, 3):
                    ahead((*L, "xq", j // 2))
                    dve.wait_ge(matmul_done.sem, matmul_done.at(((st, "xq"), j)))
                    V.tensor_copy(xqT[:, j, :], G.of(((st, "xq"), j))[:, 0:S]) \
                        .then_inc(dve_read.sem, dve_read.next(((st, "xq"), j)))
                norm((st, "mem"), mem)
                columns((st, "mem"), lambda k: gcol(("norm_mem_2", l), k), lambda k: oT[:, k, :])
                for j in (1, 3):
                    ahead((*L, "xk", j // 2))
                    dve.wait_ge(matmul_done.sem, matmul_done.at(((st, "xk"), j)))
                    V.tensor_copy(xkT[:, j, :], G.of(((st, "xk"), j))[:, 0:S]) \
                        .then_inc(dve_read.sem, dve_read.next(((st, "xk"), j)))
                for h in range(2):
                    ahead((*L, "xv", h))
                dve.wait_ge(matmul_done.sem, matmul_done.at(((st, "xv"), 1)))
                V.tensor_copy(xv[:, 1, :], G.of(((st, "xv"), 1))[:, :]).then_inc(dve_read.sem, dve_read.next(((st, "xv"), 1)))
                dve.wait_ge(pool_step.sem, pool_step.at(("zeros", l)))
                attention(st, even(st, 4, 24))
                columns((st, "oT"), None, lambda k: oT[:, k, :], 4)
                for h in range(2):
                    ahead((*L, "xo", h))
                k = (st, "y")
                add_to_x(st, lambda t, h: (G.of((k, t, h)), (k, t, h), (k, "chunk", ("l2", l, "xo", 1))))

            dve.wait_ge(consts_loaded.sem, consts_loaded.at("c"))
            for j in range(2):
                ins = V.tensor_copy(lines[:, j, 2 * REL_CLIP + 1:3 * P],
                                    lines[:, j, 2 * REL_CLIP:2 * REL_CLIP + 1].broadcast_to([HEADS_A, P - 1]))
            step(ins)
            for n in (1, 3):
                dve.wait_ge(transposed.sem, transposed.at(("gains", n)))
                if n == 1:
                    ins = V.tensor_copy(gT[:, 1, 0:gain_tiles[1]], TB.of(("gains", 1))[:, 0:gain_tiles[1]])
                else:
                    ins = V.tensor_copy(convwT[:, :, 0:TAPS * CT],
                                        TB.of(("gains", 3))[:, 0:2 * P].rearrange("p (l n) -> p l n", l=2)[:, :, 0:TAPS * CT])
                settle(dve, ins, dve_read, ("gains", n))
            dve.wait_ge(pool_step.sem, pool_step.at("bucket"))
            buckets = rtmp[0:BUCKETS, 0:2, :].rearrange("p a b -> p (a b)")[:, 0:3 * P]
            step(V.memset(buckets, -1.0))
            step(V.tensor_copy(buckets[:, P:P + 16], tmp2[0:BUCKETS, 0:16]))
            for b in range(16, BUCKETS):
                ds = [d for d in range(S) if t5_bucket(d) == b]
                step(V.memset(buckets[:, P + ds[0]:P + ds[-1] + 1], float(b)))
            step(V.tensor_scalar(onehot[:, :], buckets, tmp2[0:BUCKETS, 16:17], None, ALU.is_equal), "onehot")
            dve.wait_ge(matmul_done.sem, matmul_done.at("line"))
            settle(dve, V.tensor_copy(lines[0:NSA_HEADS, 2, :], G.of("line")[0:NSA_HEADS, 0:3 * P]), dve_read, "line")
            tick(dve_step, "lines")
            dve.wait_ge(act_read.sem, act_read.at(("gains", 2)))
            for n in range(2):
                step(V.tensor_tensor(tmp[:, 0:DH], lam_in[:, 2 * n, :], lam_in[:, 2 * n + 1, :], ALU.mult))
                step(V.tensor_reduce(lam[:, n:n + 1], tmp[:, 0:DH], AX.X, ALU.add), "lambda")
            lambda_init = 0.8 - 0.6 * math.exp(-0.3 * 2)
            dve.wait_ge(act_step.sem, act_step.at("lambda"))
            step(V.tensor_tensor(lam[:, 5:6], lam[:, 3:4], lam[:, 2:3], ALU.subtract))
            step(V.tensor_scalar(lam[:, 6:7], lam[:, 5:6], lambda_init, None, ALU.subtract))
            dve.wait_ge(pool_step.sem, pool_step.at("valid"))
            step(V.tensor_copy(pos_f[:, :], pos_i[:, :]))
            for t in range(NT):
                step(V.tensor_scalar(sinb[:, t, :], freq[:, :], pos_f[:, t:t + 1], None, ALU.mult))
            turns = tmp[:, 0:64].rearrange("p (t f) -> p t f", t=NT)
            step(V.tensor_scalar(turns, sinb[:, :, :], 1.0 / (2 * math.pi), None, ALU.mult))
            step(V.tensor_scalar(turns, turns, MAGIC, None, ALU.add))
            step(V.tensor_scalar(turns, turns, MAGIC, None, ALU.subtract))
            for part_of_turn in (6.28125, 0.0019340515136718750, 2 * math.pi - 6.28125 - 0.0019340515136718750):
                step(V.scalar_tensor_tensor(sinb[:, :, :], turns, -part_of_turn, sinb[:, :, :], ALU.mult, ALU.add))
            step(V.tensor_scalar(sinb[:, :, :], sinb[:, :, :], 3.1415925, -3.1415925, ALU.min, ALU.max))
            step(V.scalar_tensor_tensor(cosb[:, :, :], sinb[:, :, :], -1.0, sinb[:, :, :], ALU.mult, ALU.max))
            step(V.tensor_scalar(cosb[:, :, :], cosb[:, :, :], -1.0, math.pi / 2, ALU.mult, ALU.add), "angles")
            dve.wait_ge(lines_stored.sem, lines_stored.at("l"))
            ahead(chunks[0][0])
            for st in stages:
                i = st[1]
                if st[0] == "ff1":
                    ffn(st, ("g", i, 0))
                elif st[0] == "ff2":
                    ffn(st, ("g", i, 4))
                elif st[0] == "ff3":
                    ffn(st, ("norm_ffn_2", i))
                else:
                    {"mix": mixer, "l2": branches, "xattn": memory}[st[0]](st)
            if last == ("ff3", DEPTH2 - 1):
                dve.wait_ge(squared.sem, squared.at(("final", 1)))
                mean("final", 2, 2, ssum[:, 4:6], D)
                dve.wait_ge(rstd_ready.sem, rstd_ready.at("final"))
                n = gain_n["final"]
                dve.wait_ge(gain_loaded[n % 2].sem, gain_loaded[n % 2].at("final"))
                for t in range(NT):
                    ins = V.scalar_tensor_tensor(xn[:, t, :], x[:, t, :], rstd[:, 2 + t:3 + t], gain_row[n % 2][:, :], ALU.mult, ALU.mult)
                    ins.then_inc(rows_ready.sem, rows_ready.next("final"))


_INS = """x norm_g ff1_w_in ff1_w_out ff2_w_in ff2_w_out a_w_qkv a_rel_bias a_w_o b_w_in b_ln_g b_ln_b b_w_s b_b_s b_w_o
c_w_qkv c_lambda c_subln_g c_w_o mem_2 positions_2 rel_bias_2 norm_mix_2 norm_xattn_2 norm_mem_2 norm_ffn_2 norm_final_2
w_in_2 conv_w_2 conv_b_2 conv_ln_g_2 conv_ln_b_2 w_branch_conv_2 cmp_pos_k_2 cmp_w1_k_2 cmp_b1_k_2 cmp_w2_k_2 cmp_pos_v_2
cmp_w1_v_2 cmp_b1_v_2 cmp_w2_v_2 w_branch_nsa_2 mla_norm_q_2 mla_norm_kv_2 w_uq_2 w_ukv_2 w_branch_mla_2 w_out_2 w_xq_2
w_xkv_2 w_xo_2 w_gate_up_2 w_down_2""".split()
STOP = None


def kernel(**inputs):
    import numpy as np
    import concourse.bacc as bacc
    from concourse.bass_utils import run_bass_kernel_spmd

    plan = {}
    for _ in range(3):
        nc = bacc.Bacc("TRN2", target_bir_lowering=False, num_devices=1)
        arrays, args = {}, {}
        for name in _INS:
            a = np.ascontiguousarray(inputs[name])
            arrays[f"in_{name}_dram"] = a
            args[name] = nc.dram_tensor(f"in_{name}_dram", a.shape, mybir.dt.from_np(a.dtype), kind="ExternalInput").ap()
        out = nc.dram_tensor("out_0_dram", (1, S, D), F32, kind="ExternalOutput").ap()
        build(nc, args, out, plan, STOP)
    return run_bass_kernel_spmd(nc, [arrays], core_ids=[0]).results[0]["out_0_dram"]
```

```python
import math
from contextlib import ExitStack

import concourse.bass as bass
from concourse import mybir

F32 = mybir.dt.float32
F32R = mybir.dt.float32r
I32 = mybir.dt.int32
ALU = mybir.AluOpType
ACT = mybir.ActivationFunctionType
AX = mybir.AxisListType

P = 128
S = 256
NT = S // P
D = 1024
KD = D // P
DEPTH = 4
DEPTH2 = 2
D_FF = 2816
KF = D_FF // P
EPS = 1e-6
NEG = -1e30
CHUNK = 64
HEADS_A = 16
DH = 64
REL_CLIP = 128
HEADS_C = 8
GROUPS_B = 8
CONV_CH = 512
CT = CONV_CH // P
TAPS = 31
NSA_HEADS = 8
CMP_BLOCK = 32
CMP_STRIDE = 16
N_CMP = (S - CMP_BLOCK) // CMP_STRIDE + 1
MLA_HEADS = 4
NOPE = 128
ROPE = 64
X_HEADS = 4
ROPE_THETA = 10000.0
BUCKETS = 32
COL_GLU, COL_Q, COL_KV, COL_REST = 0, 1024, 1536, 2304
COL_MERGE = 3032
N_REST = COL_MERGE - COL_REST
R_GATE, R_CQ, R_CKV, R_KPE = 0, 24, 408, 664
TW = 257
SLOTS = 3
SLOT = 2048
AHEAD = 2
MAGIC = 1.5 * 2 ** 23


class Signal:

    def __init__(self, sem, reached, step=1):
        self.sem, self.reached, self.step, self.count = sem, reached, step, 0

    def next(self, key):
        self.count += self.step
        self.reached[key] = self.count
        return self.step

    def at(self, key):
        return self.reached.get(key, 1)

    def has(self, key):
        return key in self.reached


class Banks:

    def __init__(self, tiles, which, owner, taken, readers):
        self.tiles, self.which, self.owner, self.taken, self.readers, self.n = tiles, which, owner, taken, readers, 0

    def take(self, pe, key):
        i = self.which[self.n % len(self.which)]
        self.n += 1
        if i in self.owner:
            for reader in self.readers:
                if reader.has(self.owner[i]):
                    pe.wait_ge(reader.sem, reader.at(self.owner[i]))
        self.owner[i] = key
        self.taken[key] = i
        return self.tiles[i]

    def of(self, key):
        return self.tiles[self.taken.get(key, 0)]


class Split:

    def __init__(self, high, low):
        self.high, self.low = high, low

    def __getitem__(self, i):
        return Split(self.high[i], self.low[i])


def three(a, b):
    return [(a.high, b.high), (a.high, b.low), (a.low, b.high)]


def t5_bucket(d):
    exact = BUCKETS // 2
    if d < exact:
        return d
    return min(exact + int(math.log(d / exact) / math.log(128 / exact) * (BUCKETS - exact)), BUCKETS - 1)


def weight_chunks(w):
    out = []

    def cols(key, m, c0, n, each=256):
        for h, c in enumerate(range(c0, c0 + n, each)):
            nn = min(each, c0 + n - c)
            out.append(((*key, h), [(lambda s, n=nn, k=m.shape[0] // P: s[:, 0:k * n].rearrange("p (k n) -> p k n", k=k),
                                     m[:, c:c + nn].rearrange("(k p) n -> p k n", p=P))]))

    def rows(key, m, nk):
        n, total = m.shape[1], m.shape[0] // P
        for h, k0 in enumerate(range(0, total, nk)):
            out.append(((*key, h), [(lambda s, n=n, nk=min(nk, total - k0): s[:, 0:nk * n].rearrange("p (k n) -> p k n", k=nk),
                                     m[k0 * P:min(k0 + nk, total) * P, :].rearrange("(k p) n -> p k n", p=P))]))

    def ffn(key, w_in, w_out):
        for j in range(KF // 2):
            cols((key, "gate", j), w_in, j * 256, 256)
            cols((key, "up", j), w_in, D_FF + j * 256, 256)
        rows((key, "out"), w_out, 2)

    for i in range(DEPTH):
        ffn(("ff1", i), w["ff1_w_in"][i], w["ff1_w_out"][i])
        kind, j = i % 3, i // 3
        win, wo = [("a_w_qkv", "a_w_o"), ("b_w_in", "b_w_o"), ("c_w_qkv", "c_w_o")][kind]
        for c in (2, 3, 0, 1) if kind == 1 else range(w[win].shape[2] // 512):
            cols((("mix", i), "in", c), w[win][j], c * 512, 512)
        for c in range(2):
            cols((("mix", i), "out", c), w[wo][j], c * 512, 512)
        ffn(("ff2", i), w["ff2_w_in"][i], w["ff2_w_out"][i])
    for l in range(DEPTH2):
        w_in = w["w_in_2"][l]
        L = ("l2", l)
        for c in range(2):
            cols((*L, "glu", c), w_in, c * 512, 512)
        for h in range(2):
            out.append(((*L, "q", h), [
                (lambda s, c=c, g=g: s[:, :].rearrange("p (k c g d) -> p k c g d", k=KD, c=2, g=2)[:, :, c, g, :],
                 w_in[:, COL_Q + (4 * g + 2 * h + c) * DH:COL_Q + (4 * g + 2 * h + c + 1) * DH].rearrange("(k p) d -> p k d", p=P))
                for c in range(2) for g in range(2)]))
        cols((*L, "kv"), w_in, COL_KV, 768)
        cols((*L, "rest"), w_in, COL_REST, N_REST)
        for c in range(6):
            cols((*L, "merge", c), w_in, COL_MERGE + c * 512, 512)
            if c in (1, 2):
                gate = [out.pop() for _ in range(2)][::-1]
                rows((*L, "cmp", c - 1), w[("cmp_w1_k_2", "cmp_w1_v_2")[c - 1]][l], 8)
                out[-2:] = [out[-2], gate[0], out[-1], gate[1]]
        rows((*L, "conv"), w["w_branch_conv_2"][l], 2)
        rows((*L, "nsa"), w["w_branch_nsa_2"][l], 2)
        cols((*L, "uq"), w["w_uq_2"][l], 0, 768, 384)
        rows((*L, "ukv"), w["w_ukv_2"][l], 2)
        rows((*L, "mla"), w["w_branch_mla_2"][l], 2)
        for c in range(2):
            cols((*L, "out", c), w["w_out_2"][l], c * 512, 512)
        cols((*L, "xq"), w["w_xq_2"][l], 0, 512)
        cols((*L, "xk"), w["w_xkv_2"][l], 0, 512)
        cols((*L, "xv"), w["w_xkv_2"][l], 512, 512)
        rows((*L, "xo"), w["w_xo_2"][l], 2)
        ffn(("ff3", l), w["w_gate_up_2"][l], w["w_down_2"][l])
    return out


def gate_keys(L, c):
    own = [(*L, "merge", c, h) for h in range(2)]
    if c not in (1, 2):
        return own
    return [(*L, "cmp", c - 1, 0), own[0], (*L, "cmp", c - 1, 1), own[1]]


def build(nc, w, out, plan, stop=None):
    chunks = weight_chunks(w)
    chunk_index = {key: n for n, (key, _) in enumerate(chunks)}
    whole = [len(key) > 2 and key[2] == "cmp" for key, _ in chunks]
    split_no = [n - sum(whole[:n]) for n in range(len(chunks))]

    with ExitStack() as ctx:
        def sb(name, shape, dt=F32):
            return ctx.enter_context(nc.sbuf_tensor("sb_" + name, shape, dt))

        def signal(name, step=1):
            return Signal(ctx.enter_context(nc.semaphore(name)), plan.setdefault(name, {}), step)

        slots = [sb(f"slot{i}", [P, SLOT]) for i in range(SLOTS)]
        high = [sb(f"high{i}", [P, SLOT], F32R) for i in range(SLOTS)]
        low = [sb(f"low{i}", [P, SLOT], F32R) for i in range(SLOTS)]
        x = sb("x", [P, NT, D])
        hT = Split(sb("hT_high", [P, KD, S], F32R), sb("hT_low", [P, KD, S], F32R))
        oT = Split(sb("oT_high", [P, KD, S], F32R), sb("oT_low", [P, KD, S], F32R))
        xn = sb("xn", [P, NT, D])
        gain_row = [sb(f"gain_row{i}", [P, D]) for i in range(2)]
        o_rows = sb("o_rows", [P, NT, D])
        ident = sb("ident", [P, P])
        minus_half = sb("minus_half", [P, 16])
        gT = sb("gT", [P, 3, P])
        convwT = sb("convwT", [P, 2, P])
        lam = sb("lam", [P, 8])
        subln = sb("subln", [P, P])
        cosb = sb("cosb", [P, NT, 32])
        sinb = sb("sinb", [P, NT, 32])
        valid = sb("valid", [P, NT])
        ssum = sb("ssum", [P, 8])
        mean_sq = sb("mean_sq", [P, 16])
        rstd = sb("rstd", [P, 16])
        stats = sb("stats", [P, 2, 6])
        moments = sb("moments", [P, NT, 2])
        tmp = sb("tmp", [P, 512])
        sc = sb("sc", [P, 3, S])
        nmax = sb("nmax", [P, 3])
        pr = sb("pr", [P, 3, S])
        prT = sb("prT", [P, 2, S])
        sums = sb("sums", [P, NT, 32])
        inv = sb("inv", [P, NT, 32])
        silu = prT
        hid_f = sc
        tmp2 = xn[:, 1, 512:1024]
        junk = prT[:, :, :].rearrange("p a s -> p (a s)")
        diag = sc[:, :, :].rearrange("p a s -> p (a s)")[:, 0:4 * P].rearrange("p (n m) -> p n m", n=4)
        rtmp = o_rows[:, 0, :].rearrange("p (n m) -> p n m", n=4)
        line_dram = [nc.dram_tensor(f"line_dram{i}", [HEADS_A, 3 * P], F32).ap() for i in range(3)]

        with nc.sbuf_tensor("sb_hidden_high", [P, KF, S], F32R) as hid_high, \
                nc.sbuf_tensor("sb_hidden_low", [P, KF, S], F32R) as hid_low:
            hidT = Split(hid_high, hid_low)
        AR = 14500
        arena = sb("arena", [P, AR])
        used = [0]

        def part(values, pattern=None, **dims):
            a = arena[:, used[0]:used[0] + values]
            used[0] += values
            assert used[0] <= AR, used[0]
            return a.rearrange(pattern, **dims) if pattern else a

        used[0] = KF * S * 2
        gains = part(3 * P, "p (n m) -> p n m", n=3)
        convw = part(2 * P, "p (n m) -> p n m", n=2)
        lines = part(9 * P, "p (j w) -> p j w", j=3)[0:HEADS_A]
        onehot = part(3 * P)[0:BUCKETS]
        bias2 = part(NSA_HEADS)[0:BUCKETS]
        lam_in = part(4 * DH, "p (a d) -> p a d", a=4)
        pos_i = part(NT).bitcast(I32)
        pos_f = part(NT)
        freq = part(32)
        used[0] = 0
        qkT = part(16 * S, "p (c s) -> p c s", c=16)
        v_rows = part(NT * D, "p (t n) -> p t n", t=NT)
        relA = part(HEADS_A * TW, "p (h w) -> p h w", h=HEADS_A)
        relC = relA[:, 0:HEADS_C, :]
        used[0] = 0
        u_rows = part(NT * D, "p (t n) -> p t n", t=NT)
        g_rows = part(NT * D, "p (t n) -> p t n", t=NT)
        ws = part(GROUPS_B * P, "p (g s) -> p g s", g=GROUPS_B)
        wsT = part(GROUPS_B * P, "p (g s) -> p g s", g=GROUPS_B)
        used[0] = 0
        merge_gate = part(NT * 2 * D, "p (t n) -> p t n", t=NT)
        merged = merge_gate[:, :, 0:D]
        gate_half = [merge_gate[:, :, c * 512:(c + 1) * 512] for c in range(4)] + [o_rows[:, :, 512:D], xn[:, :, 512:D]]
        relN = part(NSA_HEADS * TW, "p (h w) -> p h w", h=NSA_HEADS)
        causal = part(TW)
        rest = part(NT * N_REST, "p (t n) -> p t n", t=NT)
        vwin = part(NT * P, "p (t n) -> p t n", t=NT)
        qsT = part(4 * S, "p (c s) -> p c s", c=4)
        kslcT = part(S)
        kwinT = part(S)
        vslc = part(NT * P, "p (t n) -> p t n", t=NT)
        hid_c = part(2 * 2 * 30, "p (v f n) -> p v f n", v=2, f=2)
        kcT = part(32)
        vc = part(2 * DH, "p (g d) -> p g d", g=2)
        w2k = part(2 * 2 * DH, "p (f u d) -> p f u d", f=2, u=2)
        w2v = part(2 * DH, "p (f d) -> p f d", f=2)
        here = used[0]
        bT = part(CT * S, "p (c s) -> p c s", c=CT)
        glu = part(CT * (S + TAPS - 1), "p (c s) -> p c s", c=CT)
        convT = part(CT * S, "p (c s) -> p c s", c=CT)
        aT = glu[:, :, TAPS - 1:TAPS - 1 + S]
        used[0] = here
        qnT = part(MLA_HEADS * S, "p (h s) -> p h s", h=MLA_HEADS)
        knT = part(MLA_HEADS * S, "p (h s) -> p h s", h=MLA_HEADS)
        qpT = part(2 * S, "p (h s) -> p h s", h=2)
        kpT = part(S)
        vm = part(NT * 512, "p (t n) -> p t n", t=NT)
        used[0] = 0
        xqT = part(X_HEADS * S, "p (h s) -> p h s", h=X_HEADS)
        xkT = part(X_HEADS * S, "p (h s) -> p h s", h=X_HEADS)
        xv = part(NT * 512, "p (t n) -> p t n", t=NT)
        zeros = part(S)
        mem = o_rows
        tokT = xn[:, 0, 0:2 * S].rearrange("p (v s) -> p v s", v=2)
        flat = o_rows[:, :, :].rearrange("p t n -> p (t n)")
        tok2 = flat[:, 0:4 * S].rearrange("p (v g s) -> p v g s", v=2, g=2)
        blk = flat[:, 4 * S:4 * S + 960].rearrange("p (v j g c) -> p v j g c", v=2, j=16, g=2)

        psum = [ctx.enter_context(nc.psum_tensor(f"bank{i}", [P, 512], F32)) for i in range(8)]

        slot_loaded = [signal(f"slot{i}_loaded", 16) for i in range(SLOTS)]
        x_loaded = [signal(f"x{t}_loaded", 16) for t in range(NT)]
        gains_loaded = signal("gains_loaded", 16)
        consts_loaded = signal("consts_loaded", 16)
        lines_stored = signal("lines_stored", 16)
        table_loaded = signal("table_loaded", 16)
        gain_loaded = [signal(f"gain{i}_loaded", 16) for i in range(2)]
        small_loaded = signal("small_loaded", 16)
        out_stored = signal("out_stored", 16)
        matmul_done = signal("matmul_done")
        transposed = signal("transposed")
        act_read = signal("act_read")
        dve_read = signal("dve_read")
        squared = signal("squared")
        high_ready = signal("high_ready")
        low_ready = signal("low_ready")
        dve_step = signal("dve_step")
        act_step = signal("act_step")
        pool_step = signal("pool_step")
        scored = signal("scored")
        maxed = signal("maxed")
        weighed = signal("weighed")
        mean_ready = signal("mean_ready")
        rstd_ready = signal("rstd_ready")
        x_ready = signal("x_ready")
        rows_ready = signal("rows_ready")
        tok_loaded = signal("tok_loaded", 16)
        mem_loaded = signal("mem_loaded", 16)
        spatial_loaded = signal("spatial_loaded", 16)

        readers = (act_read, dve_read)
        owner, taken = {}, plan.setdefault("taken", {})
        G, SB, TB, SCORES, SUMMED = (Banks(psum, which, owner, taken, readers) for which in
                                     ((0, 1, 2, 3), (4, 5), (6, 7), (3, 4, 5), (0, 1, 2)))
        chunk_end = plan.setdefault("chunk_end", {})

        col = {}
        loads = []

        tile, row = 0, 0
        gain_tiles = []

        def put(key, ap, n):
            nonlocal tile, row
            if row + n > P:
                gain_tiles.append(row)
                tile, row = tile + 1, 0
            col[key] = (tile, row)
            loads.append((gains[row:row + n, tile, :], ap))
            row += n

        for l in range(DEPTH2):
            put(("g", 2 * l), w["norm_g"][2 * l:2 * l + 2].rearrange("i n (a p) -> (i n a) p", p=P), 2 * 6 * KD)
            for i in (2 * l, 2 * l + 1):
                for n in (0, 2, 4):
                    col["g", i, n] = (l, (6 * (i % 2) + n) * KD)
            for name in ("norm_mix_2", "norm_xattn_2", "norm_mem_2", "norm_ffn_2"):
                put((name, l), w[name][l].rearrange("(a p) -> a p", p=P), KD)
        first_loads = len(loads) // 2
        for l in range(DEPTH2):
            for name, n in (("conv_b_2", 4), ("conv_ln_g_2", 4), ("conv_ln_b_2", 4), ("mla_norm_q_2", 3),
                            ("mla_norm_kv_2", 2), ("cmp_b1_k_2", 2), ("cmp_b1_v_2", 2)):
                put((name, l), w[name][l].rearrange("(a p) -> a p", p=P), n)
            for name in ("cmp_pos_k_2", "cmp_pos_v_2"):
                put((name, l), w[name][l].rearrange("(a b) d -> a (b d)", b=2), 16)
        put("b_b_s", w["b_b_s"][0], GROUPS_B)
        assert tile <= 2
        gain_tiles.append(row)

        def gcol(key, k=0):
            t, r = col[key]
            return gT[:, t, r + k:r + k + 1]

        row_gains = []
        for i in range(DEPTH):
            row_gains.append((("g", i, 1), w["norm_g"][i, 1]))
            if i % 3 == 1:
                row_gains += [("ln_g", w["b_ln_g"][0]), ("ln_b", w["b_ln_b"][0])]
            row_gains += [(("g", i, 3), w["norm_g"][i, 3]), (("g", i, 5), w["norm_g"][i, 5])]
        row_gains.append(("final", w["norm_final_2"]))
        gain_n = {key: n for n, (key, _) in enumerate(row_gains)}
        gain_for = {("ff1", i): ("g", i, 1) for i in range(DEPTH)}
        gain_for |= {("mix", i): ("g", i, 3) for i in range(DEPTH)}
        gain_for |= {("ff2", i): ("g", i, 5) for i in range(DEPTH)}

        block = ctx.enter_context(nc.Block())

        stages = []
        for i in range(DEPTH):
            stages += [("ff1", i), ("mix", i), ("ff2", i)]
        for l in range(DEPTH2):
            stages += [("l2", l), ("xattn", l), ("ff3", l)]
        if stop is not None:
            stages = stages[:stop]
        last = stages[-1]

        def norm_after(st):
            if st == last:
                return "final" if st == ("ff3", DEPTH2 - 1) else None
            return (stages[stages.index(st) + 1], "norm")

        def output(st, t, h):
            key = ((st, "y", h), t) if st[0] in ("mix", "l2") else ((st, "y"), t, h)
            return (SB, TB)[t].of(key), key

        def stage_of(key):
            if key[0] == "l2":
                return ("xattn", key[1]) if key[2] in ("xq", "xk", "xv", "xo") else ("l2", key[1])
            return key[0]

        def raw_view(key):
            n = chunk_index[key]
            return chunks[n][1][0][0](slots[n % SLOTS])

        def view(key):
            n = chunk_index[key]
            i = split_no[n] % SLOTS
            if key[0] == "l2" and key[2] == "q":
                return Split(*(a[i][:, :].rearrange("p (k n) -> p k n", k=KD) for a in (high, low)))
            return Split(*(chunks[n][1][0][0](a[i]) for a in (high, low)))

        last_chunk = max(n for n, (key, _) in enumerate(chunks) if stage_of(key) in stages)

        def users(n):
            before = [m for m in range(n) if not whole[m] and split_no[m] == split_no[n] - SLOTS]
            return before[0] if before else None

        def filled(n):
            return sum(src.shape[1] * src.shape[2] for _, src in chunks[n][1])

        @block.sync
        def _(sp):
            for dst, src in loads[0:first_loads]:
                sp.dma_start(dst, src).then_inc(gains_loaded.sem, gains_loaded.next("g"))
            for t in range(NT):
                sp.dma_start(x[:, t, :], w["x"][0, t * P:(t + 1) * P]).then_inc(x_loaded[t].sem, x_loaded[t].next("x"))
            for n in range(SLOTS):
                for dst, src in chunks[n][1]:
                    sp.dma_start(dst(slots[n]), src).then_inc(slot_loaded[n].sem, slot_loaded[n].next(chunks[n][0]))
            for dst, src in loads[first_loads:]:
                sp.dma_start(dst, src).then_inc(consts_loaded.sem, consts_loaded.next("c"))
            for l in range(DEPTH2):
                sp.dma_start(convw[0:TAPS * CT, l, :], w["conv_w_2"][l].rearrange("t (c p) -> (t c) p", p=P)) \
                    .then_inc(consts_loaded.sem, consts_loaded.next("c"))
            sp.dma_start(bias2[:, :], w["rel_bias_2"]).then_inc(consts_loaded.sem, consts_loaded.next("c"))
            sp.dma_start(lam_in[:, :, :].rearrange("p a d -> p (a d)"),
                         w["c_lambda"].rearrange("o a d -> o (a d)").broadcast_to([P, 4 * DH])) \
                .then_inc(consts_loaded.sem, consts_loaded.next("c"))
            sp.dma_start(subln[:, :], w["c_subln_g"].broadcast_to([P, P])).then_inc(consts_loaded.sem, consts_loaded.next("c"))
            sp.dma_start(pos_i[:, :], w["positions_2"][0].rearrange("(t p) -> p t", p=P), allow_slow_non_contiguous=True) \
                .then_inc(consts_loaded.sem, consts_loaded.next("c"))
            for j in range(2):
                sp.dma_start(lines[:, j, 0:2 * REL_CLIP + 1], w["a_rel_bias"][j]).then_inc(consts_loaded.sem, consts_loaded.next("c"))
            for n, (key, parts) in enumerate(chunks):
                st = stage_of(key)
                if st not in stages or n < SLOTS:
                    continue
                before = n - SLOTS
                if whole[before]:
                    sp.wait_ge(matmul_done.sem, matmul_done.at(chunk_end.get(chunks[before][0])))
                else:
                    sp.wait_ge(low_ready.sem, low_ready.at(before))
                slot = slots[n % SLOTS]
                for dst, src in parts:
                    sp.dma_start(dst(slot), src).then_inc(slot_loaded[n % SLOTS].sem, slot_loaded[n % SLOTS].next(key))
            if last == ("ff3", DEPTH2 - 1):
                for t in range(NT):
                    sp.wait_ge(rows_ready.sem, rows_ready.at(("final", t)))
                    sp.dma_start(out[0, t * P:(t + 1) * P], xn[:, t, :]).then_inc(out_stored.sem, out_stored.next("o"))
            else:
                sp.wait_ge(x_ready.sem, x_ready.at((last, 1, 1)))
                sp.dma_start(out[0].rearrange("(t p) d -> p t d", p=P), x[:, :, :]).then_inc(out_stored.sem, out_stored.next("o"))
            if stop is not None:
                sp.wait_ge(lines_stored.sem, lines_stored.at("l"))
                for sig in (*gain_loaded, table_loaded, small_loaded, tok_loaded, mem_loaded, spatial_loaded):
                    if sig.reached:
                        sp.wait_ge(sig.sem, max(sig.reached.values()))
            sp.wait_ge(out_stored.sem, out_stored.at("o"))

        def settle(eng, ins, sig, key=None):
            ins.then_inc(sig.sem, sig.next(key if key is not None else ("n", sig.count)))
            eng.wait_ge(sig.sem, sig.count)

        def rev(table, t, kn):
            top = P * (t + 1)
            return table[:, top:top - kn:-1]

        def units_of(st):
            kind, i = st
            units = []
            if kind == "mix":
                for t in range(NT):
                    for s in range(16):
                        half = slice(DH * (s % 2), DH * (s % 2) + DH)
                        if i % 3 == 0:
                            table, v0, width = relA[:, s, :], s * DH, DH
                        else:
                            table, v0, width = relC[:, s // 2, :], (s // 2) * P, P
                        kn = P * (t + 1)
                        per = 512 // width
                        units.append(dict(
                            qk=[(qkT[half, s // 2, t * P:(t + 1) * P], qkT[half, 8 + s // 2, 0:kn])],
                            t=t, kn=kn, bias=rev(table, t, kn), scale=DH ** -0.5,
                            v=[v_rows[:, b, v0:v0 + width] for b in range(t + 1)],
                            acc=(st, "o", t, s // per), c0=(s % per) * width, width=width, col=s))
            elif kind == "l2":
                for t in range(NT):
                    for br in range(3):
                        for h in range(NSA_HEADS):
                            g = h // 4
                            half = slice(DH * g, DH * g + DH)
                            q = qsT[half, h % 4, t * P:(t + 1) * P]
                            if br == 0:
                                kn = min(N_CMP, (P * (t + 1) - CMP_BLOCK) // CMP_STRIDE + 1)
                                k = kcT[half, g * N_CMP:g * N_CMP + kn]
                                top = P * (t + 1) - (CMP_BLOCK - 1)
                                bias = relN[:, h, top:top - CMP_STRIDE * (kn - 1) - 1:-CMP_STRIDE]
                                v = [vc[0:kn, g, :]]
                            else:
                                kn = P * (t + 1)
                                k = (kslcT if br == 1 else kwinT)[half, 0:kn]
                                bias = rev(relN[:, h, :], t, kn)
                                v = [vslc[:, b, g * DH:g * DH + DH] if br == 1 else
                                     vwin[:, b, g * DH:g * DH + DH] for b in range(t + 1)]
                            units.append(dict(qk=[(q, k)], t=t, kn=kn, bias=bias, scale=DH ** -0.5, v=v,
                                              acc=(st, "o", t, br), c0=h * DH, width=DH, col=br * 8 + h))
            elif kind == "mla":
                for t in range(NT):
                    for h in range(MLA_HEADS):
                        half = slice(DH * (h % 2), DH * (h % 2) + DH)
                        kn = P * (t + 1)
                        tok = slice(t * P, (t + 1) * P)
                        units.append(dict(
                            qk=[(qnT[:, h, tok], knT[:, h, 0:kn]), (qpT[half, h // 2, tok], kpT[half, 0:kn])],
                            t=t, kn=kn, bias=rev(causal, t, kn), scale=(NOPE + ROPE) ** -0.5,
                            v=[vm[:, b, h * P:(h + 1) * P] for b in range(t + 1)],
                            acc=(st, "o", t, 0), c0=h * P, width=P, col=24 + h))
            elif kind == "xattn":
                for t in range(NT):
                    for h in range(X_HEADS):
                        units.append(dict(
                            qk=[(xqT[:, h, t * P:(t + 1) * P], xkT[:, h, :])], t=t, kn=S, bias=zeros,
                            scale=P ** -0.5, v=[xv[:, b, h * P:(h + 1) * P] for b in range(NT)],
                            acc=(st, "o", t, 0), c0=h * P, width=P, col=24 + h))
            for n, u in enumerate(units):
                u["first"] = n == 0 or not any(m["acc"] == u["acc"] for m in units[:n])
                u["last"] = not any(m["acc"] == u["acc"] for m in units[n + 1:])
                u["blocks"] = [(b * P, min(P, u["kn"] - b * P)) for b in range(len(u["v"]))]
            return units

        @block.tensor
        def _(pe):

            def arrived(key):
                n = chunk_index[key]
                if whole[n]:
                    pe.wait_ge(slot_loaded[n % SLOTS].sem, slot_loaded[n % SLOTS].at(key))
                else:
                    pe.wait_ge(low_ready.sem, low_ready.at(n))

            def mm(o, lhsT, rhs, start, stop):
                return nc.tensor.matmul(o, lhsT, rhs, start=start, stop=stop)

            def split_mm(o, lhsT, rhs, start, stop):
                for n, (a, b) in enumerate(three(lhsT, rhs)):
                    ins = mm(o, a, b, start and n == 0, stop and n == 2)
                return ins

            awaited = []

            def product(key, pairs, width, rows=P, c0=0, bank=None, done=True):
                o = (G.take(pe, key) if bank is None else bank)[0:rows, c0:c0 + width]
                for n, (lhsT, rhs) in enumerate(pairs):
                    if awaited and n % 2 == 0:
                        pe.wait_ge(dve_read.sem, dve_read.at(awaited.pop(0)))
                    one = split_mm if type(lhsT) is Split else mm
                    ins = one(o, lhsT, rhs, n == 0, n == len(pairs) - 1)
                if done:
                    ins.then_inc(matmul_done.sem, matmul_done.next(key))

            def to_columns(key, one, nk, ready=None, nt=NT):
                banks = []
                for t in range(nt):
                    if ready:
                        pe.wait_ge(rows_ready.sem, rows_ready.at(ready(t)))
                    for b in range((nk + 1) // 2):
                        if t == 0:
                            banks.append(G.take(pe, (key, b)))
                        for kt in range(2 * b, min(2 * b + 2, nk)):
                            ins = one(banks[b][:, (kt % 2) * S + t * P:(kt % 2) * S + (t + 1) * P], t, kt)
                        if t == nt - 1:
                            ins.then_inc(transposed.sem, transposed.next((key, b)))

            def turned(src):
                return lambda o, t, kt: nc.tensor.transpose(o, src(t, kt), ident[:, :])

            def norm(n, src, d0):
                to_columns(n, lambda o, t, kt: mm(o, src[:, t, kt * P:(kt + 1) * P], diag[:, d0 + t, :], True, True),
                           KD, lambda t: (n, t))
                awaited.extend((n, b) for b in range(KD // 2))

            def columns_gemm(ckeys, key, src):
                c = 0
                for ckey in ckeys:
                    arrived(ckey)
                    s = view(ckey)
                    for h in range(s.high.shape[2] // P):
                        product((key, c), [(s[:, k, h * P:(h + 1) * P], src[:, k, :]) for k in range(KD)], S)
                        chunk_end[ckey] = (key, c)
                        c += 1

            def rows_gemm(ckeys, key, src, banks=None, before=None):
                if banks is None:
                    banks = [G.take(pe, (key, t)) for t in range(NT)]
                c0 = 0
                for h, ckey in enumerate(ckeys):
                    if before:
                        before(h)
                    arrived(ckey)
                    s = view(ckey)
                    n = s.high.shape[2]
                    for t in range(NT):
                        last_one = ckey == ckeys[-1]
                        ekey = (key, t) if last_one else (key, "part", t)
                        product(ekey, [(src[:, k, t * P:(t + 1) * P], s[:, k, :]) for k in range(KD)], n, c0=c0, bank=banks[t],
                                done=last_one or t == NT - 1)
                        chunk_end[ckey] = ekey
                    c0 += n

            def output_gemm(st, ckeys, src):
                banks = [[(SB, TB)[t].take(pe, ((st, "y", c), t)) for c in range(2)] for t in range(NT)]
                rows_gemm(ckeys[:2], (st, "y", 0), src, [banks[t][0] for t in range(NT)])
                for ckey in ckeys[2:]:
                    arrived(ckey)
                    chunk_end[ckey] = ((st, "y", 1), NT - 1)
                for t in range(NT):
                    for h, ckey in enumerate(ckeys[2:]):
                        s = view(ckey)
                        product(((st, "y", 1), t), [(src[:, k, t * P:(t + 1) * P], s[:, k, :]) for k in range(KD)], 256,
                                c0=h * 256, bank=banks[t][1], done=h == 1)

            def wide_gemm(st, ckeys, key, src, between=None):
                final = key[1] == "y"
                while awaited:
                    pe.wait_ge(dve_read.sem, dve_read.at(awaited.pop(0)))
                banks = [[((SB, TB)[t] if final else G).take(pe, (key, t, h)) for h in range(2)] for t in range(NT)]
                total = 2 * len(ckeys)

                def part_of(t, h, n, kk):
                    k = 2 * n + kk
                    return split_mm(banks[t][h][:, :], src[:, k, t * P:(t + 1) * P],
                                    view(ckeys[n])[:, kk, h * 512:(h + 1) * 512], k == 0, k == total - 1)

                def wait_for(n):
                    if st in ("ff1", "ff2", "ff3"):
                        pe.wait_ge(dve_step.sem, dve_step.at((key[0], "h", 2 * n + 1)))
                    arrived(ckeys[n])

                together = len(ckeys) - 2 if final else len(ckeys)
                for n in range(together):
                    if between and n == 4:
                        between()
                    wait_for(n)
                    for kk in range(2):
                        for t in range(NT):
                            for h in range(2):
                                ins = part_of(t, h, n, kk)
                    ins.then_inc(matmul_done.sem, matmul_done.next((key, "chunk", ckeys[n])))
                    chunk_end[ckeys[n]] = (key, "chunk", ckeys[n])
                if final:
                    for n in (together, together + 1):
                        wait_for(n)
                        chunk_end[ckeys[n]] = (key, 1, 1)
                    for t in range(NT):
                        for h in range(2):
                            for n in (together, together + 1):
                                for kk in range(2):
                                    ins = part_of(t, h, n, kk)
                            ins.then_inc(matmul_done.sem, matmul_done.next((key, t, h)))

            def ffn(st):
                norm((st, "norm"), x, 0)
                for j in range(KF // 2):
                    banks = [G.take(pe, (st, "h", 2 * j + c)) for c in range(2)]
                    for u, kind in enumerate(("gate", "up")):
                        ckey = (st, kind, j, 0)
                        arrived(ckey)
                        s = view(ckey)
                        for c in range(2):
                            key = (st, "h", 2 * j + c) if u else (st, "gate", j)
                            product(key, [(s[:, k, c * P:(c + 1) * P], hT[:, k, :]) for k in range(KD)], S,
                                    c0=u * S, bank=banks[c], done=bool(u or c))
                            chunk_end[ckey] = key
                wide_gemm(st[0], [(st, "out", m) for m in range(KF // 2)], (st, "y"), hidT, set_up if st == stages[0] else None)

            def attention(st):
                units = units_of(st)
                banks = {}
                for i in range(len(units) + 3):
                    if i < len(units):
                        u = units[i]
                        bank = SCORES.take(pe, (st, "s", i))
                        for n, (q, k) in enumerate(u["qk"]):
                            ins = mm(bank[:, 0:u["kn"]], q, k, n == 0, n == len(u["qk"]) - 1)
                        ins.then_inc(scored.sem, scored.next((st, i)))
                    if 2 <= i <= len(units) + 1:
                        u = units[i - 2]
                        pe.wait_ge(weighed.sem, weighed.at((st, i - 2)))
                        bank = TB.take(pe, (st, "p", i - 2))
                        for b, (k0, n) in enumerate(u["blocks"]):
                            ins = nc.tensor.transpose(bank[0:n, b * P:(b + 1) * P], pr[:, (i - 2) % 3, k0:k0 + n], ident[:, :])
                        ins.then_inc(transposed.sem, transposed.next((st, "p", i - 2)))
                    if i >= 3:
                        u = units[i - 3]
                        if u["first"]:
                            banks[u["acc"]] = SUMMED.take(pe, u["acc"])
                        pe.wait_ge(act_read.sem, act_read.at((st, "p", i - 3)))
                        for b, (k0, n) in enumerate(u["blocks"]):
                            ins = mm(banks[u["acc"]][:, u["c0"]:u["c0"] + u["width"]], prT[0:n, (i - 3) % 2, b * P:(b + 1) * P],
                                     u["v"][b], b == 0, b == len(u["blocks"]) - 1)
                        ins.then_inc(matmul_done.sem, matmul_done.next((st, "pv", i - 3)))

            def output_columns(st, nk):
                to_columns((st, "oT"), turned(lambda t, kt: o_rows[:, t, kt * P:(kt + 1) * P]), nk, lambda t: (st, "o", t))
                awaited.extend(((st, "oT"), b) for b in range(nk // 2))

            def mixer(st):
                i = st[1]
                norm((st, "norm"), x, 0)
                if i % 3 == 1:
                    for c in (2, 3, 0, 1):
                        rows_gemm([(st, "in", c, h) for h in range(2)], (st, "in", c), hT)
                    pe.wait_ge(pool_step.sem, pool_step.at("spatial"))
                    to_columns((st, "ws"), turned(lambda t, kt: ws[:, kt, :]), GROUPS_B, nt=1)
                    for b in range(4):
                        sig = (act_read, dve_read)[b % 2]
                        pe.wait_ge(sig.sem, sig.at(((st, "ws"), b)))
                    for t in range(NT):
                        pe.wait_ge(rows_ready.sem, rows_ready.at((st, "v", t)))
                        for h in range(2):
                            bank = G.take(pe, (st, "sv", t, h))
                            for g in range(4):
                                ins = mm(bank[:, g * P:(g + 1) * P], wsT[:, 4 * h + g, :],
                                         g_rows[:, t, (4 * h + g) * P:(4 * h + g + 1) * P], True, True)
                            ins.then_inc(matmul_done.sem, matmul_done.next((st, "sv", t, h)))
                else:
                    for c in range(4):
                        columns_gemm([(st, "in", c, h) for h in range(2)], (st, "qk", c), hT)
                    for c in range(2):
                        rows_gemm([(st, "in", 4 + c, h) for h in range(2)], (st, "v", c), hT)
                    pe.wait_ge(act_read.sem, act_read.at(((st, "qk", 3), 2)))
                    pe.wait_ge(dve_read.sem, dve_read.at(((st, "qk", 3), 3)))
                    pe.wait_ge(dve_read.sem, dve_read.at(((st, "v", 1), 1)))
                    pe.wait_ge(act_read.sem, act_read.at(((st, "v", 1), 0)))
                    attention(st)
                output_columns(st, KD)
                output_gemm(st, [(st, "out", c, h) for c in range(2) for h in range(2)], oT)

            def branches(st):
                l = st[1]
                L = ("l2", l)
                norm((st, "norm"), x, 0)
                for c in range(2):
                    columns_gemm([(*L, "glu", c, h) for h in range(2)], (st, "glu", c), hT)
                columns_gemm([(*L, "q", h) for h in range(2)], (st, "q"), hT)
                for h, names in enumerate((("tok", 0), ("tok", 1), "kslc", "vslc", "kwin", "vwin")):
                    ckey = (*L, "kv", h // 2)
                    arrived(ckey)
                    s = view(ckey)[:, :, (h % 2) * P:(h % 2 + 1) * P]
                    if names in ("vslc", "vwin"):
                        for t in range(NT):
                            product(((st, names), t), [(hT[:, k, t * P:(t + 1) * P], s[:, k, :]) for k in range(KD)], P)
                        chunk_end[ckey] = ((st, names), 1)
                    else:
                        product((st, names), [(s[:, k, :], hT[:, k, :]) for k in range(KD)], S)
                        chunk_end[ckey] = (st, names)
                rows_gemm([(*L, "rest", h) for h in range(2)], (st, "rest", 0), hT)
                rows_gemm([(*L, "rest", 2)], (st, "rest", 1), hT)
                for c in range(6):
                    banks = None
                    if c in (1, 2):
                        v = c - 1
                        pe.wait_ge(dve_read.sem, dve_read.at((st, "blk", v)))
                        hid_banks = [G.take(pe, (st, "hid", v, f)) for f in range(2)]
                        banks = [G.take(pe, ((st, "merge", c), t)) for t in range(NT)]

                    def compress(h):
                        arrived((*L, "cmp", v, h))
                        wv = raw_view((*L, "cmp", v, h))
                        for f in range(2):
                            for j in range(8):
                                ins = mm(hid_banks[f][:, 0:30], wv[:, j, f * P:(f + 1) * P],
                                         blk[:, v, 8 * h + j, :, :].rearrange("p g c -> p (g c)"), h == 0 and j == 0, h == 1 and j == 7)
                            key = (st, "hid", v, f) if h else (st, "hid half", v, f)
                            ins.then_inc(matmul_done.sem, matmul_done.next(key))
                        chunk_end[(*L, "cmp", v, h)] = key

                    rows_gemm([(*L, "merge", c, h) for h in range(2)], (st, "merge", c), hT, banks, compress if banks else None)
                    if c == 3:
                        pe.wait_ge(small_loaded.sem, small_loaded.at(st))
                        pe.wait_ge(act_read.sem, act_read.at((st, "hid", 1, 1)))
                        product((st, "kc"), [(w2k[:, f, :, :].rearrange("p u d -> p (u d)"), hid_c[:, 0, f, :]) for f in range(2)], 30)
                        for g in range(2):
                            product((st, "vc", g), [(hid_c[:, 1, f, g * N_CMP:(g + 1) * N_CMP], w2v[:, f, :]) for f in range(2)],
                                    DH, rows=N_CMP)
                pe.wait_ge(dve_step.sem, dve_step.at((st, "conv")))
                for t in range(NT):
                    bank = TB.take(pe, (st, "conv_rows", t))
                    for c in range(CT):
                        ins = nc.tensor.transpose(bank[:, c * P:(c + 1) * P], convT[:, c, t * P:(t + 1) * P], ident[:, :])
                    ins.then_inc(transposed.sem, transposed.next((st, "conv_rows", t)))
                to_columns((st, "convT"), turned(lambda t, kt: xn[:, t, kt * P:(kt + 1) * P]), CT, lambda t: (st, "conv", t))
                pe.wait_ge(dve_read.sem, dve_read.at(((st, "convT"), 1)))
                wide_gemm("conv", [(*L, "conv", h) for h in range(2)], (st, "yconv"), oT)
                pe.wait_ge(dve_read.sem, dve_read.at((st, "vc", 1)))
                pe.wait_ge(act_read.sem, act_read.at((st, "kwin")))
                attention(st)
                output_columns(st, 4)
                wide_gemm("nsa", [(*L, "nsa", h) for h in range(2)], (st, "ynsa"), oT)
                to_columns((st, "latT"), turned(lambda t, kt: rest[:, t, R_CQ + kt * P:R_CQ + (kt + 1) * P]), 5, lambda t: (st, "latent"))
                pe.wait_ge(dve_read.sem, dve_read.at(((st, "latT"), 2)))
                for h in range(2):
                    arrived((*L, "uq", h))
                    s = view((*L, "uq", h))
                    for g in range(2):
                        product((st, "qn", 2 * h + g), [(s[:, k, g * 192:g * 192 + P], hT[:, k, :]) for k in range(3)], S)
                    for t in range(NT):
                        product((st, "qp", h, t), [(hT[:, k, t * P:(t + 1) * P],
                                                    Split(*(a[:, k, :].rearrange("p (h e) -> p h e", h=2)[:, :, P:192]
                                                            for a in (s.high, s.low)))) for k in range(3)], 128)
                    chunk_end[(*L, "uq", h)] = (st, "qp", h, 1)
                arrived((*L, "ukv", 0))
                s = view((*L, "ukv", 0))
                for h in range(MLA_HEADS):
                    product((st, "kn", h), [(s[:, k, h * 256:h * 256 + P], hT[:, 3 + k, :]) for k in range(2)], S)
                for t in range(NT):
                    product((st, "vm", t), [(hT[:, 3 + k, t * P:(t + 1) * P],
                                             Split(*(a[:, k, :].rearrange("p (h e) -> p h e", h=4)[:, :, P:256]
                                                     for a in (s.high, s.low)))) for k in range(2)], 512)
                chunk_end[(*L, "ukv", 0)] = (st, "vm", 1)
                to_columns((st, "peT"), turned(lambda t, kt: xn[:, t, kt * P:(kt + 1) * P]), 3, lambda t: (st, "rope"))
                for b in range(2):
                    sig = (act_read, dve_read)[b % 2]
                    pe.wait_ge(sig.sem, sig.at(((st, "peT"), b)))
                pe.wait_ge(dve_read.sem, dve_read.at((st, "vm", 1)))
                pe.wait_ge(act_read.sem, act_read.at((st, "kn", 3)))
                attention(("mla", l))
                output_columns(("mla", l), 4)
                wide_gemm("mla", [(*L, "mla", h) for h in range(2)], (st, "ymla"), oT)
                to_columns((st, "mT"), turned(lambda t, kt: merged[:, t, kt * P:(kt + 1) * P]), KD, lambda t: (st, "merged", t))
                awaited.extend(((st, "mT"), b) for b in range(KD // 2))
                output_gemm(st, [(*L, "out", c, h) for c in range(2) for h in range(2)], oT)

            def memory(st):
                L = ("l2", st[1])
                norm((st, "norm"), x, 0)
                columns_gemm([(*L, "xq", h) for h in range(2)], (st, "xq"), hT)
                norm((st, "mem"), mem, 2)
                columns_gemm([(*L, "xk", h) for h in range(2)], (st, "xk"), oT)
                rows_gemm([(*L, "xv", h) for h in range(2)], (st, "xv"), oT)
                pe.wait_ge(act_read.sem, act_read.at(((st, "xk"), 2)))
                pe.wait_ge(dve_read.sem, dve_read.at(((st, "xk"), 3)))
                pe.wait_ge(dve_read.sem, dve_read.at(((st, "xv"), 1)))
                pe.wait_ge(act_read.sem, act_read.at(((st, "xv"), 0)))
                attention(st)
                output_columns(st, 4)
                wide_gemm("xo", [(*L, "xo", h) for h in range(2)], (st, "y"), oT)

            def transposed_gains(n):
                r = gain_tiles[n]
                bank = G.take(pe, ("gains", n))
                nc.tensor.transpose(bank[:, 0:r], gains[0:r, n, :], ident[0:r, 0:r]) \
                    .then_inc(transposed.sem, transposed.next(("gains", n)))

            def set_up():
                pe.wait_ge(consts_loaded.sem, consts_loaded.at("c"))
                transposed_gains(1)
                transposed_gains(2)
                bank = G.take(pe, ("gains", 3))
                for l in range(DEPTH2):
                    ins = nc.tensor.transpose(bank[:, l * P:l * P + TAPS * CT], convw[0:TAPS * CT, l, :],
                                              ident[0:TAPS * CT, 0:TAPS * CT])
                ins.then_inc(transposed.sem, transposed.next(("gains", 3)))
                pe.wait_ge(dve_step.sem, dve_step.at("onehot"))
                product("line", [(bias2[:, :], onehot[:, :])], 3 * P, rows=NSA_HEADS)

            pe.wait_ge(gains_loaded.sem, gains_loaded.at("g"))
            pe.wait_ge(pool_step.sem, pool_step.at("ident"))
            transposed_gains(0)
            for st in stages:
                {"ff1": ffn, "ff2": ffn, "ff3": ffn, "mix": mixer, "l2": branches, "xattn": memory}[st[0]](st)

        @block.scalar
        def _(act):

            def copy(o, i, scale=1.0):
                return nc.scalar.activation(o, i, ACT.Copy, scale=scale)

            def row_gain(n):
                if n >= 2:
                    act.wait_ge(dve_read.sem, dve_read.at(("gain", row_gains[n - 2][0])))
                if n < len(row_gains):
                    key, src = row_gains[n]
                    act.dma_start(gain_row[n % 2][:, :], src.rearrange("(a n) -> a n", a=1).broadcast_to([P, D])) \
                        .then_inc(gain_loaded[n % 2].sem, gain_loaded[n % 2].next(key))

            split_to = [0]

            def ahead(key, by=AHEAD):
                while split_to[0] <= min(chunk_index[key] + by, last_chunk):
                    n = split_to[0]
                    split_to[0] += 1
                    if whole[n]:
                        continue
                    act.wait_ge(slot_loaded[n % SLOTS].sem, slot_loaded[n % SLOTS].at(chunks[n][0]))
                    m = users(n)
                    if m is not None:
                        act.wait_ge(matmul_done.sem, matmul_done.at(chunk_end.get(chunks[m][0])))
                    i = split_no[n] % SLOTS
                    nc.scalar.activation(high[i][:, 0:filled(n)], slots[n % SLOTS][:, 0:filled(n)], ACT.Copy) \
                        .then_inc(high_ready.sem, high_ready.next(n))

            def squares_free():
                if squared.count:
                    act.wait_ge(squared.sem, squared.count)

            def squares(src, c, key):
                squares_free()
                nc.scalar.activation(junk, src, ACT.Square, accum_out=ssum[:, c:c + 1]).then_inc(squared.sem, squared.next(key))

            def turn(st):
                for t in range(NT):
                    for h in range(2):
                        if st in gain_for:
                            bank, done = output(st, t, h)
                            act.wait_ge(matmul_done.sem, matmul_done.at(done))
                            squares(bank[:, :], 2 * t + h, (st, t, h))
                    for h in range(2):
                        if norm_after(st):
                            act.wait_ge(x_ready.sem, x_ready.at((st, t, h)))
                            squares(x[:, t, h * 512:(h + 1) * 512], 4 + 2 * t + h, (norm_after(st), t, h))
                if st in gain_for:
                    row_gain(gain_n[gain_for[st]] + 2)

            def columns(n, gain, dst, nk=KD):
                for b in range((nk + 1) // 2):
                    act.wait_ge(transposed.sem, transposed.at((n, b)))
                    bank = G.of((n, b))
                    for kt in range(2 * b, min(2 * b + 2, nk)):
                        ins = copy(dst(kt).high, bank[:, (kt % 2) * S:(kt % 2 + 1) * S], gain(kt) if gain else 1.0)
                    ins.then_inc(act_step.sem, act_step.next((n, b)))

            def pre(st, key):
                columns((st, "norm"), lambda k: gcol(key, k), lambda k: hT[:, k, :])

            def stage_before_ended(st):
                act.wait_ge(x_ready.sem, x_ready.at((stages[stages.index(st) - 1], NT - 1, 1)))

            def ffn(st, key):
                pre(st, key)
                for i in range(KF):
                    ahead((st, "gate" if i % 2 == 0 else "up", i // 2, 0))
                    act.wait_ge(matmul_done.sem, matmul_done.at((st, "h", i)))
                    if i >= 2:
                        act.wait_ge(dve_read.sem, dve_read.at((st, "h", i - 2)))
                    nc.scalar.activation(silu[:, i % 2, :], G.of((st, "h", i))[:, 0:S], ACT.Silu) \
                        .then_inc(act_step.sem, act_step.next((st, "h", i)))
                    if i:
                        hidden_high(st, i - 1)
                hidden_high(st, KF - 1)
                for m in range(KF // 2 - 1):
                    ahead((st, "out", m))
                    if m == 4 and st == stages[0]:
                        set_up()
                turn(st)

            def hidden_high(st, i):
                act.wait_ge(dve_read.sem, dve_read.at((st, "h", i)))
                copy(hidT.high[:, i, :], hid_f[:, i % 3, :]).then_inc(act_step.sem, act_step.next((st, "hh", i)))

            def attention(st):
                units = units_of(st)
                for i in range(len(units) + 2):
                    if i < len(units):
                        u = units[i]
                        act.wait_ge(maxed.sem, maxed.at((st, i)))
                        if i >= 3:
                            act.wait_ge(transposed.sem, transposed.at((st, "p", i - 3)))
                        nc.scalar.activation(pr[:, i % 3, 0:u["kn"]], sc[:, i % 3, 0:u["kn"]], ACT.Exp, bias=nmax[:, i % 3:i % 3 + 1],
                                             accum_out=sums[:, u["t"], u["col"]:u["col"] + 1]) \
                            .then_inc(weighed.sem, weighed.next((st, i)))
                    if i >= 2:
                        u = units[i - 2]
                        act.wait_ge(transposed.sem, transposed.at((st, "p", i - 2)))
                        if i >= 4:
                            act.wait_ge(matmul_done.sem, matmul_done.at((st, "pv", i - 4)))
                        n, width = u["blocks"][0][1], P * len(u["blocks"])
                        copy(prT[0:n, i % 2, 0:width], TB.of((st, "p", i - 2))[0:n, 0:width]) \
                            .then_inc(act_read.sem, act_read.next((st, "p", i - 2)))

            def mixer(st):
                i = st[1]
                if i % 3 == 0:
                    stage_before_ended(st)
                    act.wait_ge(lines_stored.sem, lines_stored.at("l"))
                    act.dma_start(relA, bass.AP(tensor=line_dram[i // 3].tensor, offset=0,
                                                ap=[[1, P], [3 * P, HEADS_A], [1, TW]])) \
                        .then_inc(table_loaded.sem, table_loaded.next(st))
                if i % 3 == 1:
                    stage_before_ended(st)
                    act.dma_start(ws, w["b_w_s"][0].rearrange("g t s -> t g s")) \
                        .then_inc(spatial_loaded.sem, spatial_loaded.next("ws"))
                pre(st, ("g", i, 2))
                if i % 3 == 1:
                    for c in (2, 3, 0, 1):
                        for t in range(NT):
                            ahead((st, "in", c, t))
                            act.wait_ge(matmul_done.sem, matmul_done.at(((st, "in", c), t)))
                            dst = (u_rows if c < 2 else g_rows)[:, t, (c % 2) * 512:(c % 2) * 512 + 512]
                            nc.scalar.activation(dst, G.of(((st, "in", c), t))[:, :], ACT.Gelu) \
                                .then_inc(act_read.sem, act_read.next(((st, "in", c), t)))
                    for b in (0, 2):
                        act.wait_ge(transposed.sem, transposed.at(((st, "ws"), b)))
                        for kt in (2 * b, 2 * b + 1):
                            ins = copy(wsT[:, kt, :], G.of(((st, "ws"), b))[:, (kt % 2) * S:(kt % 2) * S + P])
                        ins.then_inc(act_read.sem, act_read.next(((st, "ws"), b)))
                    row_gain(gain_n["ln_g"] + 2)
                    row_gain(gain_n["ln_b"] + 2)
                else:
                    for c in range(4):
                        for j in (0, 2):
                            ahead((st, "in", c, j // 2))
                            act.wait_ge(matmul_done.sem, matmul_done.at(((st, "qk", c), j)))
                            copy(qkT[:, 4 * c + j, :], G.of(((st, "qk", c), j))[:, 0:S]).then_inc(act_read.sem, act_read.next(((st, "qk", c), j)))
                    for c in range(2):
                        for h in range(2):
                            ahead((st, "in", 4 + c, h))
                        act.wait_ge(matmul_done.sem, matmul_done.at(((st, "v", c), 0)))
                        copy(v_rows[:, 0, c * 512:(c + 1) * 512], G.of(((st, "v", c), 0))[:, :]) \
                            .then_inc(act_read.sem, act_read.next(((st, "v", c), 0)))
                    attention(st)
                columns((st, "oT"), None, lambda k: oT[:, k, :])
                for c, h in ((0, 0), (0, 1), (1, 0)):
                    ahead((st, "out", c, h))
                turn(st)

            def branches(st):
                l = st[1]
                L = ("l2", l)
                stage_before_ended(st)
                act.dma_start(relN, bass.AP(tensor=line_dram[2].tensor, offset=0, ap=[[1, P], [3 * P, NSA_HEADS], [1, TW]])) \
                    .then_inc(table_loaded.sem, table_loaded.next(st))
                src = w["cmp_w2_k_2"][l].rearrange("(f p) d -> p f d", p=P)
                for dst, src in ((w2k[:, :, 0, :], src), (w2k[:, :, 1, :], src),
                                 (w2v, w["cmp_w2_v_2"][l].rearrange("(f p) d -> p f d", p=P))):
                    act.dma_start(dst, src).then_inc(small_loaded.sem, small_loaded.next(st))
                pre(st, ("norm_mix_2", l))
                for j in (0, 2):
                    ahead((*L, "glu", 0, j // 2))
                    act.wait_ge(matmul_done.sem, matmul_done.at(((st, "glu", 0), j)))
                    copy(aT[:, j, :], G.of(((st, "glu", 0), j))[:, 0:S]).then_inc(act_read.sem, act_read.next(((st, "glu", 0), j)))
                for j in range(4):
                    ahead((*L, "glu", 1, j // 2))
                    act.wait_ge(matmul_done.sem, matmul_done.at(((st, "glu", 1), j)))
                    nc.scalar.activation(bT[:, j, :], G.of(((st, "glu", 1), j))[:, 0:S], ACT.Sigmoid) \
                        .then_inc(act_read.sem, act_read.next(((st, "glu", 1), j)))
                for j in (0, 2):
                    ahead((*L, "q", j // 2))
                    act.wait_ge(matmul_done.sem, matmul_done.at(((st, "q"), j)))
                    copy(qsT[:, j, :], G.of(((st, "q"), j))[:, 0:S]).then_inc(act_read.sem, act_read.next(((st, "q"), j)))
                for h, name, dst in ((0, ("tok", 0), tokT[:, 0, :]), (1, "kslc", kslcT), (2, "kwin", kwinT)):
                    ahead((*L, "kv", h))
                    act.wait_ge(matmul_done.sem, matmul_done.at((st, name)))
                    copy(dst, G.of((st, name))[:, 0:S]).then_inc(act_read.sem, act_read.next((st, name)))
                for v in range(2):
                    sig = (act_read, dve_read)[v]
                    act.wait_ge(sig.sem, sig.at((st, ("tok", v))))
                    for g in range(2):
                        for nxt in range(2):
                            act.dma_start(tok2[nxt * DH:(nxt + 1) * DH, v, g, 0:S - nxt], tokT[g * DH:(g + 1) * DH, v, nxt:S]) \
                                .then_inc(tok_loaded.sem, tok_loaded.next(st))
                for h in range(3):
                    ahead((*L, "rest", h))
                for t in range(NT):
                    act.wait_ge(dve_read.sem, dve_read.at(((st, "rest", 0), t)))
                gates = rest[:, :, R_GATE:R_GATE + 24]
                nc.scalar.activation(gates, gates, ACT.Sigmoid).then_inc(act_step.sem, act_step.next((st, "gates")))
                for t in range(NT):
                    act.wait_ge(dve_read.sem, dve_read.at(((st, "rest", 1), t)))
                    for n, (c0, c1) in enumerate(((R_CQ, R_CKV), (R_CKV, R_KPE))):
                        squares_free()
                        nc.scalar.activation(junk[:, 0:c1 - c0], rest[:, t, c0:c1], ACT.Square,
                                             accum_out=ssum[:, 2 * n + t:2 * n + t + 1]) \
                            .then_inc(squared.sem, squared.next((st, "latent", n, t)))
                for c in range(6):
                    for key in gate_keys(L, c):
                        ahead(key)
                    if c in (1, 2):
                        v = c - 1
                        for f in range(2):
                            act.wait_ge(matmul_done.sem, matmul_done.at((st, "hid", v, f)))
                            nc.scalar.activation(hid_c[:, v, f, :], G.of((st, "hid", v, f))[:, 0:30], ACT.Gelu_apprx_tanh,
                                                 bias=gcol((("cmp_b1_k_2", "cmp_b1_v_2")[v], l), f)) \
                                .then_inc(act_read.sem, act_read.next((st, "hid", v, f)))
                    for t in range(NT):
                        act.wait_ge(matmul_done.sem, matmul_done.at(((st, "merge", c), t)))
                        nc.scalar.activation(gate_half[c][:, t, :], G.of(((st, "merge", c), t))[:, :], ACT.Sigmoid) \
                            .then_inc(act_read.sem, act_read.next(((st, "merge", c), t)))
                for b in range(2):
                    act.wait_ge(transposed.sem, transposed.at(((st, "convT"), b)))
                    bank = G.of(((st, "convT"), b))
                    for kt in (2 * b, 2 * b + 1):
                        ins = nc.scalar.activation(convT[:, kt, :], bank[:, (kt % 2) * S:(kt % 2 + 1) * S], ACT.Silu,
                                                   scale=gcol(("conv_ln_g_2", l), kt), bias=gcol(("conv_ln_b_2", l), kt))
                    ins.then_inc(act_read.sem, act_read.next(((st, "convT"), b)))
                    act.wait_ge(act_read.sem, act_read.at(((st, "convT"), b)))
                    copy(oT.high[:, 2 * b:2 * b + 2, :], convT[:, 2 * b:2 * b + 2, :]) \
                        .then_inc(act_step.sem, act_step.next(((st, "convT"), b)))
                for h in range(2):
                    ahead((*L, "conv", h))
                attention(st)
                columns((st, "oT"), None, lambda k: oT[:, k, :], 4)
                for h in range(2):
                    ahead((*L, "nsa", h))
                columns((st, "latT"), lambda k: gcol(("mla_norm_q_2", l), k) if k < 3 else gcol(("mla_norm_kv_2", l), k - 3),
                        lambda k: hT[:, k, :], 5)
                for h in range(MLA_HEADS):
                    ahead((*L, "uq", h // 2))
                    act.wait_ge(matmul_done.sem, matmul_done.at((st, "qn", h)))
                    copy(qnT[:, h, :], G.of((st, "qn", h))[:, 0:S]).then_inc(act_read.sem, act_read.next((st, "qn", h)))
                ahead((*L, "ukv", 0))
                for h in range(MLA_HEADS):
                    act.wait_ge(matmul_done.sem, matmul_done.at((st, "kn", h)))
                    copy(knT[:, h, :], G.of((st, "kn", h))[:, 0:S]).then_inc(act_read.sem, act_read.next((st, "kn", h)))
                act.wait_ge(transposed.sem, transposed.at(((st, "peT"), 0)))
                copy(qpT[:, :, :].rearrange("p h s -> p (h s)"), G.of(((st, "peT"), 0))[:, :]) \
                    .then_inc(act_read.sem, act_read.next(((st, "peT"), 0)))
                attention(("mla", l))
                columns((("mla", l), "oT"), None, lambda k: oT[:, k, :], 4)
                for h in range(2):
                    ahead((*L, "mla", h))
                columns((st, "mT"), None, lambda k: oT[:, k, :])
                for c, h in ((0, 0), (0, 1), (1, 0)):
                    ahead((*L, "out", c, h))
                turn(st)

            def memory(st):
                l = st[1]
                L = ("l2", l)
                stage_before_ended(st)
                act.dma_start(mem[:, :, :], w["mem_2"][0].rearrange("(t p) d -> p t d", p=P)) \
                    .then_inc(mem_loaded.sem, mem_loaded.next(st))
                pre(st, ("norm_xattn_2", l))
                act.wait_ge(transposed.sem, transposed.at(((st, "norm"), 3)))
                act.wait_ge(mem_loaded.sem, mem_loaded.at(st))
                for t in range(NT):
                    for h in range(2):
                        squares(mem[:, t, h * 512:(h + 1) * 512], 4 + 2 * t + h, ((st, "mem"), t, h))
                for j in (0, 2):
                    ahead((*L, "xq", j // 2))
                    act.wait_ge(matmul_done.sem, matmul_done.at(((st, "xq"), j)))
                    copy(xqT[:, j, :], G.of(((st, "xq"), j))[:, 0:S]).then_inc(act_read.sem, act_read.next(((st, "xq"), j)))
                columns((st, "mem"), lambda k: gcol(("norm_mem_2", l), k), lambda k: oT[:, k, :])
                for j in (0, 2):
                    ahead((*L, "xk", j // 2))
                    act.wait_ge(matmul_done.sem, matmul_done.at(((st, "xk"), j)))
                    copy(xkT[:, j, :], G.of(((st, "xk"), j))[:, 0:S]).then_inc(act_read.sem, act_read.next(((st, "xk"), j)))
                for h in range(2):
                    ahead((*L, "xv", h))
                act.wait_ge(matmul_done.sem, matmul_done.at(((st, "xv"), 0)))
                copy(xv[:, 0, :], G.of(((st, "xv"), 0))[:, :]).then_inc(act_read.sem, act_read.next(((st, "xv"), 0)))
                attention(st)
                columns((st, "oT"), None, lambda k: oT[:, k, :], 4)
                ahead((*L, "xo", 0))
                turn(st)

            def gains_in(n):
                r = gain_tiles[n]
                act.wait_ge(transposed.sem, transposed.at(("gains", n)))
                copy(gT[:, n, 0:r], G.of(("gains", n))[:, 0:r]).then_inc(act_read.sem, act_read.next(("gains", n)))

            def set_up():
                gains_in(2)
                act.wait_ge(dve_step.sem, dve_step.at("lambda"))
                nc.scalar.activation(lam[:, 2:4], lam[:, 0:2], ACT.Exp).then_inc(act_step.sem, act_step.next("lambda"))
                act.wait_ge(dve_step.sem, dve_step.at("angles"))
                nc.scalar.activation(sinb[:, :, :], sinb[:, :, :], ACT.Sin).then_inc(act_step.sem, act_step.next("sin"))
                nc.scalar.activation(cosb[:, :, :], cosb[:, :, :], ACT.Sin).then_inc(act_step.sem, act_step.next("cos"))
                act.wait_ge(dve_step.sem, dve_step.at("lines"))
                for j in range(3):
                    n = HEADS_A if j < 2 else NSA_HEADS
                    act.dma_start(line_dram[j][0:n, 0:3 * P], lines[0:n, j, 0:3 * P]).then_inc(lines_stored.sem, lines_stored.next("l"))

            for t in range(NT):
                act.wait_ge(x_loaded[t].sem, x_loaded[t].at("x"))
                for h in range(2):
                    squares(x[:, t, h * 512:(h + 1) * 512], 4 + 2 * t + h, ((stages[0], "norm"), t, h))
            gains_in(0)
            act.wait_ge(act_read.sem, act_read.at(("gains", 0)))
            ahead(chunks[0][0], 0)
            row_gain(0)
            row_gain(1)
            for st in stages:
                i = st[1]
                if st[0] == "ff1":
                    ffn(st, ("g", i, 0))
                elif st[0] == "ff2":
                    ffn(st, ("g", i, 4))
                elif st[0] == "ff3":
                    ffn(st, ("norm_ffn_2", i))
                else:
                    {"mix": mixer, "l2": branches, "xattn": memory}[st[0]](st)

        @block.gpsimd
        def _(pool):

            def step(ins, key=None):
                settle(pool, ins, pool_step, key)

            def power(key, c0, n):
                pool.wait_ge(mean_ready.sem, mean_ready.at(key))
                pool.tensor_tensor(rstd[:, c0:c0 + n], mean_sq[:, c0:c0 + n], minus_half[:, 0:n], ALU.pow) \
                    .then_inc(rstd_ready.sem, rstd_ready.next(key))

            step(pool.memset(ident[:, :], 0.0))
            step(pool.affine_select(out=ident[:, :], in_=ident[:, :], compare_op=ALU.not_equal, fill=1.0, base=0,
                                    pattern=[[-1, P]], channel_multiplier=1), "ident")
            step(pool.memset(minus_half[:, :], -0.5))
            step(pool.iota(tmp2[0:BUCKETS, 0:16], pattern=[[1, 16]], base=0, channel_multiplier=0,
                           allow_small_or_imprecise_dtypes=True), "exact")
            step(pool.iota(tmp2[0:BUCKETS, 16:17], pattern=[[0, 1]], base=0, channel_multiplier=1,
                           allow_small_or_imprecise_dtypes=True), "bucket")
            for i in range(ROPE // 2):
                ins = pool.memset(freq[:, i:i + 1], ROPE_THETA ** (-i / (ROPE // 2)))
            step(ins, "freq")
            step(pool.memset(valid[:, :], 1.0))
            step(pool.affine_select(out=valid[:, 0:1], in_=valid[:, 0:1], compare_op=ALU.is_ge, fill=0.0,
                                    base=-(CMP_BLOCK - 1), pattern=[[0, 1]], channel_multiplier=1), "valid")
            for t in range(NT):
                power(((stages[0], "norm"), t), 2 + t, 1)
            for st in stages:
                kind, i = st
                if kind == "mix" and i % 3 == 1:
                    pool.wait_ge(spatial_loaded.sem, spatial_loaded.at("ws"))
                    step(pool.affine_select(out=ws, in_=ws, compare_op=ALU.is_ge, fill=0.0, base=0,
                                            pattern=[[0, GROUPS_B], [-1, P]], channel_multiplier=1), "spatial")
                    power((st, "ln"), 4, 2)
                if kind == "mix" and i % 3 == 2:
                    for h in range(HEADS_C):
                        ins = pool.iota(relC[:, h, :], pattern=[[1, TW]], base=-P, channel_multiplier=1,
                                        allow_small_or_imprecise_dtypes=True)
                    step(ins, "distances")
                    power((st, "subln"), 0, 16)
                if kind == "l2":
                    step(pool.memset(causal, 0.0))
                    step(pool.affine_select(out=causal, in_=causal, compare_op=ALU.is_ge, fill=NEG, base=-P,
                                            pattern=[[1, TW]], channel_multiplier=1))
                    pool.wait_ge(table_loaded.sem, table_loaded.at(st))
                    step(pool.affine_select(out=relN, in_=relN, compare_op=ALU.is_ge, fill=NEG, base=-P,
                                            pattern=[[0, NSA_HEADS], [1, TW]], channel_multiplier=1), ("relN", i))
                    power((st, "latent"), 4, 4)
                    power((st, "conv"), 4, 2)
                if kind == "xattn":
                    step(pool.memset(zeros, 0.0), ("zeros", i))
                    for t in range(NT):
                        power(((st, "mem"), t), 2 + t, 1)
                for t in range(NT):
                    if st in gain_for:
                        power((st, "post", t), t, 1)
                    if norm_after(st):
                        power((norm_after(st), t), 2 + t, 1)

        @block.vector
        def _(dve):
            V = nc.vector

            def step(ins, key=None):
                settle(dve, ins, dve_step, key)

            split_to = [0]

            def ahead(key, by=AHEAD):
                while split_to[0] <= min(chunk_index[key] + by, last_chunk):
                    n = split_to[0]
                    split_to[0] += 1
                    if whole[n]:
                        continue
                    dve.wait_ge(high_ready.sem, high_ready.at(n))
                    i, size = split_no[n] % SLOTS, filled(n)
                    V.tensor_tensor(low[i][:, 0:size], slots[n % SLOTS][:, 0:size], high[i][:, 0:size].bitcast(F32), ALU.subtract) \
                        .then_inc(low_ready.sem, low_ready.next(n))

            def tick(sig, key):
                dve.sem_inc(sig.sem, sig.next(key))

            def mean(key, c0, n, src, count):
                V.tensor_scalar(mean_sq[:, c0:c0 + n], src, 1.0 / count, EPS, ALU.mult, ALU.add) \
                    .then_inc(mean_ready.sem, mean_ready.next(key))

            def mean_of_halves(n, t, c, s0, key, factor=1.0, between=None):
                f2 = factor ** 2
                dve.wait_ge(squared.sem, squared.at((n, t, 0)))
                step(V.tensor_scalar(mean_sq[:, c:c + 1], ssum[:, s0:s0 + 1], 1.0 / (D * f2), EPS / f2, ALU.mult, ALU.add))
                if between:
                    between()
                dve.wait_ge(squared.sem, squared.at((n, t, 1)))
                V.scalar_tensor_tensor(mean_sq[:, c:c + 1], ssum[:, s0 + 1:s0 + 2], 1.0 / (D * f2), mean_sq[:, c:c + 1],
                                       ALU.mult, ALU.add).then_inc(mean_ready.sem, mean_ready.next(key))

            def row_factor(n, t, d0=0):
                mean_of_halves(n, t, 2 + t, 4 + 2 * t, (n, t))
                dve.wait_ge(rstd_ready.sem, rstd_ready.at((n, t)))
                V.tensor_scalar(diag[:, d0 + t, :], ident[:, :], rstd[:, 2 + t:3 + t], None, ALU.mult) \
                    .then_inc(rows_ready.sem, rows_ready.next((n, t)))

            def turn(st):
                factor = 1.0 if st[0] == "mix" else 0.5
                gkey = gain_for.get(st)
                for t in range(NT):
                    if gkey:
                        n = gain_n[gkey]
                        dve.wait_ge(gain_loaded[n % 2].sem, gain_loaded[n % 2].at(gkey))
                        def times_gain(h):
                            half = slice(h * 512, (h + 1) * 512)
                            bank, key = output(st, t, h)
                            V.tensor_tensor(xn[:, t, half], bank[:, :], gain_row[n % 2][:, half], ALU.mult) \
                                .then_inc(dve_read.sem, dve_read.next(key))

                        mean_of_halves(st, t, t, 2 * t, (st, "post", t), factor, lambda: times_gain(0))
                        times_gain(1)
                        dve.wait_ge(rstd_ready.sem, rstd_ready.at((st, "post", t)))
                    for h in range(2):
                        half = slice(h * 512, (h + 1) * 512)
                        bank, key = output(st, t, h)
                        if gkey:
                            dve.wait_ge(dve_read.sem, dve_read.at(key))
                            V.scalar_tensor_tensor(x[:, t, half], xn[:, t, half], rstd[:, t:t + 1], x[:, t, half], ALU.mult, ALU.add) \
                                .then_inc(x_ready.sem, x_ready.next((st, t, h)))
                        else:
                            dve.wait_ge(matmul_done.sem, matmul_done.at(key))
                            settle(dve, V.tensor_tensor(x[:, t, half], x[:, t, half], bank[:, :], ALU.add), dve_read, key)
                            tick(x_ready, (st, t, h))
                    if gkey and t == NT - 1:
                        tick(dve_read, ("gain", gkey))
                    if norm_after(st) == "final":
                        mean_of_halves("final", t, 2 + t, 4 + 2 * t, ("final", t))
                        dve.wait_ge(rstd_ready.sem, rstd_ready.at(("final", t)))
                        n = gain_n["final"]
                        dve.wait_ge(gain_loaded[n % 2].sem, gain_loaded[n % 2].at("final"))
                        V.scalar_tensor_tensor(xn[:, t, :], x[:, t, :], rstd[:, 2 + t:3 + t], gain_row[n % 2][:, :],
                                               ALU.mult, ALU.mult).then_inc(rows_ready.sem, rows_ready.next(("final", t)))
                    elif norm_after(st):
                        row_factor(norm_after(st), t)

            def columns(n, gain, dst, nk=KD):
                for b in range((nk + 1) // 2):
                    dve.wait_ge(act_step.sem, act_step.at((n, b)))
                    bank = G.of((n, b))
                    for kt in range(2 * b, min(2 * b + 2, nk)):
                        src = bank[:, (kt % 2) * S:(kt % 2 + 1) * S]
                        d = dst(kt)
                        if gain:
                            ins = V.scalar_tensor_tensor(d.low, src, gain(kt), d.high.bitcast(F32), ALU.mult, ALU.subtract)
                        else:
                            ins = V.tensor_tensor(d.low, src, d.high.bitcast(F32), ALU.subtract)
                    ins.then_inc(dve_read.sem, dve_read.next((n, b)))

            def pre(st, key):
                columns((st, "norm"), lambda k: gcol(key, k), lambda k: hT[:, k, :])

            def ffn(st, key):
                pre(st, key)
                for i in range(KF):
                    ahead((st, "gate" if i % 2 == 0 else "up", i // 2, 0))
                    if i >= 3:
                        dve.wait_ge(act_step.sem, act_step.at((st, "hh", i - 3)))
                        dve.wait_ge(dve_step.sem, dve_step.at((st, "h", i - 3)))
                    dve.wait_ge(act_step.sem, act_step.at((st, "h", i)))
                    V.tensor_tensor(hid_f[:, i % 3, :], silu[:, i % 2, :], G.of((st, "h", i))[:, S:2 * S], ALU.mult) \
                        .then_inc(dve_read.sem, dve_read.next((st, "h", i)))
                    if i:
                        hidden_low(st, i - 1)
                    if st == stages[0] and i in (4, 8):
                        (set_up_lines if i == 4 else set_up_angles)()
                hidden_low(st, KF - 1)
                for m in range(KF // 2 - 1):
                    ahead((st, "out", m))
                    if m == 4 and st == stages[0]:
                        set_up_rest()
                turn(st)

            def hidden_low(st, i):
                dve.wait_ge(act_step.sem, act_step.at((st, "hh", i)))
                V.tensor_tensor(hidT.low[:, i, :], hid_f[:, i % 3, :], hidT.high[:, i, :].bitcast(F32), ALU.subtract) \
                    .then_inc(dve_step.sem, dve_step.next((st, "h", i)))

            def attention(st, evacuate):
                units = units_of(st)
                for i in range(len(units) + 4):
                    if i < len(units):
                        u = units[i]
                        kn = u["kn"]
                        dve.wait_ge(scored.sem, scored.at((st, i)))
                        if i >= 3:
                            dve.wait_ge(weighed.sem, weighed.at((st, i - 3)))
                        settle(dve, V.scalar_tensor_tensor(sc[:, i % 3, 0:kn], SB.of((st, "s", i))[:, 0:kn], u["scale"], u["bias"],
                                                           ALU.mult, ALU.add), dve_read, (st, "s", i))
                        V.tensor_reduce(nmax[:, i % 3:i % 3 + 1], sc[:, i % 3, 0:kn], AX.X, ALU.max, negate=True) \
                            .then_inc(maxed.sem, maxed.next((st, i)))
                    if i >= 4 and units[i - 4]["last"]:
                        u = units[i - 4]
                        dve.wait_ge(matmul_done.sem, matmul_done.at((st, "pv", i - 4)))
                        evacuate(u["acc"], G.of(u["acc"]))

            def heads(bank, n):
                return bank[:, :].rearrange("p (h d) -> p h d", h=n)

            def spread(a, width):
                return a.unsqueeze(2).broadcast_to([a.shape[0], a.shape[1], width])

            def even(st, n, c0):
                def f(acc, bank):
                    _, _, t, b = acc
                    cols = slice(c0 + b * n, c0 + (b + 1) * n)
                    step(V.reciprocal(inv[:, t, cols], sums[:, t, cols]))
                    o = o_rows[:, t, b * 512:(b + 1) * 512].rearrange("p (h d) -> p h d", h=n)
                    settle(dve, V.tensor_tensor(o, heads(bank, n), spread(inv[:, t, cols], 512 // n), ALU.mult), dve_read, acc)
                    if b == (1 if st[0] == "mix" else 0):
                        tick(rows_ready, (st, "o", t))
                return f

            def differential(st):
                def f(acc, bank):
                    _, _, t, b = acc
                    cols = inv[:, t, 4 * b:4 * b + 4]
                    step(V.reciprocal(cols, sums[:, t, 4 * b:4 * b + 4]))
                    step(V.tensor_scalar(cols[:, 1:4:2], cols[:, 1:4:2], lam[:, 6:7], None, ALU.mult))
                    both = bank[:, :].rearrange("p (h m d) -> p h m d", h=2, m=2)
                    o = o_rows[:, t, b * 256:(b + 1) * 256].rearrange("p (h d) -> p h d", h=2)
                    t0 = tmp[:, 0:256].rearrange("p (h d) -> p h d", h=2)
                    t1 = tmp2[:, 0:256].rearrange("p (h d) -> p h d", h=2)
                    step(V.tensor_tensor(t0, both[:, :, 0, :], spread(cols[:, 0:4:2], P), ALU.mult))
                    settle(dve, V.tensor_tensor(t1, both[:, :, 1, :], spread(cols[:, 1:4:2], P), ALU.mult), dve_read, acc)
                    step(V.tensor_tensor(o, t0, t1, ALU.add))
                return f

            def sparse(st):
                def f(acc, bank):
                    _, _, t, br = acc
                    cols = inv[:, t, 8 * br:8 * br + 8]
                    step(V.reciprocal(cols, sums[:, t, 8 * br:8 * br + 8]))
                    if t == 0 and br == 0:
                        step(V.tensor_scalar(cols, cols, valid[:, 0:1], None, ALU.mult))
                    if br == 0:
                        dve.wait_ge(act_step.sem, act_step.at((st, "gates")))
                    step(V.tensor_tensor(cols, cols, rest[:, t, R_GATE + br:R_GATE + 24:3], ALU.mult))
                    o = o_rows[:, t, 0:512]
                    oh = o.rearrange("p (h d) -> p h d", h=8)
                    th = tmp[:, :].rearrange("p (h d) -> p h d", h=8)
                    settle(dve, V.tensor_tensor(oh if br == 0 else th, heads(bank, 8), spread(cols, DH), ALU.mult), dve_read, acc)
                    if br:
                        ins = V.tensor_tensor(o, o, tmp[:, :], ALU.add)
                        if br == 2:
                            settle(dve, ins, rows_ready, (st, "o", t))
                        else:
                            step(ins)
                return f

            def mixer(st):
                i = st[1]
                pre(st, ("g", i, 2))
                if i % 3 == 1:
                    for c in (2, 3):
                        for h in range(2):
                            ahead((st, "in", c, h))
                    ahead((st, "in", 0, 0))
                    for t in range(NT):
                        dve.wait_ge(act_read.sem, act_read.at(((st, "in", 3), 1)))
                        for h in range(2):
                            step(V.bn_stats(stats[:, h, :], g_rows[:, t, h * 512:(h + 1) * 512]))
                        step(V.bn_aggr(moments[:, t, :], stats[:, :, :]))
                    mean((st, "ln"), 4, 2, moments[:, :, 1], 1.0)
                    dve.wait_ge(rstd_ready.sem, rstd_ready.at((st, "ln")))
                    for key in ("ln_g", "ln_b"):
                        dve.wait_ge(gain_loaded[gain_n[key] % 2].sem, gain_loaded[gain_n[key] % 2].at(key))
                    for t in range(NT):
                        g = g_rows[:, t, :]
                        step(V.tensor_scalar(g, g, moments[:, t, 0:1], rstd[:, 4 + t:5 + t], ALU.subtract, ALU.mult))
                        ins = V.tensor_tensor(g, g, gain_row[gain_n["ln_g"] % 2][:, :], ALU.mult)
                        settle(dve, ins, dve_read, ("gain", "ln_g") if t == 1 else ("ln", t))
                        ins = V.tensor_tensor(g, g, gain_row[gain_n["ln_b"] % 2][:, :], ALU.add)
                        settle(dve, ins, rows_ready, (st, "v", t))
                        ahead((st, "in", *((0, 1), (1, 0))[t]))
                    tick(dve_read, ("gain", "ln_b"))
                    ahead((st, "in", 1, 1))
                    for b in (1, 3):
                        dve.wait_ge(transposed.sem, transposed.at(((st, "ws"), b)))
                        for kt in (2 * b, 2 * b + 1):
                            ins = V.tensor_copy(wsT[:, kt, :], G.of(((st, "ws"), b))[:, (kt % 2) * S:(kt % 2) * S + P])
                        ins.then_inc(dve_read.sem, dve_read.next(((st, "ws"), b)))
                    for t in range(NT):
                        for h in range(2):
                            dve.wait_ge(matmul_done.sem, matmul_done.at((st, "sv", t, h)))
                            dve.wait_ge(act_read.sem, act_read.at(((st, "in", 1), 1)))
                            bank = G.of((st, "sv", t, h))
                            for g in range(4):
                                c = slice((4 * h + g) * P, (4 * h + g + 1) * P)
                                ins = V.scalar_tensor_tensor(o_rows[:, t, c], bank[:, g * P:(g + 1) * P], gcol("b_b_s", 4 * h + g),
                                                             u_rows[:, t, c], ALU.add, ALU.mult)
                            settle(dve, ins, dve_read, (st, "sv", t, h))
                        tick(rows_ready, (st, "o", t))
                else:
                    for c in range(4):
                        for j in (1, 3):
                            ahead((st, "in", c, j // 2))
                            dve.wait_ge(matmul_done.sem, matmul_done.at(((st, "qk", c), j)))
                            V.tensor_copy(qkT[:, 4 * c + j, :], G.of(((st, "qk", c), j))[:, 0:S]) \
                                .then_inc(dve_read.sem, dve_read.next(((st, "qk", c), j)))
                    if i % 3 == 0:
                        dve.wait_ge(table_loaded.sem, table_loaded.at(st))
                        step(V.memset(relA[0:CHUNK, :, 1:CHUNK + 1], NEG))
                    else:
                        dve.wait_ge(pool_step.sem, pool_step.at("distances"))
                        step(V.scalar_tensor_tensor(relC, relC, -1.0, relC, ALU.mult, ALU.max))
                        for h in range(HEADS_C):
                            step(V.tensor_scalar(relC[:, h, :], relC[:, h, :], -(2.0 ** (-8.0 * (h + 1) / HEADS_C)), None, ALU.mult))
                        step(V.memset(relC[0:CHUNK, :, 1:CHUNK + 1], NEG))
                    for c in range(2):
                        for h in range(2):
                            ahead((st, "in", 4 + c, h))
                        dve.wait_ge(matmul_done.sem, matmul_done.at(((st, "v", c), 1)))
                        V.tensor_copy(v_rows[:, 1, c * 512:(c + 1) * 512], G.of(((st, "v", c), 1))[:, :]) \
                            .then_inc(dve_read.sem, dve_read.next(((st, "v", c), 1)))
                    attention(st, even(st, 8, 0) if i % 3 == 0 else differential(st))
                    if i % 3 == 2:
                        o4 = o_rows[:, :, :].rearrange("p t (h d) -> p t h d", h=HEADS_C)
                        x4 = xn[:, :, :].rearrange("p t (h d) -> p t h d", h=HEADS_C)
                        for t in range(NT):
                            step(V.tensor_tensor(xn[:, t, :], o_rows[:, t, :], o_rows[:, t, :], ALU.mult))
                            step(V.tensor_reduce(mean_sq[:, 8 * t:8 * t + 8], x4[:, t, :, :], AX.X, ALU.add))
                        mean((st, "subln"), 0, 16, mean_sq[:, 0:16], P)
                        dve.wait_ge(rstd_ready.sem, rstd_ready.at((st, "subln")))
                        lambda_init = 0.8 - 0.6 * math.exp(-0.3 * i)
                        step(V.tensor_scalar(rstd[:, 0:16], rstd[:, 0:16], 1.0 - lambda_init, None, ALU.mult))
                        for t in range(NT):
                            step(V.tensor_tensor(o4[:, t, :, :], o4[:, t, :, :], spread(rstd[:, 8 * t:8 * t + 8], P), ALU.mult))
                            ins = V.tensor_tensor(o4[:, t, :, :], o4[:, t, :, :],
                                                  subln[:, :].unsqueeze(1).broadcast_to([P, HEADS_C, P]), ALU.mult)
                            ins.then_inc(rows_ready.sem, rows_ready.next((st, "o", t)))
                columns((st, "oT"), None, lambda k: oT[:, k, :])
                for c, h in ((0, 0), (0, 1), (1, 0)):
                    ahead((st, "out", c, h))
                turn(st)

            def merge(st, name, n):
                k = (st, name)
                if n == 2:
                    dve.wait_ge(act_read.sem, act_read.at(((st, "merge", 5), 1)))
                for t in range(NT):
                    for h in range(2):
                        dve.wait_ge(matmul_done.sem, matmul_done.at((k, "chunk", ("l2", st[1], name[1:], 1))))
                        bank = G.of((k, t, h))
                        gate = gate_half[2 * n + h][:, t, :]
                        m = merged[:, t, h * 512:(h + 1) * 512]
                        ins = V.tensor_tensor(m if n == 0 else tmp[:, :], bank[:, :], gate, ALU.mult)
                        settle(dve, ins, dve_read, (k, t, h))
                        if n:
                            ins = V.tensor_tensor(m, m, tmp[:, :], ALU.add)
                            if n == 2 and h == 1:
                                settle(dve, ins, rows_ready, (st, "merged", t))
                            else:
                                step(ins)

            def branches(st):
                l = st[1]
                pre(st, ("norm_mix_2", l))
                L = ("l2", l)
                for j in (1, 3):
                    ahead((*L, "glu", 0, j // 2))
                    dve.wait_ge(matmul_done.sem, matmul_done.at(((st, "glu", 0), j)))
                    V.tensor_copy(aT[:, j, :], G.of(((st, "glu", 0), j))[:, 0:S]) \
                        .then_inc(dve_read.sem, dve_read.next(((st, "glu", 0), j)))
                for h in range(2):
                    ahead((*L, "glu", 1, h))
                for j in (1, 3):
                    ahead((*L, "q", j // 2))
                    dve.wait_ge(matmul_done.sem, matmul_done.at(((st, "q"), j)))
                    V.tensor_copy(qsT[:, j, :], G.of(((st, "q"), j))[:, 0:S]) \
                        .then_inc(dve_read.sem, dve_read.next(((st, "q"), j)))
                ahead((*L, "kv", 0))
                dve.wait_ge(matmul_done.sem, matmul_done.at((st, ("tok", 1))))
                V.tensor_copy(tokT[:, 1, :], G.of((st, ("tok", 1)))[:, 0:S]).then_inc(dve_read.sem, dve_read.next((st, ("tok", 1))))
                for h, name, dst in ((1, "vslc", vslc), (2, "vwin", vwin)):
                    ahead((*L, "kv", h))
                    for t in range(NT):
                        dve.wait_ge(matmul_done.sem, matmul_done.at(((st, name), t)))
                        V.tensor_copy(dst[:, t, :], G.of(((st, name), t))[:, 0:P]) \
                            .then_inc(dve_read.sem, dve_read.next(((st, name), t)))
                for n, (c0, c1) in enumerate(((0, 512), (512, N_REST))):
                    for h in ((0, 1), (2,))[n]:
                        ahead((*L, "rest", h))
                    for t in range(NT):
                        dve.wait_ge(matmul_done.sem, matmul_done.at(((st, "rest", n), t)))
                        V.tensor_copy(rest[:, t, c0:c1], G.of(((st, "rest", n), t))[:, 0:c1 - c0]) \
                            .then_inc(dve_read.sem, dve_read.next(((st, "rest", n), t)))
                for n, (c0, c1) in enumerate(((R_CQ, R_CKV), (R_CKV, R_KPE))):
                    dve.wait_ge(squared.sem, squared.at((st, "latent", 1, 1)))
                    ins = V.tensor_scalar(mean_sq[:, 4 + 2 * n:6 + 2 * n], ssum[:, 2 * n:2 * n + 2], 1.0 / (c1 - c0), EPS,
                                          ALU.mult, ALU.add)
                    if n:
                        ins.then_inc(mean_ready.sem, mean_ready.next((st, "latent")))
                    else:
                        step(ins)
                dve.wait_ge(rstd_ready.sem, rstd_ready.at((st, "latent")))
                for n, (c0, c1) in enumerate(((R_CQ, R_CKV), (R_CKV, R_KPE))):
                    for t in range(NT):
                        step(V.tensor_scalar(rest[:, t, c0:c1], rest[:, t, c0:c1],
                                             rstd[:, 4 + 2 * n + t:5 + 2 * n + t], None, ALU.mult))
                tick(rows_ready, (st, "latent"))
                dve.wait_ge(tok_loaded.sem, tok_loaded.at(st))
                for v in range(2):
                    for g in range(2):
                        for half in range(2):
                            src = tok2[:, v, g, half * CMP_STRIDE:half * CMP_STRIDE + N_CMP * CMP_STRIDE] \
                                .rearrange("p (c r) -> p r c", r=CMP_STRIDE)[:, 0:CMP_STRIDE:2, :]
                            t_, r = col[(("cmp_pos_k_2", "cmp_pos_v_2")[v], l)]
                            pos = gT[:, t_, r + 8 * half:r + 8 * half + 8].unsqueeze(2).broadcast_to([P, 8, N_CMP])
                            ins = V.tensor_tensor(blk[:, v, 8 * half:8 * half + 8, g, :], src, pos, ALU.add)
                    ins.then_inc(dve_read.sem, dve_read.next((st, "blk", v)))
                step(V.memset(glu[:, :, 0:TAPS - 1], 0.0))
                dve.wait_ge(act_read.sem, act_read.at(((st, "glu", 1), 3)))
                dve.wait_ge(dve_read.sem, dve_read.at(((st, "glu", 0), 3)))
                step(V.tensor_tensor(glu[:, :, TAPS - 1:TAPS - 1 + S], aT, bT, ALU.mult))
                shared = [key for c in range(6) for key in gate_keys(L, c)]

                def gate_ahead(key):
                    ahead(key)
                    if key == (*L, "merge", 4, 0):
                        compressed()

                def compressed():
                    dve.wait_ge(matmul_done.sem, matmul_done.at((st, "kc")))
                    V.tensor_copy(kcT[:, 0:30], G.of((st, "kc"))[:, 0:30]).then_inc(dve_read.sem, dve_read.next((st, "kc")))
                    for g in range(2):
                        dve.wait_ge(matmul_done.sem, matmul_done.at((st, "vc", g)))
                        V.tensor_copy(vc[0:N_CMP, g, :], G.of((st, "vc", g))[0:N_CMP, 0:DH]) \
                            .then_inc(dve_read.sem, dve_read.next((st, "vc", g)))

                for tap in range(TAPS):
                    if tap % 2 == 1:
                        gate_ahead(shared.pop(0))
                    for c in range(CT):
                        if tap:
                            dve.wait_ge(dve_step.sem, dve_step.count - CT + 1)
                        wt = convwT[:, l, tap * CT + c:tap * CT + c + 1]
                        src = glu[:, c, tap:tap + S]
                        if tap == 0:
                            ins = V.tensor_scalar(convT[:, c, :], src, wt, gcol(("conv_b_2", l), c), ALU.mult, ALU.add)
                        else:
                            ins = V.scalar_tensor_tensor(convT[:, c, :], src, wt, convT[:, c, :], ALU.mult, ALU.add)
                        ins.then_inc(dve_step.sem, dve_step.next((st, "conv")))
                for key in shared:
                    gate_ahead(key)
                for t in range(NT):
                    dve.wait_ge(transposed.sem, transposed.at((st, "conv_rows", t)))
                    step(V.bn_stats(stats[:, 0, :], TB.of((st, "conv_rows", t))[:, :]))
                    step(V.bn_aggr(moments[:, t, :], stats[:, 0, :]))
                mean((st, "conv"), 4, 2, moments[:, :, 1], 1.0)
                dve.wait_ge(rstd_ready.sem, rstd_ready.at((st, "conv")))
                for t in range(NT):
                    ins = V.tensor_scalar(xn[:, t, 0:CONV_CH], TB.of((st, "conv_rows", t))[:, :], moments[:, t, 0:1],
                                          rstd[:, 4 + t:5 + t], ALU.subtract, ALU.mult)
                    settle(dve, ins, dve_read, (st, "conv_rows", t))
                    tick(rows_ready, (st, "conv", t))
                for b in range(2):
                    dve.wait_ge(act_step.sem, act_step.at(((st, "convT"), b)))
                    d = oT[:, 2 * b:2 * b + 2, :]
                    V.tensor_tensor(d.low, convT[:, 2 * b:2 * b + 2, :], d.high.bitcast(F32), ALU.subtract) \
                        .then_inc(dve_read.sem, dve_read.next(((st, "convT"), b)))
                for h in range(2):
                    ahead((*L, "conv", h))
                dve.wait_ge(act_read.sem, act_read.at(((st, "merge", 3), 1)))
                merge(st, "yconv", 0)
                dve.wait_ge(pool_step.sem, pool_step.at(("relN", l)))
                attention(st, sparse(st))
                columns((st, "oT"), None, lambda k: oT[:, k, :], 4)
                for h in range(2):
                    ahead((*L, "nsa", h))
                merge(st, "ynsa", 1)
                columns((st, "latT"), lambda k: gcol(("mla_norm_q_2", l), k) if k < 3 else gcol(("mla_norm_kv_2", l), k - 3),
                        lambda k: hT[:, k, :], 5)
                def rotate(x1, x2, cos, sin, shape, outs, key):
                    r = [tmp[:, n * DH:(n + 1) * DH].rearrange("p (h d) -> p h d", h=shape[0]) for n in range(4)]
                    step(V.tensor_tensor(r[0], x1, cos, ALU.mult))
                    step(V.tensor_tensor(r[1], x2, sin, ALU.mult))
                    step(V.tensor_tensor(r[2], x2, cos, ALU.mult))
                    ins = V.tensor_tensor(r[3], x1, sin, ALU.mult)
                    settle(dve, ins, dve_read, key)
                    for o1, o2 in outs:
                        step(V.tensor_tensor(o1, r[0], r[1], ALU.subtract))
                        step(V.tensor_tensor(o2, r[2], r[3], ALU.add))

                dve.wait_ge(act_step.sem, act_step.at("cos"))
                for h in range(2):
                    ahead((*L, "uq", h))
                    for t in range(NT):
                        dve.wait_ge(matmul_done.sem, matmul_done.at((st, "qp", h, t)))
                        q = G.of((st, "qp", h, t))[:, 0:128].rearrange("p (h e) -> p h e", h=2)
                        o = xn[:, t, h * P:(h + 1) * P].rearrange("p (h e) -> p h e", h=2)
                        cos, sin = (a[:, t, :].unsqueeze(1).broadcast_to([P, 2, 32]) for a in (cosb, sinb))
                        rotate(q[:, :, 0:32], q[:, :, 32:64], cos, sin, (2, 32), [(o[:, :, 0:32], o[:, :, 32:64])],
                               (st, "qp", h, t))
                ahead((*L, "ukv", 0))
                rotate(rest[:, :, R_KPE:R_KPE + 32], rest[:, :, R_KPE + 32:R_KPE + 64], cosb[:, :, :], sinb[:, :, :], (2, 32),
                       [(xn[:, :, 256 + 64 * u:288 + 64 * u], xn[:, :, 288 + 64 * u:320 + 64 * u]) for u in range(2)], (st, "kpe"))
                tick(rows_ready, (st, "rope"))
                for t in range(NT):
                    dve.wait_ge(matmul_done.sem, matmul_done.at((st, "vm", t)))
                    V.tensor_copy(vm[:, t, :], G.of((st, "vm", t))[:, :]).then_inc(dve_read.sem, dve_read.next((st, "vm", t)))
                dve.wait_ge(transposed.sem, transposed.at(((st, "peT"), 1)))
                V.tensor_copy(kpT, G.of(((st, "peT"), 1))[:, 0:S]).then_inc(dve_read.sem, dve_read.next(((st, "peT"), 1)))
                attention(("mla", l), even(("mla", l), 4, 24))
                columns((("mla", l), "oT"), None, lambda k: oT[:, k, :], 4)
                for h in range(2):
                    ahead((*L, "mla", h))
                merge(st, "ymla", 2)
                columns((st, "mT"), None, lambda k: oT[:, k, :])
                for c, h in ((0, 0), (0, 1), (1, 0)):
                    ahead((*L, "out", c, h))
                turn(st)

            def memory(st):
                l = st[1]
                L = ("l2", l)
                pre(st, ("norm_xattn_2", l))
                for j in (1, 3):
                    ahead((*L, "xq", j // 2))
                    dve.wait_ge(matmul_done.sem, matmul_done.at(((st, "xq"), j)))
                    V.tensor_copy(xqT[:, j, :], G.of(((st, "xq"), j))[:, 0:S]) \
                        .then_inc(dve_read.sem, dve_read.next(((st, "xq"), j)))
                for t in range(NT):
                    row_factor((st, "mem"), t, 2)
                columns((st, "mem"), lambda k: gcol(("norm_mem_2", l), k), lambda k: oT[:, k, :])
                for j in (1, 3):
                    ahead((*L, "xk", j // 2))
                    dve.wait_ge(matmul_done.sem, matmul_done.at(((st, "xk"), j)))
                    V.tensor_copy(xkT[:, j, :], G.of(((st, "xk"), j))[:, 0:S]) \
                        .then_inc(dve_read.sem, dve_read.next(((st, "xk"), j)))
                for h in range(2):
                    ahead((*L, "xv", h))
                dve.wait_ge(matmul_done.sem, matmul_done.at(((st, "xv"), 1)))
                V.tensor_copy(xv[:, 1, :], G.of(((st, "xv"), 1))[:, :]).then_inc(dve_read.sem, dve_read.next(((st, "xv"), 1)))
                dve.wait_ge(pool_step.sem, pool_step.at(("zeros", l)))
                attention(st, even(st, 4, 24))
                columns((st, "oT"), None, lambda k: oT[:, k, :], 4)
                ahead((*L, "xo", 0))
                turn(st)

            def set_up_lines():
                dve.wait_ge(consts_loaded.sem, consts_loaded.at("c"))
                for j in range(2):
                    ins = V.tensor_copy(lines[:, j, 2 * REL_CLIP + 1:3 * P],
                                        lines[:, j, 2 * REL_CLIP:2 * REL_CLIP + 1].broadcast_to([HEADS_A, P - 1]))
                step(ins)
                dve.wait_ge(pool_step.sem, pool_step.at("bucket"))
                buckets = rtmp[0:BUCKETS, 0:2, :].rearrange("p a b -> p (a b)")[:, 0:3 * P]
                step(V.memset(buckets, -1.0))
                step(V.tensor_copy(buckets[:, P:P + 16], tmp2[0:BUCKETS, 0:16]))
                for b in range(16, BUCKETS):
                    ds = [d for d in range(S) if t5_bucket(d) == b]
                    step(V.memset(buckets[:, P + ds[0]:P + ds[-1] + 1], float(b)))
                step(V.tensor_scalar(onehot[:, :], buckets, tmp2[0:BUCKETS, 16:17], None, ALU.is_equal), "onehot")

            def set_up_angles():
                for n in range(2):
                    step(V.tensor_tensor(tmp[:, 0:DH], lam_in[:, 2 * n, :], lam_in[:, 2 * n + 1, :], ALU.mult))
                    step(V.tensor_reduce(lam[:, n:n + 1], tmp[:, 0:DH], AX.X, ALU.add), "lambda")
                dve.wait_ge(pool_step.sem, pool_step.at("valid"))
                step(V.tensor_copy(pos_f[:, :], pos_i[:, :]))
                for t in range(NT):
                    step(V.tensor_scalar(sinb[:, t, :], freq[:, :], pos_f[:, t:t + 1], None, ALU.mult))
                turns = tmp[:, 0:64].rearrange("p (t f) -> p t f", t=NT)
                step(V.tensor_scalar(turns, sinb[:, :, :], 1.0 / (2 * math.pi), None, ALU.mult))
                step(V.tensor_scalar(turns, turns, MAGIC, None, ALU.add))
                step(V.tensor_scalar(turns, turns, MAGIC, None, ALU.subtract))
                for part_of_turn in (6.28125, 0.0019340515136718750, 2 * math.pi - 6.28125 - 0.0019340515136718750):
                    step(V.scalar_tensor_tensor(sinb[:, :, :], turns, -part_of_turn, sinb[:, :, :], ALU.mult, ALU.add))
                step(V.tensor_scalar(sinb[:, :, :], sinb[:, :, :], 3.1415925, -3.1415925, ALU.min, ALU.max))
                step(V.scalar_tensor_tensor(cosb[:, :, :], sinb[:, :, :], -1.0, sinb[:, :, :], ALU.mult, ALU.max))
                step(V.tensor_scalar(cosb[:, :, :], cosb[:, :, :], -1.0, math.pi / 2, ALU.mult, ALU.add), "angles")

            def set_up_rest():
                for n in (1, 3):
                    dve.wait_ge(transposed.sem, transposed.at(("gains", n)))
                    if n == 1:
                        ins = V.tensor_copy(gT[:, 1, 0:gain_tiles[1]], G.of(("gains", 1))[:, 0:gain_tiles[1]])
                    else:
                        ins = V.tensor_copy(convwT[:, :, 0:TAPS * CT],
                                            G.of(("gains", 3))[:, 0:2 * P].rearrange("p (l n) -> p l n", l=2)[:, :, 0:TAPS * CT])
                    settle(dve, ins, dve_read, ("gains", n))
                dve.wait_ge(matmul_done.sem, matmul_done.at("line"))
                settle(dve, V.tensor_copy(lines[0:NSA_HEADS, 2, :], G.of("line")[0:NSA_HEADS, 0:3 * P]), dve_read, "line")
                tick(dve_step, "lines")
                dve.wait_ge(act_read.sem, act_read.at(("gains", 2)))
                lambda_init = 0.8 - 0.6 * math.exp(-0.3 * 2)
                dve.wait_ge(act_step.sem, act_step.at("lambda"))
                step(V.tensor_tensor(lam[:, 5:6], lam[:, 3:4], lam[:, 2:3], ALU.subtract))
                step(V.tensor_scalar(lam[:, 6:7], lam[:, 5:6], lambda_init, None, ALU.subtract))

            for t in range(NT):
                row_factor((stages[0], "norm"), t)
            ahead(chunks[0][0], 0)
            for st in stages:
                i = st[1]
                if st[0] == "ff1":
                    ffn(st, ("g", i, 0))
                elif st[0] == "ff2":
                    ffn(st, ("g", i, 4))
                elif st[0] == "ff3":
                    ffn(st, ("norm_ffn_2", i))
                else:
                    {"mix": mixer, "l2": branches, "xattn": memory}[st[0]](st)


_INS = """x norm_g ff1_w_in ff1_w_out ff2_w_in ff2_w_out a_w_qkv a_rel_bias a_w_o b_w_in b_ln_g b_ln_b b_w_s b_b_s b_w_o
c_w_qkv c_lambda c_subln_g c_w_o mem_2 positions_2 rel_bias_2 norm_mix_2 norm_xattn_2 norm_mem_2 norm_ffn_2 norm_final_2
w_in_2 conv_w_2 conv_b_2 conv_ln_g_2 conv_ln_b_2 w_branch_conv_2 cmp_pos_k_2 cmp_w1_k_2 cmp_b1_k_2 cmp_w2_k_2 cmp_pos_v_2
cmp_w1_v_2 cmp_b1_v_2 cmp_w2_v_2 w_branch_nsa_2 mla_norm_q_2 mla_norm_kv_2 w_uq_2 w_ukv_2 w_branch_mla_2 w_out_2 w_xq_2
w_xkv_2 w_xo_2 w_gate_up_2 w_down_2""".split()
STOP = None


def kernel(**inputs):
    import numpy as np
    import concourse.bacc as bacc
    from concourse.bass_utils import run_bass_kernel_spmd

    plan = {}
    for _ in range(3):
        nc = bacc.Bacc("TRN2", target_bir_lowering=False, num_devices=1)
        arrays, args = {}, {}
        for name in _INS:
            a = np.ascontiguousarray(inputs[name])
            arrays[f"in_{name}_dram"] = a
            args[name] = nc.dram_tensor(f"in_{name}_dram", a.shape, mybir.dt.from_np(a.dtype), kind="ExternalInput").ap()
        out = nc.dram_tensor("out_0_dram", (1, S, D), F32, kind="ExternalOutput").ap()
        build(nc, args, out, plan, STOP)
    return run_bass_kernel_spmd(nc, [arrays], core_ids=[0]).results[0]["out_0_dram"]
```
